# Optimizing a Trainium2 kernel written in Bass

```python
import jax, jax.numpy as jnp
from jax import lax
import numpy as np

D_MODEL = 1024
BATCH = 1
SEQ = 256
DEPTH = 2

GRID_W = 64
CTX_LEN = 256
HEAD_DIM = 64
A_HEADS = (D_MODEL // HEAD_DIM) // 2
A_KV_HEADS = 2
A_WIDTH = A_HEADS * HEAD_DIM
B_HEADS = (D_MODEL // HEAD_DIM) // 2
B_WIDTH = B_HEADS * HEAD_DIM
DECAY_LORA = 64
ICLR_LORA = 64
GATE_LORA = 128
C_HEADS = D_MODEL // HEAD_DIM
C_KV_HEADS = 4
C_WIDTH = C_HEADS * HEAD_DIM
WINDOW = 128
Q_BLOCK = 128
D_FF = 2816
N_MOD = 9
ROPE_THETA = 10000.0
EPS = 1e-6
GN_EPS = 64e-5
NEG_BIG = -1e30

A_COLS = A_WIDTH + 2 * A_KV_HEADS * HEAD_DIM
A_SPLITS = (A_WIDTH, A_WIDTH + A_KV_HEADS * HEAD_DIM)
RWKV_COLS = 3 * B_WIDTH + 2 * DECAY_LORA + 2 * ICLR_LORA + GATE_LORA
RWKV_SPLITS = (B_WIDTH, 2 * B_WIDTH, 3 * B_WIDTH, 3 * B_WIDTH + 2 * DECAY_LORA,
               3 * B_WIDTH + 2 * DECAY_LORA + 2 * ICLR_LORA)
EVEN_COLS = A_COLS + RWKV_COLS
ODD_COLS = C_WIDTH + 2 * C_KV_HEADS * HEAD_DIM
ODD_SPLITS = (C_WIDTH, C_WIDTH + C_KV_HEADS * HEAD_DIM)


def rms_norm(x, gain=None):
    xf = x.astype(jnp.float32)
    y = xf * lax.rsqrt(jnp.mean(xf * xf, axis=-1, keepdims=True) + EPS)
    if gain is not None:
        y = y * gain
    return y.astype(x.dtype)

def modulate(h, shift, scale):
    return h * (1.0 + scale) + shift

def swiglu(h, w_in, w_out):
    gate, up = jnp.split(h @ w_in, 2, axis=-1)
    return (jax.nn.silu(gate) * up) @ w_out

def axial_rope_tables(n_tokens):
    rows = n_tokens // GRID_W
    row = jnp.repeat(jnp.arange(rows, dtype=jnp.float32), GRID_W)
    col = jnp.tile(jnp.arange(GRID_W, dtype=jnp.float32), rows)
    n_freq = HEAD_DIM // 4
    inv_freq = ROPE_THETA ** (-jnp.arange(n_freq, dtype=jnp.float32) / n_freq)
    ang = jnp.concatenate([row[:, None] * inv_freq, col[:, None] * inv_freq], axis=-1)
    return jnp.cos(ang), jnp.sin(ang)

def apply_rope(x, cos, sin):
    xp = x.reshape(*x.shape[:-1], HEAD_DIM // 2, 2)
    x0, x1 = xp[..., 0], xp[..., 1]
    c = cos[None, :, None, :].astype(x.dtype)
    s = sin[None, :, None, :].astype(x.dtype)
    return jnp.stack([x0 * c - x1 * s, x0 * s + x1 * c], axis=-1).reshape(x.shape)

def attend(q, k, v):
    s = jnp.einsum('bqhgd,bkhd->bhgqk', q, k).astype(jnp.float32)
    p = jax.nn.softmax(s, axis=-1).astype(v.dtype)
    return jnp.einsum('bhgqk,bkhd->bqhgd', p, v)

def global_gqa(q_l, k_l, v_l, q_c, k_c, v_c, ctx_out):
    Bsz, N = q_l.shape[:2]
    G = A_HEADS // A_KV_HEADS
    scale = HEAD_DIM ** -0.5
    k_all = jnp.concatenate([k_l, k_c], axis=1)
    v_all = jnp.concatenate([v_l, v_c], axis=1)
    qb = (q_l * scale).reshape(Bsz, N // Q_BLOCK, Q_BLOCK, A_KV_HEADS, G, HEAD_DIM).swapaxes(0, 1)
    o_lat = lax.map(lambda qblk: attend(qblk, k_all, v_all), qb)
    o_lat = o_lat.swapaxes(0, 1).reshape(Bsz, N, A_WIDTH)
    o_ctx = None
    if ctx_out:
        L = q_c.shape[1]
        qc = (q_c * scale).reshape(Bsz, L, A_KV_HEADS, G, HEAD_DIM)
        o_ctx = attend(qc, k_c, v_c).reshape(Bsz, L, A_WIDTH)
    return o_lat, o_ctx

def window_gqa(q_l, k_l, v_l, q_c, k_c, v_c, sink, ctx_out):
    Bsz, N = q_l.shape[:2]
    G = C_HEADS // C_KV_HEADS
    scale = HEAD_DIM ** -0.5
    nb = N // Q_BLOCK
    span = Q_BLOCK + 2 * WINDOW
    pad = ((0, 0), (WINDOW, WINDOW), (0, 0), (0, 0))
    k_pad = jnp.pad(k_l, pad)
    v_pad = jnp.pad(v_l, pad)
    qb = (q_l * scale).reshape(Bsz, nb, Q_BLOCK, C_KV_HEADS, G, HEAD_DIM).swapaxes(0, 1)
    sink_hg = sink.reshape(C_KV_HEADS, G).astype(jnp.float32)
    q_off = jnp.arange(Q_BLOCK)
    k_off = jnp.arange(span) - WINDOW
    in_window = jnp.abs(k_off[None, :] - q_off[:, None]) <= WINDOW

    def softmax_with_sink(s):
        sink_col = jnp.broadcast_to(sink_hg[None, :, :, None, None], s.shape[:-1] + (1,))
        return jax.nn.softmax(jnp.concatenate([s, sink_col], axis=-1), axis=-1)[..., :-1]

    def block(args):
        b, qblk = args
        start = b * Q_BLOCK
        kb = lax.dynamic_slice_in_dim(k_pad, start, span, axis=1)
        vb = lax.dynamic_slice_in_dim(v_pad, start, span, axis=1)
        kpos = start - WINDOW + k_off
        valid = in_window & ((kpos >= 0) & (kpos < N))[None, :]
        s_win = jnp.einsum('bqhgd,bkhd->bhgqk', qblk, kb).astype(jnp.float32)
        s_win = jnp.where(valid, s_win, NEG_BIG)
        s_ctx = jnp.einsum('bqhgd,bkhd->bhgqk', qblk, k_c).astype(jnp.float32)
        p = softmax_with_sink(jnp.concatenate([s_win, s_ctx], axis=-1)).astype(vb.dtype)
        return (jnp.einsum('bhgqk,bkhd->bqhgd', p[..., :span], vb)
                + jnp.einsum('bhgqk,bkhd->bqhgd', p[..., span:], v_c))

    o_lat = lax.map(block, (jnp.arange(nb), qb)).swapaxes(0, 1).reshape(Bsz, N, C_WIDTH)
    o_ctx = None
    if ctx_out:
        L = q_c.shape[1]
        qc = (q_c * scale).reshape(Bsz, L, C_KV_HEADS, G, HEAD_DIM)
        s = jnp.einsum('bqhgd,bkhd->bhgqk', qc, k_c).astype(jnp.float32)
        p = softmax_with_sink(s).astype(v_c.dtype)
        o_ctx = jnp.einsum('bhgqk,bkhd->bqhgd', p, v_c).reshape(Bsz, L, C_WIDTH)
    return o_lat, o_ctx

def centred_shift(f, mu):
    prev = jnp.pad(f[:, :-1], ((0, 0), (1, 0), (0, 0)))
    nxt = jnp.pad(f[:, 1:], ((0, 0), (0, 1), (0, 0)))
    return f + mu[0] * (prev - f) + mu[1] * (nxt - f)

def rwkv7_features(f, mu, w0, w2, a0, a2, g2, k_k, k_a):
    Bsz, T, _ = f.shape
    f = centred_shift(f, mu)
    r, k, v, wl, al, gl = jnp.split(f, RWKV_SPLITS, axis=-1)
    heads = lambda t: t.reshape(Bsz, T, B_HEADS, HEAD_DIM)
    dir_heads = lambda t: t.reshape(Bsz, T, 2, B_HEADS, HEAD_DIM)
    kk = heads(k * k_k).astype(jnp.float32)
    kk = kk * lax.rsqrt(jnp.sum(kk * kk, axis=-1, keepdims=True) + EPS)
    w_log = (w0 + jnp.einsum('btdr,drc->btdc', jnp.tanh(wl.reshape(Bsz, T, 2, DECAY_LORA)), w2)).astype(jnp.float32)
    decay = jnp.exp(-jnp.exp(-jax.nn.softplus(-w_log) - 0.5))
    a = jax.nn.sigmoid((a0 + jnp.einsum('btdr,drc->btdc', al.reshape(Bsz, T, 2, ICLR_LORA), a2)).astype(jnp.float32))
    k_dir = k[:, :, None, :].astype(jnp.float32) * (1.0 + (a - 1.0) * k_a)
    g = jax.nn.sigmoid(gl) @ g2
    return (heads(r), heads(k), heads(v), kk, g, dir_heads(decay), dir_heads(a), dir_heads(k_dir))

def wkv7_scan(S0, inputs, reverse):
    xs = tuple(jnp.swapaxes(t.astype(jnp.float32), 0, 1) for t in inputs)

    def step(S, inp):
        r, w, k, v, kk, a = inp
        S = (S * w[:, :, None, :]
             - jnp.einsum('bhvk,bhk->bhv', S, kk)[..., None] * (kk * a)[:, :, None, :]
             + v[..., None] * k[:, :, None, :])
        return S, jnp.einsum('bhvk,bhk->bhv', S, r)

    S, y = lax.scan(step, S0, xs, reverse=reverse)
    return S, jnp.swapaxes(y, 0, 1)

def rwkv7_readout(y, feat, r_k, gn_w, gn_b):
    r, k, v, _, g = feat[:5]
    Bsz, T = y.shape[:2]
    mean = jnp.mean(y, axis=-1, keepdims=True)
    var = jnp.mean(jnp.square(y - mean), axis=-1, keepdims=True)
    yn = ((y - mean) * lax.rsqrt(var + GN_EPS)).reshape(Bsz, T, B_WIDTH) * gn_w + gn_b
    bonus = (jnp.sum(r * k * r_k, axis=-1, keepdims=True) * v).reshape(Bsz, T, B_WIDTH)
    return ((yn + bonus.astype(jnp.float32)) * g.astype(jnp.float32)).astype(g.dtype)

def rwkv7_bidir(f_lat, f_ctx, r_k, gn_w, gn_b, ctx_out):
    Bsz = f_lat[0].shape[0]
    S0 = jnp.zeros((Bsz, B_HEADS, HEAD_DIM, HEAD_DIM), jnp.float32)

    def dir_inputs(f, d):
        r, _, v, kk, _, decay, a, k_dir = f
        return (r, decay[:, :, d], k_dir[:, :, d], v, kk, a[:, :, d])

    S_cf, y_cf = wkv7_scan(S0, dir_inputs(f_ctx, 0), reverse=False)
    S_cb, y_cb = wkv7_scan(S0, dir_inputs(f_ctx, 1), reverse=True)
    _, y_lf = wkv7_scan(S_cf, dir_inputs(f_lat, 0), reverse=False)
    _, y_lb = wkv7_scan(S_cb, dir_inputs(f_lat, 1), reverse=True)
    o_lat = rwkv7_readout(y_lf + y_lb, f_lat, r_k, gn_w, gn_b)
    o_ctx = rwkv7_readout(y_cf + y_cb, f_ctx, r_k, gn_w, gn_b) if ctx_out else None
    return o_lat, o_ctx

def even_mixer(h_lat, h_ctx, cos, sin, w_in, w_out, q_gain, k_gain, mu, w0, w2, a0, a2, g2,
               k_k, k_a, r_k, gn_w, gn_b, ctx_out):
    Bsz, N, _ = h_lat.shape
    L = h_ctx.shape[1]
    p_lat = h_lat @ w_in
    p_ctx = h_ctx @ w_in

    def qkv_a(p, T):
        q, k, v = jnp.split(p[..., :A_COLS], A_SPLITS, axis=-1)
        q = rms_norm(q.reshape(Bsz, T, A_HEADS, HEAD_DIM), q_gain)
        k = rms_norm(k.reshape(Bsz, T, A_KV_HEADS, HEAD_DIM), k_gain)
        return q, k, v.reshape(Bsz, T, A_KV_HEADS, HEAD_DIM)

    q_l, k_l, v_l = qkv_a(p_lat, N)
    q_c, k_c, v_c = qkv_a(p_ctx, L)
    oa_lat, oa_ctx = global_gqa(apply_rope(q_l, cos, sin), apply_rope(k_l, cos, sin), v_l,
                                q_c, k_c, v_c, ctx_out)
    f_lat = rwkv7_features(p_lat[..., A_COLS:], mu, w0, w2, a0, a2, g2, k_k, k_a)
    f_ctx = rwkv7_features(p_ctx[..., A_COLS:], mu, w0, w2, a0, a2, g2, k_k, k_a)
    ob_lat, ob_ctx = rwkv7_bidir(f_lat, f_ctx, r_k, gn_w, gn_b, ctx_out)
    o_lat = jnp.concatenate([oa_lat, ob_lat], axis=-1) @ w_out
    o_ctx = jnp.concatenate([oa_ctx, ob_ctx], axis=-1) @ w_out if ctx_out else None
    return o_lat, o_ctx

def odd_mixer(h_lat, h_ctx, cos, sin, w_in, w_out, sink, ctx_out):
    Bsz, N, _ = h_lat.shape
    L = h_ctx.shape[1]

    def qkv_c(h, T):
        q, k, v = jnp.split(h @ w_in, ODD_SPLITS, axis=-1)
        return (q.reshape(Bsz, T, C_HEADS, HEAD_DIM), k.reshape(Bsz, T, C_KV_HEADS, HEAD_DIM),
                v.reshape(Bsz, T, C_KV_HEADS, HEAD_DIM))

    q_l, k_l, v_l = qkv_c(h_lat, N)
    q_c, k_c, v_c = qkv_c(h_ctx, L)
    o_lat, o_ctx = window_gqa(apply_rope(q_l, cos, sin), apply_rope(k_l, cos, sin), v_l,
                              q_c, k_c, v_c, sink, ctx_out)
    return o_lat @ w_out, (o_ctx @ w_out if ctx_out else None)

def first_inputs(seed: int = 0) -> dict:
    key = jax.random.key(seed)
    ks = iter(jax.random.split(key, 32))
    nrm = lambda shape, s: s * jax.random.normal(next(ks), shape, jnp.float32)
    uni = lambda shape, lo, hi: jax.random.uniform(next(ks), shape, jnp.float32, lo, hi)
    n_even = (DEPTH + 1) // 2
    n_odd = DEPTH // 2
    D = D_MODEL
    return {
        "x": nrm((BATCH, SEQ, D), 1.0),
        "c": nrm((BATCH, D), 1.0),
        "ctx": nrm((BATCH, CTX_LEN, D), 1.0),
        "c_ctx": nrm((D,), 1.0),
        "w_mod": nrm((DEPTH, D, N_MOD * D), 0.5 * D ** -0.5),
        "b_mod": nrm((DEPTH, N_MOD * D), 0.02),
        "ffn_in": nrm((DEPTH, 2, D, 2 * D_FF), D ** -0.5),
        "ffn_out": nrm((DEPTH, 2, D_FF, D), D_FF ** -0.5),
        "even_w_in": nrm((n_even, D, EVEN_COLS), D ** -0.5),
        "even_w_out": nrm((n_even, A_WIDTH + B_WIDTH, D), (A_WIDTH + B_WIDTH) ** -0.5),
        "q_gain": 1.0 + nrm((n_even, HEAD_DIM), 0.05),
        "k_gain": 1.0 + nrm((n_even, HEAD_DIM), 0.05),
        "rwkv_mu": uni((n_even, 2, RWKV_COLS), 0.0, 0.5),
        "rwkv_w0": uni((n_even, 2, B_WIDTH), -4.0, 1.0),
        "rwkv_w2": nrm((n_even, 2, DECAY_LORA, B_WIDTH), 0.1),
        "rwkv_a0": nrm((n_even, 2, B_WIDTH), 0.5),
        "rwkv_a2": nrm((n_even, 2, ICLR_LORA, B_WIDTH), 0.1),
        "rwkv_g2": nrm((n_even, GATE_LORA, B_WIDTH), GATE_LORA ** -0.5),
        "rwkv_k_k": 0.85 + nrm((n_even, B_WIDTH), 0.05),
        "rwkv_k_a": 1.0 + nrm((n_even, B_WIDTH), 0.05),
        "rwkv_r_k": nrm((n_even, B_HEADS, HEAD_DIM), 0.1),
        "rwkv_gn_w": 1.0 + nrm((n_even, B_WIDTH), 0.05),
        "rwkv_gn_b": nrm((n_even, B_WIDTH), 0.02),
        "odd_w_in": nrm((n_odd, D, ODD_COLS), D ** -0.5),
        "odd_w_out": nrm((n_odd, C_WIDTH, D), C_WIDTH ** -0.5),
        "sink": nrm((n_odd, C_HEADS), 1.0),
        "final_gain": 1.0 + nrm((D,), 0.05),
    }

def first_block(x, c, ctx, c_ctx, w_mod, b_mod, ffn_in, ffn_out, even_w_in, even_w_out, q_gain, k_gain,
              rwkv_mu, rwkv_w0, rwkv_w2, rwkv_a0, rwkv_a2, rwkv_g2, rwkv_k_k, rwkv_k_a, rwkv_r_k,
              rwkv_gn_w, rwkv_gn_b, odd_w_in, odd_w_out, sink, final_gain):
    Bsz, N, D = x.shape
    cos, sin = axial_rope_tables(N)
    silu_c = jax.nn.silu(c)
    silu_cc = jax.nn.silu(c_ctx)
    for l in range(DEPTH):
        ctx_out = l < DEPTH - 1
        m_lat = (silu_c @ w_mod[l] + b_mod[l]).reshape(Bsz, N_MOD, 1, D)
        m_ctx = (silu_cc @ w_mod[l] + b_mod[l]).reshape(N_MOD, D)
        x = x + 0.5 * m_lat[:, 2] * swiglu(modulate(rms_norm(x), m_lat[:, 0], m_lat[:, 1]), ffn_in[l, 0], ffn_out[l, 0])
        ctx = ctx + 0.5 * m_ctx[2] * swiglu(modulate(rms_norm(ctx), m_ctx[0], m_ctx[1]), ffn_in[l, 0], ffn_out[l, 0])
        h_lat = modulate(rms_norm(x), m_lat[:, 3], m_lat[:, 4])
        h_ctx = modulate(rms_norm(ctx), m_ctx[3], m_ctx[4])
        if l % 2 == 0:
            e = l // 2
            o_lat, o_ctx = even_mixer(h_lat, h_ctx, cos, sin, even_w_in[e], even_w_out[e], q_gain[e], k_gain[e],
                                      rwkv_mu[e], rwkv_w0[e], rwkv_w2[e], rwkv_a0[e], rwkv_a2[e], rwkv_g2[e],
                                      rwkv_k_k[e], rwkv_k_a[e], rwkv_r_k[e], rwkv_gn_w[e], rwkv_gn_b[e], ctx_out)
        else:
            o = l // 2
            o_lat, o_ctx = odd_mixer(h_lat, h_ctx, cos, sin, odd_w_in[o], odd_w_out[o], sink[o], ctx_out)
        x = x + m_lat[:, 5] * o_lat
        x = x + 0.5 * m_lat[:, 8] * swiglu(modulate(rms_norm(x), m_lat[:, 6], m_lat[:, 7]), ffn_in[l, 1], ffn_out[l, 1])
        if ctx_out:
            ctx = ctx + m_ctx[5] * o_ctx
            ctx = ctx + 0.5 * m_ctx[8] * swiglu(modulate(rms_norm(ctx), m_ctx[6], m_ctx[7]), ffn_in[l, 1], ffn_out[l, 1])
    return rms_norm(x, final_gain)


ATTN_QBLOCK = 128
ROPE_BASE = 10000.0

MLA_HEADS = 8
MLA_Q_RANK = 384
MLA_KV_RANK = 256
MLA_NOPE = 64
MLA_ROPE = 32
MLA_V = 64
ROPE_PAIRS = MLA_ROPE // 4
MLSTM_HEADS = 4
MLSTM_DH = 128
MLSTM_CONV = 3
MLSTM_CHUNK = 64
GLA_HEADS = 4
GLA_DK = 64
GLA_DV = 128
GLA_GATE_RANK = 16
GLA_TAU = 16.0
GLA_CHUNK = 64
NA_HEADS = 8
NA_DH = 64
NA_KH = 8
NA_KW = 16

BRANCH_A = MLA_HEADS * MLA_V
BRANCH_B = MLSTM_HEADS * MLSTM_DH
BRANCH_C = GLA_HEADS * GLA_DV
BRANCH_D = NA_HEADS * NA_DH
EVEN_SPLITS = (MLA_Q_RANK, MLA_KV_RANK, MLA_ROPE, BRANCH_B, BRANCH_B, BRANCH_B, BRANCH_B, 4 * MLSTM_HEADS, BRANCH_A + BRANCH_B)
ODD_SPLITS_2 = (GLA_HEADS * GLA_DK, GLA_HEADS * GLA_DK, BRANCH_C, 2 * GLA_GATE_RANK, BRANCH_D, BRANCH_D, BRANCH_D, BRANCH_C + BRANCH_D)
EVEN_IN = sum(EVEN_SPLITS)
ODD_IN = sum(ODD_SPLITS_2)


def split_cols(a, sizes):
    return jnp.split(a, np.cumsum(sizes)[:-1].tolist(), axis=-1)

def rmsnorm(x, g):
    xf = x.astype(jnp.float32)
    xf = xf * lax.rsqrt(jnp.mean(xf * xf, axis=-1, keepdims=True) + EPS)
    return xf.astype(x.dtype) * g

def head_rmsnorm(x, g, n_heads):
    B, T, W = x.shape
    return rmsnorm(x.reshape(B, T, n_heads, W // n_heads), g.reshape(n_heads, -1)).reshape(B, T, W)

def to_heads(a, n_heads):
    B, T, W = a.shape
    return a.reshape(B, T, n_heads, W // n_heads).transpose(0, 2, 1, 3)

def merge_heads(a):
    B, H, T, d = a.shape
    return a.transpose(0, 2, 1, 3).reshape(B, T, H * d)

def centred_dwconv(x, w, b):
    K = w.shape[0]
    T = x.shape[1]
    pad = K // 2
    xp = jnp.pad(x, ((0, 0), (pad, K - 1 - pad), (0, 0)))
    y = xp[:, 0:T] * w[0]
    for j in range(1, K):
        y = y + xp[:, j:j + T] * w[j]
    return y + b

def rope2d_tables(S):
    t = jnp.arange(S)
    inv = 1.0 / (ROPE_BASE ** (jnp.arange(ROPE_PAIRS, dtype=jnp.float32) / ROPE_PAIRS))
    ang = jnp.concatenate([(t // GRID_W)[:, None] * inv, (t % GRID_W)[:, None] * inv], axis=-1)
    return jnp.cos(ang), jnp.sin(ang)

def apply_rope2d(x, cos, sin):
    cos = cos.astype(x.dtype)
    sin = sin.astype(x.dtype)
    parts = []
    for a in range(2):
        y = x[..., a * 2 * ROPE_PAIRS:(a + 1) * 2 * ROPE_PAIRS]
        y1, y2 = y[..., :ROPE_PAIRS], y[..., ROPE_PAIRS:]
        ca = cos[:, a * ROPE_PAIRS:(a + 1) * ROPE_PAIRS]
        sa = sin[:, a * ROPE_PAIRS:(a + 1) * ROPE_PAIRS]
        parts += [y1 * ca - y2 * sa, y2 * ca + y1 * sa]
    return jnp.concatenate(parts, axis=-1)

def to_chunks(a, L):
    B, H, T = a.shape[:3]
    return jnp.moveaxis(a.reshape(B, H, T // L, L, *a.shape[3:]), 2, 0)

def from_chunks(a):
    nc, B, H, L = a.shape[:4]
    return jnp.moveaxis(a, 0, 2).reshape(B, H, nc * L, *a.shape[4:])

def block_attention(q, k, v, scale):
    B, H, S, dq = q.shape
    nb = S // ATTN_QBLOCK
    qb = jnp.moveaxis(q.reshape(B, H, nb, ATTN_QBLOCK, dq), 2, 0)

    def one_block(qi):
        s = jnp.einsum('bhqd,bhkd->bhqk', qi, k).astype(jnp.float32) * scale
        p = jax.nn.softmax(s, axis=-1).astype(v.dtype)
        return jnp.einsum('bhqk,bhkd->bhqd', p, v)

    o = lax.map(one_block, qb)
    return jnp.moveaxis(o, 0, 2).reshape(B, H, S, v.shape[-1])

def mlstm_chunked(q, k, v, ig, lf, state):
    L = MLSTM_CHUNK
    causal = jnp.tril(jnp.ones((L, L), dtype=bool))

    def step(carry, xs):
        C, n, m = carry
        qc, kc, vc, ic, fc = xs
        b = jnp.cumsum(fc, axis=-1)
        logw = jnp.where(causal, b[..., :, None] - b[..., None, :] + ic[..., None, :], -jnp.inf)
        inter = b + m[..., None]
        m_t = jnp.maximum(inter, jnp.max(logw, axis=-1))
        w_intra = jnp.exp(logw - m_t[..., None])
        w_inter = jnp.exp(inter - m_t)
        qk = jnp.einsum('bhtd,bhsd->bhts', qc, kc) * w_intra
        num = jnp.einsum('bhts,bhsv->bhtv', qk, vc) + w_inter[..., None] * jnp.einsum('bhtd,bhdv->bhtv', qc, C)
        den = jnp.sum(qk, axis=-1) + w_inter * jnp.einsum('bhtd,bhd->bht', qc, n)
        h = num / jnp.maximum(jnp.abs(den), jnp.exp(-m_t))[..., None]
        b_last = b[..., -1]
        logk = b_last[..., None] - b + ic
        m_new = jnp.maximum(b_last + m, jnp.max(logk, axis=-1))
        carry_decay = jnp.exp(b_last + m - m_new)
        kw = jnp.exp(logk - m_new[..., None])[..., None] * kc
        C = carry_decay[..., None, None] * C + jnp.einsum('bhsd,bhsv->bhdv', kw, vc)
        n = carry_decay[..., None] * n + jnp.sum(kw, axis=2)
        return (C, n, m_new), h

    xs = tuple(to_chunks(a.astype(jnp.float32), L) for a in (q, k, v, ig, lf))
    state, h = lax.scan(step, state, xs)
    return from_chunks(h), state

def gla_chunked(q, k, v, lg, S0):
    L = GLA_CHUNK
    causal = jnp.tril(jnp.ones((L, L), dtype=bool))

    def step(S, xs):
        qc, kc, vc, gc = xs
        bcum = jnp.cumsum(gc, axis=2)
        rel = bcum[:, :, :, None, :] - bcum[:, :, None, :, :]
        decay = jnp.exp(jnp.where(causal[:, :, None], rel, -jnp.inf))
        att = jnp.einsum('bhtd,bhsd,bhtsd->bhts', qc, kc, decay)
        o = jnp.einsum('bhts,bhsv->bhtv', att, vc) + jnp.einsum('bhtd,bhdv->bhtv', qc * jnp.exp(bcum), S)
        b_last = bcum[:, :, -1:]
        S_new = jnp.exp(b_last[:, :, 0])[..., None] * S + jnp.einsum('bhsd,bhsv->bhdv', kc * jnp.exp(b_last - bcum), vc)
        return S_new, o

    xs = tuple(to_chunks(a.astype(jnp.float32), L) for a in (q, k, v, lg))
    S, o = lax.scan(step, S0, xs)
    return from_chunks(o), S

def bidirectional_scan(chunk_fn, init_state, shared_c, gates_c, shared_l, gates_l):
    outs_c, outs_l = [], []
    for d in range(2):
        if d == 0:
            f = lambda a: a
        else:
            f = lambda a: jnp.flip(a, axis=2)
        hc, st = chunk_fn(*[f(a) for a in shared_c], *[f(g[d]) for g in gates_c], init_state)
        hl, _ = chunk_fn(*[f(a) for a in shared_l], *[f(g[d]) for g in gates_l], st)
        outs_c.append(f(hc))
        outs_l.append(f(hl))
    return outs_c[0] + outs_c[1], outs_l[0] + outs_l[1]

def neighbourhood_attention(q, k, v, k_ctx, v_ctx, rpb, rows):
    B, H, S, d = q.shape
    kh = min(NA_KH, rows)
    qg = q.reshape(B, H, rows, GRID_W, d)
    kg = k.reshape(B, H, rows, GRID_W, d)
    vg = v.reshape(B, H, rows, GRID_W, d)
    r_idx = jnp.arange(rows)
    c_idx = jnp.arange(GRID_W)
    win_rows = jnp.clip(r_idx - kh // 2, 0, rows - kh)[:, None] + jnp.arange(kh)
    win_cols = jnp.clip(c_idx - NA_KW // 2, 0, GRID_W - NA_KW)[:, None] + jnp.arange(NA_KW)
    dcol = win_cols - c_idx[:, None] + (NA_KW - 1)
    scale = d ** -0.5
    n_loc = kh * NA_KW

    def one_row(r):
        rws = win_rows[r]
        drow = rws - r + (NA_KH - 1)
        bias = rpb[:, drow[None, :, None], dcol[:, None, :]].astype(jnp.float32)
        qr = qg[:, :, r]
        kw = kg[:, :, rws][:, :, :, win_cols]
        vw = vg[:, :, rws][:, :, :, win_cols]
        s_loc = jnp.einsum('bhcd,bhicjd->bhcij', qr, kw).astype(jnp.float32) * scale + bias
        s_ctx = jnp.einsum('bhcd,bhnd->bhcn', qr, k_ctx).astype(jnp.float32) * scale
        logits = jnp.concatenate([s_loc.reshape(B, H, GRID_W, n_loc), s_ctx], axis=-1)
        p = jax.nn.softmax(logits, axis=-1).astype(v.dtype)
        p_loc = p[..., :n_loc].reshape(B, H, GRID_W, kh, NA_KW)
        return jnp.einsum('bhcij,bhicjd->bhcd', p_loc, vw) + jnp.einsum('bhcn,bhnd->bhcd', p[..., n_loc:], v_ctx)

    o = lax.map(one_row, r_idx)
    return jnp.moveaxis(o, 0, 2).reshape(B, H, S, d)

def mla_mlstm_mixer(u_lat, u_ctx, cos, sin, w_in, q_norm, w_uq, kv_norm, w_ukv, conv_w, conv_b, b_i, b_f, h_norm, w_out, need_ctx):
    def project(u, rotate):
        B, T, _ = u.shape
        cq, ckv, k_rope, mq, mk, mv, mo, gates, z = split_cols(u @ w_in, EVEN_SPLITS)
        q = to_heads(rmsnorm(cq, q_norm) @ w_uq, MLA_HEADS)
        kv = to_heads(rmsnorm(ckv, kv_norm) @ w_ukv, MLA_HEADS)
        q_nope, q_rope = q[..., :MLA_NOPE], q[..., MLA_NOPE:]
        k_nope, v = kv[..., :MLA_NOPE], kv[..., MLA_NOPE:]
        k_rope = k_rope[:, None]
        if rotate:
            q_rope = apply_rope2d(q_rope, cos, sin)
            k_rope = apply_rope2d(k_rope, cos, sin)
        q = jnp.concatenate([q_nope, q_rope], axis=-1)
        k = jnp.concatenate([k_nope, jnp.broadcast_to(k_rope, (B, MLA_HEADS, T, MLA_ROPE))], axis=-1)
        qk = jax.nn.silu(centred_dwconv(jnp.concatenate([mq, mk], axis=-1), conv_w, conv_b))
        mq = to_heads(qk[..., :BRANCH_B], MLSTM_HEADS) * MLSTM_DH ** -0.5
        mk = to_heads(qk[..., BRANCH_B:], MLSTM_HEADS)
        mv = to_heads(mv, MLSTM_HEADS)
        g = gates.reshape(B, T, 2, 2, MLSTM_HEADS).astype(jnp.float32)
        ig = (g[:, :, :, 0] + b_i).transpose(2, 0, 3, 1)
        lf = jax.nn.log_sigmoid(g[:, :, :, 1] + b_f).transpose(2, 0, 3, 1)
        return (q, k, v), (mq, mk, mv), (ig, lf), mo, z

    (qa_l, ka_l, va_l), seq_l, gates_l, mo_l, z_l = project(u_lat, True)
    (qa_c, ka_c, va_c), seq_c, gates_c, mo_c, z_c = project(u_ctx, False)
    scale = (MLA_NOPE + MLA_ROPE) ** -0.5
    a_lat = block_attention(qa_l, jnp.concatenate([ka_c, ka_l], axis=2), jnp.concatenate([va_c, va_l], axis=2), scale)
    B = u_lat.shape[0]
    init = (jnp.zeros((B, MLSTM_HEADS, MLSTM_DH, MLSTM_DH), jnp.float32),
            jnp.zeros((B, MLSTM_HEADS, MLSTM_DH), jnp.float32),
            jnp.zeros((B, MLSTM_HEADS), jnp.float32))
    h_c, h_l = bidirectional_scan(mlstm_chunked, init, seq_c, gates_c, seq_l, gates_l)

    def combine(a, h, mo, z, dtype):
        hm = head_rmsnorm(jax.nn.sigmoid(mo.astype(jnp.float32)) * merge_heads(h), h_norm, MLSTM_HEADS).astype(dtype)
        return (jnp.concatenate([merge_heads(a), hm], axis=-1) * jax.nn.silu(z)) @ w_out

    y_lat = combine(a_lat, h_l, mo_l, z_l, u_lat.dtype)
    y_ctx = None
    if need_ctx:
        y_ctx = combine(block_attention(qa_c, ka_c, va_c, scale), h_c, mo_c, z_c, u_ctx.dtype)
    return y_lat, y_ctx

def gla_na_mixer(u_lat, u_ctx, rows, w_in, w_gate, b_gate, gla_norm, rpb, w_out, need_ctx):
    def project(u):
        B, T, _ = u.shape
        gq, gk, gv, ga, nq, nk, nv, z = split_cols(u @ w_in, ODD_SPLITS_2)
        ga = ga.reshape(B, T, 2, GLA_GATE_RANK)
        lg = jax.nn.log_sigmoid(jnp.einsum('btdr,drk->dbtk', ga, w_gate).astype(jnp.float32) + b_gate[:, None, None]) / GLA_TAU
        lg = lg.reshape(2, B, T, GLA_HEADS, GLA_DK).transpose(0, 1, 3, 2, 4)
        seq = (to_heads(gq, GLA_HEADS) * GLA_DK ** -0.5, to_heads(gk, GLA_HEADS), to_heads(gv, GLA_HEADS))
        na = (to_heads(nq, NA_HEADS), to_heads(nk, NA_HEADS), to_heads(nv, NA_HEADS))
        return seq, (lg,), na, z

    seq_l, gates_l, (nq_l, nk_l, nv_l), z_l = project(u_lat)
    seq_c, gates_c, (nq_c, nk_c, nv_c), z_c = project(u_ctx)
    B = u_lat.shape[0]
    init = jnp.zeros((B, GLA_HEADS, GLA_DK, GLA_DV), jnp.float32)
    o_c, o_l = bidirectional_scan(gla_chunked, init, seq_c, gates_c, seq_l, gates_l)
    na_l = neighbourhood_attention(nq_l, nk_l, nv_l, nk_c, nv_c, rpb, rows)

    def combine(o, na, z, dtype):
        g = head_rmsnorm(merge_heads(o), gla_norm, GLA_HEADS).astype(dtype)
        return (jnp.concatenate([g, merge_heads(na)], axis=-1) * jax.nn.silu(z)) @ w_out

    y_lat = combine(o_l, na_l, z_l, u_lat.dtype)
    y_ctx = None
    if need_ctx:
        y_ctx = combine(o_c, block_attention(nq_c, nk_c, nv_c, NA_DH ** -0.5), z_c, u_ctx.dtype)
    return y_lat, y_ctx

def second_inputs(seed: int = 0) -> dict:
    key = jax.random.key(seed)
    keys = iter(jax.random.split(key, 32))

    def rnd(shape, s):
        return jax.random.normal(next(keys), shape, jnp.float32) * s

    def gain(n):
        return 1.0 + rnd((n,), 0.05)

    D = D_MODEL
    return {
        'x': rnd((BATCH, SEQ, D), 1.0),
        'c': rnd((BATCH, D), 1.0),
        'ctx': rnd((BATCH, CTX_LEN, D), 1.0),
        'c_ctx': rnd((D,), 1.0),
        'l0_norm': gain(D),
        'l0_w_mod': rnd((D, 3 * D), 0.5 * D ** -0.5),
        'l0_b_mod': rnd((3 * D,), 0.02),
        'l0_w_in': rnd((D, EVEN_IN), D ** -0.5),
        'l0_mla_q_norm': gain(MLA_Q_RANK),
        'l0_mla_w_uq': rnd((MLA_Q_RANK, MLA_HEADS * (MLA_NOPE + MLA_ROPE)), MLA_Q_RANK ** -0.5),
        'l0_mla_kv_norm': gain(MLA_KV_RANK),
        'l0_mla_w_ukv': rnd((MLA_KV_RANK, MLA_HEADS * (MLA_NOPE + MLA_V)), MLA_KV_RANK ** -0.5),
        'l0_mlstm_conv_w': rnd((MLSTM_CONV, 2 * BRANCH_B), MLSTM_CONV ** -0.5),
        'l0_mlstm_conv_b': rnd((2 * BRANCH_B,), 0.02),
        'l0_mlstm_b_i': rnd((2, MLSTM_HEADS), 0.1),
        'l0_mlstm_b_f': jnp.linspace(3.0, 6.0, MLSTM_HEADS)[None] + rnd((2, MLSTM_HEADS), 0.1),
        'l0_mlstm_norm': gain(BRANCH_B),
        'l0_w_out': rnd((BRANCH_A + BRANCH_B, D), (BRANCH_A + BRANCH_B) ** -0.5),
        'l1_norm': gain(D),
        'l1_w_mod': rnd((D, 3 * D), 0.5 * D ** -0.5),
        'l1_b_mod': rnd((3 * D,), 0.02),
        'l1_w_in': rnd((D, ODD_IN), D ** -0.5),
        'l1_gla_w_gate': rnd((2, GLA_GATE_RANK, GLA_HEADS * GLA_DK), GLA_GATE_RANK ** -0.5),
        'l1_gla_b_gate': rnd((2, GLA_HEADS * GLA_DK), 0.5),
        'l1_gla_norm': gain(BRANCH_C),
        'l1_na_rpb': rnd((NA_HEADS, 2 * NA_KH - 1, 2 * NA_KW - 1), 0.1),
        'l1_w_out': rnd((BRANCH_C + BRANCH_D, D), (BRANCH_C + BRANCH_D) ** -0.5),
        'final_norm': gain(D),
    }

def second_block(x, c, ctx, c_ctx,
              l0_norm, l0_w_mod, l0_b_mod, l0_w_in, l0_mla_q_norm, l0_mla_w_uq, l0_mla_kv_norm, l0_mla_w_ukv,
              l0_mlstm_conv_w, l0_mlstm_conv_b, l0_mlstm_b_i, l0_mlstm_b_f, l0_mlstm_norm, l0_w_out,
              l1_norm, l1_w_mod, l1_b_mod, l1_w_in, l1_gla_w_gate, l1_gla_b_gate, l1_gla_norm, l1_na_rpb, l1_w_out,
              final_norm):
    S = x.shape[1]
    rows = S // GRID_W
    cos, sin = rope2d_tables(S)
    norms = (l0_norm, l1_norm)
    mods = ((l0_w_mod, l0_b_mod), (l1_w_mod, l1_b_mod))
    mixer_params = (
        (l0_w_in, l0_mla_q_norm, l0_mla_w_uq, l0_mla_kv_norm, l0_mla_w_ukv, l0_mlstm_conv_w, l0_mlstm_conv_b,
         l0_mlstm_b_i, l0_mlstm_b_f, l0_mlstm_norm, l0_w_out),
        (l1_w_in, l1_gla_w_gate, l1_gla_b_gate, l1_gla_norm, l1_na_rpb, l1_w_out),
    )
    h_lat, h_ctx = x, ctx
    for layer in range(DEPTH):
        need_ctx = layer < DEPTH - 1
        w_mod, b_mod = mods[layer]
        shift_l, scale_l, gate_l = jnp.split(jax.nn.silu(c) @ w_mod + b_mod, 3, axis=-1)
        shift_c, scale_c, gate_c = jnp.split(jax.nn.silu(c_ctx) @ w_mod + b_mod, 3, axis=-1)
        u_lat = rmsnorm(h_lat, norms[layer]) * (1 + scale_l[:, None]) + shift_l[:, None]
        u_ctx = rmsnorm(h_ctx, norms[layer]) * (1 + scale_c) + shift_c
        if layer % 2 == 0:
            y_lat, y_ctx = mla_mlstm_mixer(u_lat, u_ctx, cos, sin, *mixer_params[layer], need_ctx=need_ctx)
        else:
            y_lat, y_ctx = gla_na_mixer(u_lat, u_ctx, rows, *mixer_params[layer], need_ctx=need_ctx)
        h_lat = h_lat + gate_l[:, None] * y_lat
        if need_ctx:
            h_ctx = h_ctx + gate_c * y_ctx
    return rmsnorm(h_lat, final_norm)


def setup_inputs(seed=0):
    out = dict(first_inputs(seed))
    for name, value in second_inputs(seed + 1).items():
        if name != "x":
            out[name + "_2"] = value
    return out


def reference(
    x, c, ctx, c_ctx, w_mod, b_mod, ffn_in, ffn_out, even_w_in, even_w_out, q_gain, k_gain,
    rwkv_mu, rwkv_w0, rwkv_w2, rwkv_a0, rwkv_a2, rwkv_g2, rwkv_k_k, rwkv_k_a, rwkv_r_k,
    rwkv_gn_w, rwkv_gn_b, odd_w_in, odd_w_out, sink, final_gain, c_2, ctx_2, c_ctx_2, l0_norm_2,
    l0_w_mod_2, l0_b_mod_2, l0_w_in_2, l0_mla_q_norm_2, l0_mla_w_uq_2, l0_mla_kv_norm_2,
    l0_mla_w_ukv_2, l0_mlstm_conv_w_2, l0_mlstm_conv_b_2, l0_mlstm_b_i_2, l0_mlstm_b_f_2,
    l0_mlstm_norm_2, l0_w_out_2, l1_norm_2, l1_w_mod_2, l1_b_mod_2, l1_w_in_2, l1_gla_w_gate_2,
    l1_gla_b_gate_2, l1_gla_norm_2, l1_na_rpb_2, l1_w_out_2, final_norm_2,
):
    x = first_block(
        x, c, ctx, c_ctx, w_mod, b_mod, ffn_in, ffn_out, even_w_in, even_w_out, q_gain, k_gain,
        rwkv_mu, rwkv_w0, rwkv_w2, rwkv_a0, rwkv_a2, rwkv_g2, rwkv_k_k, rwkv_k_a, rwkv_r_k,
        rwkv_gn_w, rwkv_gn_b, odd_w_in, odd_w_out, sink, final_gain,
    )
    return second_block(
        x, c_2, ctx_2, c_ctx_2, l0_norm_2, l0_w_mod_2, l0_b_mod_2, l0_w_in_2, l0_mla_q_norm_2,
        l0_mla_w_uq_2, l0_mla_kv_norm_2, l0_mla_w_ukv_2, l0_mlstm_conv_w_2, l0_mlstm_conv_b_2,
        l0_mlstm_b_i_2, l0_mlstm_b_f_2, l0_mlstm_norm_2, l0_w_out_2, l1_norm_2, l1_w_mod_2,
        l1_b_mod_2, l1_w_in_2, l1_gla_w_gate_2, l1_gla_b_gate_2, l1_gla_norm_2, l1_na_rpb_2,
        l1_w_out_2, final_norm_2,
    )


_drawn_inputs = setup_inputs


def setup_inputs(seed=0):
    import zlib

    import numpy as np

    out = dict(_drawn_inputs(seed))
    spreads = {}
    factors = {'q_gain': 8.0,
     'k_gain': 8.0,
     'rwkv_w2': 4.206,
     'rwkv_k_k': 6.811,
     'rwkv_k_a': 4.948,
     'rwkv_gn_w': 8.0,
     'rwkv_gn_b': 8.0,
     'sink': 8.0,
     'l0_norm_2': 5.519,
     'l0_b_mod_2': 3.897,
     'l0_mla_q_norm_2': 8.0,
     'l0_mla_w_uq_2': 4.408,
     'l0_mla_kv_norm_2': 8.0,
     'l0_mlstm_conv_b_2': 64.0,
     'l0_mlstm_b_i_2': 63.922,
     'l0_mlstm_norm_2': 6.803,
     'l1_norm_2': 3.949,
     'l1_b_mod_2': 4.035,
     'l1_gla_norm_2': 8.0,
     'l1_na_rpb_2': 8.0}
    for name, (base, spread) in spreads.items():
        noise = np.random.default_rng([zlib.crc32(name.encode()), seed]).standard_normal(out[name].shape)
        drawn = base * np.exp(spread * noise) if base else spread * noise
        out[name] = __import__('jax').numpy.asarray(drawn.astype(out[name].dtype))
    for name, factor in factors.items():
        out[name] = (out[name] * factor).astype(out[name].dtype)
    return out
```

```python
from contextlib import ExitStack

import numpy as np

import concourse.bass as bass
from concourse import mybir

F32 = mybir.dt.float32
ALU = mybir.AluOpType
ACT = mybir.ActivationFunctionType
AX = mybir.AxisListType

P = 128
D = 1024
KT = D // P
TC = 256
T = 2 * TC
TT = T // P
DFF = 2816
FT = DFF // P
HALF_FT = FT // 2
GRID_W = 64
HD = 64
EPS, GN_EPS = 1e-6, 64e-5
NEG = -1e30
DECAY_C = float(np.exp(-0.5))
RING = 4
SLOT = HALF_FT * P
LEVELS = (1, 2, 4, 8, 16, 32, 64)
CHUNK = 64
NCH = T // CHUNK
BLOCK_LEVELS = (2, 4, 8, 16, 32)
CTX, LAT, ALL = (0, TC), (TC, T), (0, T)

VECS = [("c", 16), ("bmod0", 72), ("bmod1", 72), ("qgain", 1), ("kgain", 1), ("mu", 30), ("w0", 8), ("a0", 8),
        ("kk", 4), ("ka", 4), ("rk", 4), ("gnw", 4), ("gnb", 4), ("sink", 16), ("fgain", 8), ("c2", 16),
        ("n0", 8), ("bm0", 24), ("qn", 3), ("kvn", 2), ("cw", 24), ("cb", 8), ("bi", 1), ("bf", 1), ("mn", 4),
        ("n1", 8), ("bm1", 24), ("bg", 4), ("gln", 4), ("fn", 8)]
CONSTS = [("ident", P), ("ones", P), ("blk", P), ("rot", P), ("rotm", P), ("ident64", 64), ("sel_i", 64),
          ("sel_f", 64), ("mu", 7 * P), ("ml", 7 * P), ("su", P), ("sl", P), ("iu", P), ("il", P),
          ("nu", P), ("nl", P), ("cosa", TC), ("sina", TC), ("cosme", TC), ("sinme", TC), ("cosmo", TC),
          ("sinmo", TC), ("cosmk", TC), ("sinmk", TC), ("wmask", 2 * TC), ("namask", 2 * TC), ("reset", T), ("padkeys", 1)]
SMALL = [("w2", 512), ("a2", 512), ("g2", 512), ("wg", 256)]


def offsets(table):
    at, out = 0, {}
    for name, n in table:
        out[name] = (at, n)
        at += n
    return out, at


def ffn_slabs(f):
    return [(f"ffn_in{f}", D, 2 * FT), (f"ffn_out{f}", SLOT, 2 * KT)]


SLABS = [("mod0", D, 72), *ffn_slabs(0), ("even_in", D, 21), ("even_out", D, KT), *ffn_slabs(1),
         ("mod1", D, 72), *ffn_slabs(2), ("odd_in", D, 12), ("odd_out", D, KT), *ffn_slabs(3),
         ("mod2", D, 24), ("l0_in", D, 30), ("mla_up", D, 6), ("l0_out", D, KT),
         ("mod3", D, 24), ("l1_in", D, 29), ("l1_out", D, KT)]
SLAB_AT, N_SLABS = offsets([(name, n) for name, _, n in SLABS])
MODULATIONS = [("c", "bmod0", 72, None), ("c", "bmod1", 72, None), ("c2", "bm0", 24, "n0"), ("c2", "bm1", 24, "n1")]
MOD_AT = (0, 72, 144, 168)
NORMS = [(ALL, 0, KT, 0, 0), (ALL, 3 * KT, 4 * KT, 0, 1), (ALL, 6 * KT, 7 * KT, 4, 2),
         (ALL, 72, 72 + KT, 0, 3), (ALL, 72 + 3 * KT, 72 + 4 * KT, 0, 4), (LAT, 72 + 6 * KT, 72 + 7 * KT, 4, 5),
         (ALL, 144, 144 + KT, 2, 7), (ALL, 168, 168 + KT, 4, 8)]
GAIN_NORMS = [("fgain", 0, 6), ("fn", 4, 9)]
FFNS = [(ALL, 2 * KT), (ALL, 8 * KT), (ALL, 72 + 2 * KT), (LAT, 72 + 8 * KT)]
LINEARS = [("even_in", 21, 1), ("odd_in", 12, 4), ("l0_in", 30, 6), ("l1_in", 29, 7)]
RESIDUALS = [("even_out", ALL, 5 * KT), ("odd_out", LAT, 72 + 5 * KT), ("l0_out", ALL, 144 + 2 * KT),
             ("l1_out", LAT, 168 + 2 * KT)]
ATTENTIONS = ("even", "odd", "mla", "na")


def linear_copies_before(p, who):
    return 2 + sum((n + 1 - who) // 2 for _, n, _ in LINEARS[:p])


def attention_units(which):
    if which == "even":
        return [(t, b, qt) for t in range(4) for qt in range(TT) for b in range(2)]
    if which == "odd":
        return [(t, b, qt) for t in range(8) for qt in (2, 3) for b in range(2)]
    if which == "mla":
        return [(t, b, qt) for t in range(4) for qt in range(TT) for b in range(2)]
    return [(t, b, qt) for t in range(4) for qt in (2, 3) for b in range(2)]


def units_before(a):
    return sum(len(attention_units(which)) for which in ATTENTIONS[:a])


def build(nc, xin, ctx2, stream_k, stream_f, vecs, consts, small, nabias, out):
    VO, NV = offsets(VECS)
    CO, NCST = offsets(CONSTS)
    SO, NS = offsets(SMALL)
    with ExitStack() as ctx:
        def sb(name, shape):
            return ctx.enter_context(nc.sbuf_tensor(name, shape, F32))

        def sem(name):
            return ctx.enter_context(nc.semaphore(name))

        X = sb("residual_stream", [P, KT, T])
        H = sb("mixer_io", [P, KT, T])
        BIG = sb("projections", [P, 30, T])
        WORK = sb("work", [P, 28, T])
        ring = sb("weight_ring", [P, RING, SLOT])
        vec = sb("vectors", [P, NV])
        cst = sb("constants", [P, NCST])
        smallw = sb("small_weights", [P, NS])
        MODS = sb("modulation", [P, 192, 2])
        conds = sb("silu_conditions", [P, 2 * KT])
        stat = sb("row_statistics", [P, 2, 5])
        wstat = sb("wkv_vectors", [P, 4, NCH])
        omka = sb("one_minus_ka", [P, 4])
        mu_rest = sb("one_minus_mus", [P, 15])
        epsb = sb("epsilons", [P, 4])
        pb = [ctx.enter_context(nc.psum_tensor(f"bank{i}", [P, 512], F32)) for i in range(8)]

        def V(name, i=0, n=1):
            return vec[:, VO[name][0] + i:VO[name][0] + i + n]

        def C(name, i=0, n=None):
            o, w = CO[name]
            return cst[:, o + i:o + i + (w if n is None else n)]

        def S(name, p0, p1, i, n):
            o = SO[name][0]
            return smallw[p0:p1, o + i:o + i + n]

        def tiles(ap, n=P):
            return ap.rearrange("p (a n) -> p a n", n=n)

        def over(ap, n):
            return ap.unsqueeze(1).to_broadcast([ap.shape[0], n, ap.shape[1]])

        def along(ap, n):
            return ap.unsqueeze(2).to_broadcast([ap.shape[0], ap.shape[1], n])

        def segments(cols):
            return [(s, a, b) for s, (a, b) in enumerate((CTX, LAT)) if a >= cols[0] and b <= cols[1]]

        loaded = sem("inputs_loaded")
        prepared = sem("vectors_prepared")
        ctx2_loaded = sem("ctx2_loaded")
        nab_loaded = sem("na_bias_loaded")
        stored = sem("output_stored")
        slot_full = [sem(f"slot_full{i}") for i in range(RING)]
        slab_done = sem("slab_multiplied")
        conds_ready = sem("silu_of_condition_ready")
        mods_ready = sem("modulation_ready")
        squared = sem("tile_squared")
        summed = sem("squares_summed")
        rooted = sem("rms_ready")
        scaled = sem("tile_scaled")
        modulated = sem("tile_modulated")
        copied = [sem("tile_copied_by_scalar"), sem("tile_copied_by_vector")]
        gated = sem("gate_tile_silu")
        hidden = sem("hidden_tile_ready")
        ffn_added = sem("ffn_tile_added")
        mixer_added = sem("mixer_tile_added")
        heads_ready = sem("heads_ready")
        values_ready = sem("values_by_token_ready")
        scores_ready = sem("scores_ready")
        max_ready = sem("row_max_ready")
        probs_ready = sem("probs_ready")
        probs_scaled = sem("probs_scaled")
        probs_turned = sem("probs_transposed")
        turned_copied = sem("transposed_probs_copied")
        mixed = sem("values_mixed")
        mixed_copied = sem("mixed_values_copied")
        mixer_ready = sem("mixer_output_ready")

        def take(pe, n, i=None, per=0):
            full = 16 * (n // RING + 1)
            pe.wait_ge(slot_full[n % RING], full if i is None else i * (16 * per // RING) + full)
            return ring[:, n % RING, :]

        def setup_scalar(act):
            act.sem_inc(copied[0], 2)
            act.sem_inc(gated, 2)
            act.wait_ge(loaded, 16 * 4)
            act.wait_ge(prepared, 1)

        def setup_vector(dve):
            dve.sem_inc(copied[1], 2)
            dve.sem_inc(hidden, 2)
            dve.sem_inc(ffn_added, 4)
            dve.sem_inc(mixer_added, 4)
            dve.memset(epsb[:, 0:1], EPS)
            dve.memset(epsb[:, 1:2], HD * EPS)
            dve.memset(epsb[:, 2:3], GN_EPS).then_inc(prepared, 1)
            dve.wait_ge(loaded, 16 * 4)
            dve.tensor_scalar(omka[:, :], V("ka", 0, 4), -1.0, 1.0, ALU.mult, ALU.add)
            dve.tensor_tensor(mu_rest[:, :], V("mu", 0, 15), V("mu", 15, 15), ALU.add)
            dve.drain()
            dve.tensor_scalar(mu_rest[:, :], mu_rest[:, :], -1.0, 1.0, ALU.mult, ALU.add)

        def mod_scalar(act, m):
            act.activation(conds[:, :], V(MODULATIONS[m][0], 0, 2 * KT), ACT.Silu).then_inc(conds_ready, 1)

        def mod_tensor(pe, m):
            n, n0 = MODULATIONS[m][2], SLAB_AT[f"mod{m}"][0]
            pe.wait_ge(conds_ready, m + 1)
            if m:
                pe.wait_ge(mods_ready, m)
                pe.wait_ge(ffn_added, 4 + (0, 2, 4, 4)[m] * KT)
            with pe.Fori(0, n // RING) as i:
                for k in range(RING):
                    w = take(pe, n0 + k, i, RING)
                    for kt in range(KT):
                        mm = pe.matmul(pb[7][:, bass.ds(i * (2 * RING) + 2 * k, 2)], w[:, kt * P:(kt + 1) * P],
                                       conds[:, 2 * kt:2 * kt + 2], start=kt == 0, stop=kt == KT - 1)
                    mm.then_inc(slab_done, 1)

        def mod_vector(dve, m):
            _, bias, n, gain = MODULATIONS[m]
            o = MOD_AT[m]
            dve.wait_ge(slab_done, SLAB_AT[f"mod{m}"][0] + n)
            dve.tensor_tensor(MODS[:, o:o + n, :], pb[7][:, 0:2 * n].rearrange("p (m s) -> p m s", s=2),
                              along(V(bias, 0, n), 2), ALU.add)
            dve.drain()
            if gain is None:
                for q in (1, 4, 7):
                    sc = MODS[:, o + q * KT:o + (q + 1) * KT, :]
                    dve.tensor_scalar(sc, sc, 1.0, None, ALU.add)
                for q in (2, 8):
                    ga = MODS[:, o + q * KT:o + (q + 1) * KT, :]
                    dve.tensor_scalar(ga, ga, 0.5, None, ALU.mult)
            else:
                sc = MODS[:, o + KT:o + 2 * KT, :]
                dve.tensor_scalar(sc, sc, 1.0, None, ALU.add)
                dve.drain()
                dve.tensor_tensor(sc, sc, along(V(gain, 0, KT), 2), ALU.mult)
            dve.drain().then_inc(mods_ready, 1)

        SQ = WORK[:, 20:28, :]

        def square_tiles(act, cols, x_ready, x0):
            a, b = cols
            for kt in range(KT):
                if x_ready is not None:
                    act.wait_ge(x_ready, x0 + kt)
                act.activation(SQ[:, kt, a:b], X[:, kt, a:b], ACT.Square).then_inc(squared, 1)

        def root(act, cols, bank, place):
            a, b = cols
            act.wait_ge(summed, place + 1)
            act.activation(WORK[:, 0, a:b], pb[bank][:, a:b], ACT.Sqrt, bias=epsb[:, 0:1], scale=1.0 / D)\
               .then_inc(rooted, 1)

        def norm_scalar(act, n, x_ready=None, x0=0):
            cols, shift, scale, bank, place = NORMS[n]
            square_tiles(act, cols, x_ready, x0)
            root(act, cols, bank, place)
            act.wait_ge(mods_ready, (1, 1, 1, 2, 2, 2, 3, 4)[n])
            for kt in range(KT):
                act.wait_ge(scaled, place * KT + kt + 1)
                for s, p, q in segments(cols):
                    ins = act.activation(H[:, kt, p:q], H[:, kt, p:q], ACT.Identity,
                                         bias=MODS[:, shift + kt, s:s + 1], scale=MODS[:, scale + kt, s:s + 1])
                ins.then_inc(modulated, 1)

        def sum_squares(pe, cols, bank, place):
            a, b = cols
            for kt in range(KT):
                pe.wait_ge(squared, place * KT + kt + 1)
                mm = pe.matmul(pb[bank][:, a:b], C("ones"), SQ[:, kt, a:b], start=kt == 0, stop=kt == KT - 1)
            mm.then_inc(summed, 1)

        def norm_tensor(pe, n):
            sum_squares(pe, NORMS[n][0], NORMS[n][3], NORMS[n][4])

        def norm_vector(dve, n):
            (a, b), _, _, bank, place = NORMS[n]
            dve.wait_ge(rooted, place + 1)
            dve.reciprocal(pb[bank + 1][:, a:b], WORK[:, 0, a:b])
            dve.drain()
            for kt in range(KT):
                dve.tensor_tensor(H[:, kt, a:b], X[:, kt, a:b], pb[bank + 1][:, a:b], ALU.mult).then_inc(scaled, 1)

        def gain_norm_scalar(act, g, x_ready, x0):
            _, bank, place = GAIN_NORMS[g]
            square_tiles(act, LAT, x_ready, x0)
            root(act, LAT, bank, place)

        def gain_norm_tensor(pe, g):
            sum_squares(pe, LAT, *GAIN_NORMS[g][1:])

        def gain_norm_vector(dve, g):
            gain, bank, place = GAIN_NORMS[g]
            a, b = LAT
            dve.wait_ge(rooted, place + 1)
            dve.reciprocal(pb[bank + 1][:, a:b], WORK[:, 0, a:b])
            dve.drain()
            for kt in range(KT):
                dve.scalar_tensor_tensor(out=X[:, kt, a:b], in0=X[:, kt, a:b], scalar=V(gain, kt),
                                         in1=pb[bank + 1][:, a:b], op0=ALU.mult, op1=ALU.mult).then_inc(scaled, 1)

        def linear_tensor(pe, p):
            stage, n, norm = LINEARS[p]
            n0 = SLAB_AT[stage][0]

            def product(m, i=None):
                w = take(pe, n0 + m, i, RING)
                c = linear_copies_before(p, m % 2) - 2 + m // 2 + 1
                pe.wait_ge(copied[m % 2], c if i is None else i * 2 + c)
                for kt in range(KT):
                    if m == 0:
                        pe.wait_ge(modulated, norm * KT + kt + 1)
                    mm = pe.matmul(pb[m % 4][:, :], w[:, kt * P:(kt + 1) * P], H[:, kt, :], start=kt == 0,
                                   stop=kt == KT - 1)
                mm.then_inc(slab_done, 1)

            with pe.Fori(0, n // 4) as i:
                for k in range(4):
                    product(k, i)
            for m in range(n // 4 * 4, n):
                product(m)

        def linear_copies(eng, copy, p, who):
            stage, n, _ = LINEARS[p]

            def one(m, i=None):
                d = SLAB_AT[stage][0] + m + 1
                eng.wait_ge(slab_done, d if i is None else i * 4 + d)
                dst = BIG[:, m, :] if i is None else BIG[:, bass.ds(i * 4 + m, 1), :].rearrange("p o t -> p (o t)")
                copy(dst, pb[m % 4][:, :]).then_inc(copied[who], 1)

            with eng.Fori(0, n // 4) as i:
                for k in range(who, 4, 2):
                    one(k, i)
            for m in range(n // 4 * 4, n):
                if m % 2 == who:
                    one(m)

        def linear_scalar(act, p):
            linear_copies(act, lambda d, s: act.activation(d, s, ACT.Copy), p, 0)

        def linear_vector(dve, p):
            linear_copies(dve, dve.tensor_copy, p, 1)

        def all_copied(eng, p, who):
            eng.wait_ge(copied[who], linear_copies_before(p + 1, who))

        def add_tiles(dve, cols, gate, slabs_each, n0, bank0, added):
            with dve.Fori(0, KT // 4) as i:
                for k in range(4):
                    dve.wait_ge(slab_done, i * (4 * slabs_each) + (n0 + slabs_each * (k + 1)))
                    for s, p, q in segments(cols):
                        x = X[:, bass.ds(i * 4 + k, 1), p:q].rearrange("p o t -> p (o t)")
                        g = MODS[:, bass.ds(i * 4 + (gate + k), 1), s:s + 1].rearrange("p o t -> p (o t)")
                        ins = dve.scalar_tensor_tensor(out=x, in0=pb[bank0 + k][:, p:q], scalar=g, in1=x,
                                                       op0=ALU.mult, op1=ALU.add)
                    ins.then_inc(added, 1)

        def residual_tensor(pe, r):
            stage, (a, b), _ = RESIDUALS[r]
            pe.wait_ge(mixer_ready, r + 1)
            with pe.Fori(0, KT // 4) as i:
                for k in range(4):
                    w = take(pe, SLAB_AT[stage][0] + k, i, 4)
                    pe.wait_ge(mixer_added, i * 4 + (r * KT + k + 1))
                    for kt in range(KT):
                        mm = pe.matmul(pb[k][:, a:b], w[:, kt * P:(kt + 1) * P], H[:, kt, a:b], start=kt == 0,
                                       stop=kt == KT - 1)
                    mm.then_inc(slab_done, 1)

        def residual_vector(dve, r):
            stage, cols, gate = RESIDUALS[r]
            add_tiles(dve, cols, gate, 1, SLAB_AT[stage][0], 0, mixer_added)

        def ffn_tensor(pe, f):
            a, b = FFNS[f][0]
            n0, norm = SLAB_AT[f"ffn_in{f}"][0], (0, 2, 3, 5)[f]
            with pe.Fori(0, FT // 2) as i:
                for j in range(2):
                    for part, free in ((0, gated), (1, hidden)):
                        k = 2 * j + part
                        w = take(pe, n0 + k, i, 4)
                        pe.wait_ge(free, i * 2 + (f * FT + j + 1))
                        for kt in range(KT):
                            if k == 0:
                                pe.wait_ge(modulated, norm * KT + kt + 1)
                            mm = pe.matmul(pb[k][:, a:b], w[:, kt * P:(kt + 1) * P], H[:, kt, a:b], start=kt == 0,
                                           stop=kt == KT - 1)
                        mm.then_inc(slab_done, 1)
            n0 = SLAB_AT[f"ffn_out{f}"][0]
            pe.wait_ge(hidden, 2 + (f + 1) * FT)
            with pe.Fori(0, KT // 4) as i:
                for k in range(4):
                    pe.wait_ge(ffn_added, i * 4 + (f * KT + k + 1))
                    for half in range(2):
                        w = take(pe, n0 + 2 * k + half, i, 8)
                        for t in range(HALF_FT):
                            mm = pe.matmul(pb[4 + k][:, a:b], w[:, t * P:(t + 1) * P],
                                           BIG[:, half * HALF_FT + t, a:b], start=half + t == 0,
                                           stop=half * HALF_FT + t == FT - 1)
                        mm.then_inc(slab_done, 1)

        def ffn_scalar(act, f):
            (a, b), n0 = FFNS[f][0], SLAB_AT[f"ffn_in{f}"][0]
            with act.Fori(0, FT // 2) as i:
                for j in range(2):
                    act.wait_ge(slab_done, i * 4 + (n0 + 2 * j + 1))
                    act.wait_ge(hidden, i * 2 + (f * FT + j + 1))
                    act.activation(WORK[:, j, a:b], pb[2 * j][:, a:b], ACT.Silu).then_inc(gated, 1)

        def ffn_vector(dve, f):
            (a, b), gate = FFNS[f]
            n0 = SLAB_AT[f"ffn_in{f}"][0]
            with dve.Fori(0, FT // 2) as i:
                for j in range(2):
                    dve.wait_ge(slab_done, i * 4 + (n0 + 2 * j + 2))
                    dve.wait_ge(gated, i * 2 + (2 + f * FT + j + 1))
                    h = BIG[:, bass.ds(i * 2 + j, 1), a:b].rearrange("p o t -> p (o t)")
                    dve.tensor_tensor(h, WORK[:, j, a:b], pb[2 * j + 1][:, a:b], ALU.mult).then_inc(hidden, 1)
            add_tiles(dve, (a, b), gate, 2, SLAB_AT[f"ffn_out{f}"][0], 4, ffn_added)

        def attention_operands(which, t, b, qt):
            q0, nk = qt * P, (TC if qt < 2 else T)
            rows = slice(HD * b, HD * b + HD)
            if which == "even":
                pairs = [(BIG[rows, t, q0:q0 + P], BIG[rows, 4, 0:nk])]
                return pairs, nk, H[rows, t, q0:q0 + P], HD * b
            if which == "odd":
                pairs = [(BIG[rows, t, q0:q0 + P], BIG[rows, 8 + t // 4, 0:nk])]
                return pairs, nk, H[rows, t, q0:q0 + P], t // 4 * P + HD * b
            if which == "mla":
                rope = slice(64 * (1 - b), 64 * (1 - b) + 32)
                pairs = [(WORK[rows, 2 * t + b, q0:q0 + P], WORK[rows, 8 + t, 0:nk]),
                         (WORK[rope, 2 * t + b, q0:q0 + P], BIG[rope, 29, 0:nk])]
                return pairs, nk, H[rows, t, q0:q0 + P], t * P + HD * b
            pairs = [(BIG[rows, 8 + t, q0:q0 + P], BIG[rows, 12 + t, 0:nk])]
            return pairs, nk, H[rows, 4 + t, q0:q0 + P], t * P + HD * b

        def attend_tensor(pe, a):
            which, u0 = ATTENTIONS[a], units_before(a)
            units = attention_units(which)
            n = len(units)
            pe.wait_ge(heads_ready, a + 1)
            pe.wait_ge(values_ready, a + 1)
            for it in range(n + 2):
                if it < n:
                    pairs, nk, _, _ = attention_operands(which, *units[it])
                    if it >= 2:
                        pe.wait_ge(probs_ready, u0 + it - 1)
                    for i, (q, k) in enumerate(pairs):
                        mm = pe.matmul(pb[it % 2][:, 0:nk], q, k, start=i == 0, stop=i == len(pairs) - 1)
                    mm.then_inc(scores_ready, 1)
                u = it - 1
                if 0 <= u < n:
                    nk = attention_operands(which, *units[u])[1]
                    pe.wait_ge(probs_scaled, u0 + u + 1)
                    if u >= 2:
                        pe.wait_ge(turned_copied, u0 + u - 1)
                    for i in range(nk // P):
                        mm = pe.transpose(pb[2 + u % 2][:, i * P:(i + 1) * P], WORK[:, 20 + u % 2, i * P:(i + 1) * P],
                                          C("ident"))
                    mm.then_inc(probs_turned, 1)
                u = it - 2
                if 0 <= u < n:
                    _, nk, _, ch = attention_operands(which, *units[u])
                    b = units[u][1]
                    pe.wait_ge(turned_copied, u0 + u + 1)
                    if u >= 2:
                        pe.wait_ge(mixed_copied, u0 + u - 1)
                    for i in range(nk // P):
                        mm = pe.matmul(pb[4 + u % 2][HD * b:HD * b + HD, 0:P], WORK[:, 12 + i, ch:ch + HD],
                                       WORK[:, 22 + u % 2, i * P:(i + 1) * P], start=i == 0, stop=i == nk // P - 1)
                    mm.then_inc(mixed, 1)

        def attend_vector(dve, a):
            which, u0 = ATTENTIONS[a], units_before(a)
            units = attention_units(which)
            n = len(units)
            if which == "na":
                dve.wait_ge(nab_loaded, 16)
            for it in range(n + 3):
                if it < n:
                    t, b, qt = units[it]
                    nk = attention_operands(which, t, b, qt)[1]
                    sc, st = pb[it % 2], stat[:, it % 2, :]
                    dve.wait_ge(scores_ready, u0 + it + 1)
                    if which in ("odd", "na"):
                        mask = C("wmask" if which == "odd" else "namask", (qt - 2) * TC, TC)
                        dve.tensor_tensor(sc[:, TC:T], sc[:, TC:T], mask, ALU.add)
                        dve.drain()
                    if which == "na":
                        bias = WORK[:, 0:8, :].rearrange("p a (b k) -> p (a b) k", k=TC)[:, it, :]
                        dve.tensor_tensor(sc[:, TC:T], sc[:, TC:T], bias, ALU.add)
                        dve.drain()
                    ins = dve.tensor_reduce(st[:, 0:1], sc[:, 0:nk], AX.X, ALU.max, negate=True)
                    if which == "odd":
                        dve.drain()
                        sink = V("sink", 8 * (t // 4) + 4 * b + t % 4)
                        ins = dve.scalar_tensor_tensor(out=st[:, 0:1], in0=sink, scalar=-1.0, in1=st[:, 0:1],
                                                       op0=ALU.mult, op1=ALU.min)
                        if qt == 3:
                            dve.drain()
                            ins = dve.tensor_scalar(st[:, 0:1], st[:, 0:1], 0.0, None, ALU.min)
                    ins.then_inc(max_ready, 1)
                u = it - 1
                if 0 <= u < n:
                    nk = attention_operands(which, *units[u])[1]
                    st, probs = stat[:, u % 2, :], WORK[:, 20 + u % 2, 0:nk]
                    dve.wait_ge(probs_ready, u0 + u + 1)
                    if which == "odd":
                        dve.tensor_tensor(st[:, 1:2], st[:, 1:2], st[:, 2:3], ALU.add)
                        dve.drain()
                        if units[u][2] == 3:
                            dve.scalar_tensor_tensor(out=st[:, 1:2], in0=C("padkeys"), scalar=st[:, 4:5],
                                                     in1=st[:, 1:2], op0=ALU.mult, op1=ALU.add)
                            dve.drain()
                    dve.reciprocal(st[:, 3:4], st[:, 1:2])
                    dve.drain()
                    dve.tensor_scalar(probs, probs, st[:, 3:4], None, ALU.mult).then_inc(probs_scaled, 1)
                u = it - 3
                if 0 <= u < n:
                    b = units[u][1]
                    o = attention_operands(which, *units[u])[2]
                    dve.wait_ge(mixed, u0 + u + 1)
                    dve.tensor_copy(o, pb[4 + u % 2][HD * b:HD * b + HD, 0:P]).then_inc(mixed_copied, 1)
            if which == "odd":
                dve.drain().then_inc(mixer_ready, 1)

        def attend_scalar(act, a):
            which, u0 = ATTENTIONS[a], units_before(a)
            units = attention_units(which)
            n = len(units)
            for it in range(n + 1):
                if it < n:
                    t, b, qt = units[it]
                    nk = attention_operands(which, t, b, qt)[1]
                    st = stat[:, it % 2, :]
                    act.wait_ge(max_ready, u0 + it + 1)
                    if it >= 2:
                        act.wait_ge(probs_turned, u0 + it - 1)
                    if which == "odd":
                        act.activation(st[:, 2:3], V("sink", 8 * (t // 4) + 4 * b + t % 4), ACT.Exp, bias=st[:, 0:1])
                        if qt == 3:
                            act.activation(st[:, 4:5], st[:, 0:1], ACT.Exp)
                    act.activation(WORK[:, 20 + it % 2, 0:nk], pb[it % 2][:, 0:nk], ACT.Exp, bias=st[:, 0:1],
                                   accum_out=st[:, 1:2]).then_inc(probs_ready, 1)
                u = it - 1
                if 0 <= u < n:
                    nk = attention_operands(which, *units[u])[1]
                    act.wait_ge(probs_turned, u0 + u + 1)
                    if u >= 2:
                        act.wait_ge(mixed, u0 + u - 1)
                    act.activation(WORK[:, 22 + u % 2, 0:nk], pb[2 + u % 2][:, 0:nk], ACT.Copy)\
                       .then_inc(turned_copied, 1)

        qk_squared, qk_summed, qk_rooted = sem("head_squared"), sem("head_squares_summed"), sem("head_rms_ready")
        qk_normed, qk_turned = sem("head_normed"), sem("head_rotated_half_ready")
        values_turned = sem("values_transposed")
        q_turned, q_rotated, k_turned = sem("query_half_ready"), sem("queries_rotated"), sem("key_half_ready")
        low_squared, low_summed, low_rooted = sem("low_rank_squared"), sem("low_rank_summed"), sem("low_rank_rms_ready")
        low_normed = sem("low_rank_normed")
        q_copied, k_copied, v_copied = sem("mla_query_copied"), sem("mla_key_copied"), sem("mla_value_copied")
        mq_turned, mq_rotated, mk_turned = sem("mla_query_half_ready"), sem("mla_queries_rotated"), sem("mla_key_half_ready")

        def rotate(dve, jobs, scale, scratch, turned):
            for i, (x, bank, cos, sin) in enumerate(jobs):
                tmp = scratch[:, i, :]
                dve.scalar_tensor_tensor(out=tmp[:, 0:TC], in0=x[:, TC:T], scalar=scale, in1=C(cos), op0=ALU.mult,
                                         op1=ALU.mult)
                dve.wait_ge(turned, i + 1)
                dve.scalar_tensor_tensor(out=tmp[:, TC:T], in0=bank[:, TC:T], scalar=scale, in1=C(sin), op0=ALU.mult,
                                         op1=ALU.mult)
            dve.drain()
            for i, (x, _, _, _) in enumerate(jobs):
                dve.tensor_tensor(x[:, TC:T], scratch[:, i, 0:TC], scratch[:, i, TC:T], ALU.add)

        def turn_values(pe, src, n, bank0):
            for tt in range(TT):
                for j in range(n):
                    mm = pe.transpose(pb[bank0 + tt][:, j * P:(j + 1) * P], src[:, j, tt * P:(tt + 1) * P], C("ident"))
            return mm

        def even_heads_scalar(act):
            all_copied(act, 0, 1)
            act.drain()
            for i in range(5):
                act.activation(WORK[:, i, :], BIG[:, i, :], ACT.Square).then_inc(qk_squared, 1)
            for i in range(5):
                act.wait_ge(qk_summed, i + 1)
                act.activation(WORK[:, i, :], pb[i][:, :], ACT.Sqrt, bias=epsb[:, 1:2] if i < 4 else epsb[:, 0:1],
                               scale=1.0 if i < 4 else 1.0 / HD).then_inc(qk_rooted, 1)
            act.wait_ge(values_turned, 1)
            act.activation(WORK[:, 12:16, 0:P], tiles(pb[5][:, :]), ACT.Copy).then_inc(values_ready, 1)

        def even_heads_tensor(pe):
            all_copied(pe, 0, 0)
            all_copied(pe, 0, 1)
            for i in range(5):
                pe.wait_ge(qk_squared, i + 1)
                pe.matmul(pb[i][:, :], C("blk"), WORK[:, i, :], start=True, stop=True).then_inc(qk_summed, 1)
            for tt in range(TT):
                mm = pe.transpose(pb[5][:, tt * P:(tt + 1) * P], BIG[:, 5, tt * P:(tt + 1) * P], C("ident"))
            mm.then_inc(values_turned, 1)
            for i in range(5):
                pe.wait_ge(qk_normed, i + 1)
                pe.matmul(pb[i][:, TC:T], C("rot"), BIG[:, i, TC:T], start=True, stop=True).then_inc(qk_turned, 1)

        def even_heads_vector(dve):
            for i in range(5):
                dve.wait_ge(qk_rooted, i + 1)
                dve.reciprocal(pb[i][:, :], WORK[:, i, :])
                dve.drain()
                dve.scalar_tensor_tensor(out=BIG[:, i, :], in0=BIG[:, i, :], scalar=V("qgain" if i < 4 else "kgain"),
                                         in1=pb[i][:, :], op0=ALU.mult, op1=ALU.mult).then_inc(qk_normed, 1)
            dve.drain()
            rotate(dve, [(BIG[:, i, :], pb[i], "cosa", "sina") for i in range(5)], 1.0, WORK[:, 0:5, :], qk_turned)
            dve.drain().then_inc(heads_ready, 1)

        def odd_heads_tensor(pe):
            all_copied(pe, 1, 0)
            all_copied(pe, 1, 1)
            for i in range(8):
                pe.matmul(pb[i][:, TC:T], C("rot"), BIG[:, i, TC:T], start=True, stop=True).then_inc(q_turned, 1)
            pe.wait_ge(q_rotated, 1)
            for i in range(2):
                pe.matmul(pb[i][:, TC:T], C("rot"), BIG[:, 8 + i, TC:T], start=True, stop=True).then_inc(k_turned, 1)
            turn_values(pe, BIG[:, 10:12, :], 2, 2).then_inc(values_turned, 1)

        def odd_heads_vector(dve):
            all_copied(dve, 1, 0)
            rotate(dve, [(BIG[:, i, :], pb[i], "cosa", "sina") for i in range(8)], HD ** -0.5, WORK[:, 0:8, :], q_turned)
            dve.drain().then_inc(q_rotated, 1)
            rotate(dve, [(BIG[:, 8 + i, :], pb[i], "cosa", "sina") for i in range(2)], 1.0, WORK[:, 0:2, :], k_turned)
            dve.drain().then_inc(heads_ready, 1)

        def odd_heads_scalar(act):
            act.wait_ge(values_turned, 2)
            for tt in range(TT):
                ins = act.activation(WORK[:, 12 + tt, 0:2 * P], pb[2 + tt][:, 0:2 * P], ACT.Copy)
            ins.then_inc(values_ready, 1)

        UP0 = SLAB_AT["mla_up"][0]

        def mla_heads_scalar(act):
            all_copied(act, 2, 1)
            act.drain()
            for i in range(5):
                act.activation(WORK[:, i, :], BIG[:, i, :], ACT.Square).then_inc(low_squared, 1)
            for i, n in enumerate((3, 2)):
                act.wait_ge(low_summed, i + 1)
                act.activation(WORK[:, 5 + i, :], pb[i][:, :], ACT.Sqrt, bias=epsb[:, 0:1], scale=1.0 / (n * P))\
                   .then_inc(low_rooted, 1)
            act.wait_ge(low_normed, 5)
            for h in range(8):
                act.wait_ge(slab_done, UP0 + h // 2 + 1)
                act.activation(WORK[:, h, :], pb[h][:, :], ACT.Copy, scale=96 ** -0.5).then_inc(q_copied, 1)
            act.wait_ge(slab_done, UP0 + 5)
            for t in range(4):
                act.activation(WORK[:, 8 + t, :], pb[t][:, :], ACT.Copy).then_inc(k_copied, 1)
            act.wait_ge(values_turned, 3)
            for tt in range(TT):
                ins = act.activation(WORK[:, 12 + tt, :], pb[4 + tt][:, :], ACT.Copy)
            ins.then_inc(values_ready, 1)

        def mla_heads_tensor(pe):
            all_copied(pe, 2, 0)
            all_copied(pe, 2, 1)
            for i in range(5):
                bank, first, last = (0, 0, 2) if i < 3 else (1, 3, 4)
                pe.wait_ge(low_squared, i + 1)
                mm = pe.matmul(pb[bank][:, :], C("ones"), WORK[:, i, :], start=i == first, stop=i == last)
                if i == last:
                    mm.then_inc(low_summed, 1)
            pe.wait_ge(low_normed, 3)
            for n in range(4):
                w = take(pe, UP0 + n)
                if n == 3:
                    pe.wait_ge(low_normed, 5)
                for j in range(2):
                    for i in range(3):
                        mm = pe.matmul(pb[2 * n + j][:, :], w[:, (3 * j + i) * P:(3 * j + i + 1) * P], BIG[:, i, :],
                                       start=i == 0, stop=i == 2)
                mm.then_inc(slab_done, 1)
            for n in range(2):
                w = take(pe, UP0 + 4 + n)
                pe.wait_ge(q_copied, 4 * n + 4)
                for t in range(4):
                    for i in range(2):
                        mm = pe.matmul(pb[4 * n + t][:, :], w[:, (2 * t + i) * P:(2 * t + i + 1) * P], BIG[:, 3 + i, :],
                                       start=i == 0, stop=i == 1)
                mm.then_inc(slab_done, 1)
            for h in range(8):
                pe.wait_ge(*((k_copied, h + 1) if h < 4 else (v_copied, h - 3)))
                pe.matmul(pb[h][:, TC:T], C("rotm"), WORK[:, h, TC:T], start=True, stop=True).then_inc(mq_turned, 1)
            pe.wait_ge(mq_rotated, 1)
            pe.matmul(pb[0][:, TC:T], C("rotm"), BIG[:, 29, TC:T], start=True, stop=True).then_inc(mk_turned, 1)
            turn_values(pe, WORK[:, 16:20, :], 4, 4).then_inc(values_turned, 1)

        def mla_heads_vector(dve):
            for i in range(2):
                dve.wait_ge(low_rooted, i + 1)
                dve.reciprocal(pb[6 + i][:, :], WORK[:, 5 + i, :])
            dve.drain()
            for i in range(5):
                dve.scalar_tensor_tensor(out=BIG[:, i, :], in0=BIG[:, i, :], scalar=V("qn", i) if i < 3 else V("kvn", i - 3),
                                         in1=pb[6 + i // 3][:, :], op0=ALU.mult, op1=ALU.mult).then_inc(low_normed, 1)
            dve.wait_ge(slab_done, UP0 + 6)
            for t in range(4):
                dve.tensor_copy(WORK[:, 16 + t, :], pb[4 + t][:, :]).then_inc(v_copied, 1)
            dve.wait_ge(q_copied, 8)
            rotate(dve, [(WORK[:, h, :], pb[h], "cosmo" if h % 2 else "cosme", "sinmo" if h % 2 else "sinme")
                         for h in range(8)], 1.0, WORK[:, 20:28, :], mq_turned)
            dve.drain().then_inc(mq_rotated, 1)
            rotate(dve, [(BIG[:, 29, :], pb[0], "cosmk", "sinmk")], 1.0, WORK[:, 20:21, :], mk_turned)
            dve.drain().then_inc(heads_ready, 1)

        def na_heads_gpsimd(pool):
            pool.wait_ge(modulated, 8 * KT)
            pool.dma_start(WORK[:, 0:8, :].rearrange("p a b -> p (a b)"), nabias).then_inc(nab_loaded, 16)

        def na_heads_tensor(pe):
            all_copied(pe, 3, 0)
            all_copied(pe, 3, 1)
            turn_values(pe, BIG[:, 16:20, :], 4, 0).then_inc(values_turned, 1)

        def na_heads_scalar(act):
            all_copied(act, 3, 1)
            act.drain()
            for i in (0, 1, 8, 9, 10, 11):
                ins = act.activation(BIG[:, i, TC:T], BIG[:, i, TC:T], ACT.Copy, scale=HD ** -0.5)
            ins.then_inc(heads_ready, 1)
            act.wait_ge(values_turned, 4)
            for tt in range(TT):
                ins = act.activation(WORK[:, 12 + tt, :], pb[tt][:, :], ACT.Copy)
            ins.then_inc(values_ready, 1)

        def add_neighbours(dve, jobs):
            for x, y, before, after in jobs:
                for a, b in (CTX, LAT):
                    dve.scalar_tensor_tensor(out=y[:, a + 1:b], in0=x[:, a:b - 1], scalar=before, in1=y[:, a + 1:b],
                                             op0=ALU.mult, op1=ALU.add)
            dve.drain()
            for x, y, before, after in jobs:
                for a, b in (CTX, LAT):
                    dve.scalar_tensor_tensor(out=y[:, a:b - 1], in0=x[:, a + 1:b], scalar=after, in1=y[:, a:b - 1],
                                             op0=ALU.mult, op1=ALU.add)
            dve.drain()

        R_, K_, V_, WL, AL, GL = 5, 9, 13, 17, 18, 19
        KK = BIG[:, 0:4, :]
        EIT, FF = BIG[:, 20:24, :], BIG[:, 24:28, :]
        RR = WORK[:, 0:4, :]
        VTOK = WORK[:, 4:8, :]
        TOK = WORK[:, 8:11, :]
        SIG, CUM, AA, EX, AL_, BE_, KA_ = (WORK[:, 11 + i, :] for i in range(7))
        MT, MB, TI, TTI, XS = ([WORK[:, 18 + 5 * hb + i, :] for hb in range(2)] for i in range(5))
        NGH = [BIG[:, 28 + hb, :] for hb in range(2)]
        shifted, ranks_ready = sem("tokens_shifted"), sem("low_ranks_ready")
        kk_squared, kk_summed, kk_rooted, kk_ready = (sem(f"removal_key_{x}") for x in ("squared", "summed", "rms", "ready"))
        v_turned = sem("rwkv_values_transposed")
        lora_ready, rates_ready = sem("decay_and_rate_products"), sem("decay_and_rate_ready")
        decay_summed, decays_ready = sem("log_decays_summed"), sem("decays_ready")
        factors_ready = sem("alpha_beta_kappa_rho_ready")
        factors_turned, factors_by_token = sem("factors_transposed"), sem("factors_by_token_ready")
        within_ready, triangles_ready = sem("alpha_beta_products"), sem("triangles_masked")
        t_started, level_masked = sem("inverse_started"), sem("level_mask_applied")
        x_ready, x_copied = sem("off_block_product_ready"), sem("off_block_product_copied")
        z_ready, t_updated = sem("inverse_update_ready"), sem("inverse_updated")
        mixes_ready, mixes_masked = sem("kappa_rho_products"), sem("kappa_rho_masked")
        kv_ready, rhs_ready = sem("kappa_alpha_values_ready"), sem("right_sides_ready")
        solved, solved_copied = sem("right_sides_solved"), sem("solutions_copied")
        group_ready, group_added, inputs_copied = sem("group_products"), sem("group_added"), sem("state_inputs_copied")
        step_ready, state_ready = sem("state_products"), sem("state_ready")

        def wkv_features_vector(dve):
            all_copied(dve, 0, 0)
            for i in range(15):
                x, y = BIG[:, 6 + i, :], BIG[:, 5 + i, :]
                dve.tensor_scalar(y, x, mu_rest[:, i:i + 1], None, ALU.mult)
                dve.drain()
                add_neighbours(dve, [(x, y, V("mu", i), V("mu", 15 + i))])
            for j in range(4):
                dve.tensor_scalar(KK[:, j, :], BIG[:, K_ + j, :], V("kk", j), None, ALU.mult)
            dve.drain().then_inc(shifted, 1)
            dve.wait_ge(v_turned, 1)
            for tt in range(TT):
                dve.tensor_copy(VTOK[:, tt, :], pb[4 + tt][:, :])
            for j in range(4):
                dve.wait_ge(kk_rooted, j + 1)
                dve.reciprocal(WORK[:, 8 + j, :], WORK[:, 8 + j, :])
            dve.drain()
            for j in range(4):
                dve.tensor_tensor(KK[:, j, :], KK[:, j, :], WORK[:, 8 + j, :], ALU.mult)
            dve.drain().then_inc(kk_ready, 1)

        def wkv_features_scalar(act):
            act.wait_ge(shifted, 1)
            for j in range(4):
                act.activation(WORK[:, 8 + j, :], KK[:, j, :], ACT.Square).then_inc(kk_squared, 1)
            act.activation(BIG[:, WL, :], BIG[:, WL, :], ACT.Tanh)
            act.activation(BIG[:, GL, :], BIG[:, GL, :], ACT.Sigmoid).then_inc(ranks_ready, 1)
            for j in range(4):
                act.wait_ge(kk_summed, j + 1)
                act.activation(WORK[:, 8 + j, :], pb[j][:, :], ACT.Sqrt, bias=epsb[:, 0:1]).then_inc(kk_rooted, 1)

        def wkv_features_tensor(pe):
            pe.wait_ge(shifted, 1)
            turn_values(pe, BIG[:, V_:V_ + 4, :], 4, 4).then_inc(v_turned, 1)
            for j in range(4):
                pe.wait_ge(kk_squared, j + 1)
                pe.matmul(pb[j][:, :], C("blk"), WORK[:, 8 + j, :], start=True, stop=True).then_inc(kk_summed, 1)

        NLEV = 2 * len(BLOCK_LEVELS)

        def chunk_order(d):
            return list(range(NCH)) if d == 0 else [3, 2, 1, 0, 7, 6, 5, 4]

        def heads_of(j):
            return [(hb, slice(HD * hb, HD * hb + HD), slice(j * P + hb * HD, j * P + hb * HD + HD)) for hb in (0, 1)]

        def tok(i):
            return slice(i * P, (i + 1) * P)

        def wkv_tensor(pe):
            pe.wait_ge(ranks_ready, 1)
            pe.wait_ge(kk_rooted, 4)
            for d in range(2):
                if d:
                    pe.wait_ge(state_ready, NCH)
                for j in range(4):
                    wkv_group_tensor(pe, d, j, 4 * d + j)
                for s, c in enumerate(chunk_order(d)):
                    if s:
                        st = tiles(WORK[:, 11 + (s - 1) % 2, 0:4 * HD], HD)
                        pe.wait_ge(state_ready, NCH * d + s)
                        for j in range(4):
                            for hb, rows, _ in heads_of(j):
                                o = slice(j * HD, (j + 1) * HD)
                                cc = slice(c * HD, (c + 1) * HD)
                                mm = pe.matmul(pb[hb][rows, o], st[rows, j, :], RR[rows, j, cc], start=True, stop=True)
                                if s < NCH - 1:
                                    mm = pe.matmul(pb[2 + hb][rows, o], EIT[rows, j, cc], st[rows, j, :], start=True,
                                                   stop=True)
                        mm.then_inc(step_ready, 1)

        def wkv_group_tensor(pe, d, j, g):
            low = slice(HD * d, HD * d + HD)
            pe.matmul(pb[0][:, :], S("w2", HD * d, HD * d + HD, j * P, P), BIG[low, WL, :], start=True, stop=True)
            pe.matmul(pb[1][:, :], S("a2", HD * d, HD * d + HD, j * P, P), BIG[low, AL, :], start=True, stop=True)\
              .then_inc(lora_ready, 1)
            pe.wait_ge(factors_ready, g + 1)
            if g:
                pe.wait_ge(inputs_copied, g)
            for i, x in enumerate((AL_, BE_, KA_)):
                for tt in range(TT):
                    mm = pe.transpose(pb[i][:, tok(tt)], x[:, tok(tt)], C("ident"))
            mm.then_inc(factors_turned, 1)
            for hb, rows, _ in heads_of(j):
                for tt in range(TT):
                    pe.matmul(pb[4 + hb][:, tok(tt)], BE_[rows, tok(tt)], AL_[rows, tok(tt)], start=True, stop=True)
                for tt in range(TT):
                    mm = pe.matmul(pb[6 + hb][:, tok(tt)], AL_[rows, tok(tt)], BE_[rows, tok(tt)], start=True, stop=True)
            mm.then_inc(within_ready, 1)
            pe.wait_ge(factors_by_token, g + 1)
            pe.wait_ge(t_started, g + 1)
            for li in range(len(BLOCK_LEVELS)):
                for hb in range(2):
                    q = NLEV * g + 2 * li + hb
                    pe.wait_ge(level_masked, q + 1)
                    if li:
                        pe.wait_ge(t_updated, q - 1)
                    for tt in range(TT):
                        mm = pe.matmul(pb[hb][:, tok(tt)], MB[hb][:, tok(tt)], TI[hb][:, tok(tt)], start=True, stop=True)
                    mm.then_inc(x_ready, 1)
                for hb in range(2):
                    q = NLEV * g + 2 * li + hb
                    pe.wait_ge(x_copied, q + 1)
                    for tt in range(TT):
                        pe.matmul(pb[2 + hb][:, tok(tt)], TTI[hb][:, tok(tt)], XS[hb][:, tok(tt)], start=True, stop=True)
                    for tt in range(TT):
                        mm = pe.matmul(pb[4 + hb][:, tok(tt)], XS[hb][:, tok(tt)], TTI[hb][:, tok(tt)], start=True,
                                       stop=True)
                    mm.then_inc(z_ready, 1)
            pe.wait_ge(t_updated, NLEV * (g + 1))
            for hb, rows, _ in heads_of(j):
                for tt in range(TT):
                    pe.matmul(pb[hb][:, tok(tt)], KA_[rows, tok(tt)], AL_[rows, tok(tt)], start=True, stop=True)
                for tt in range(TT):
                    pe.matmul(pb[2 + hb][:, tok(tt)], KA_[rows, tok(tt)], RR[rows, j, tok(tt)], start=True, stop=True)
                for tt in range(TT):
                    mm = pe.matmul(pb[4 + hb][:, tok(tt)], BE_[rows, tok(tt)], RR[rows, j, tok(tt)], start=True, stop=True)
            mm.then_inc(mixes_ready, 1)
            pe.wait_ge(mixes_masked, g + 1)
            for hb, _, ch in heads_of(j):
                for tt in range(TT):
                    mm = pe.matmul(pb[6 + hb][:, tt * HD:(tt + 1) * HD], MB[hb][:, tok(tt)], VTOK[:, tt, ch], start=True,
                                   stop=True)
            mm.then_inc(kv_ready, 1)
            pe.wait_ge(rhs_ready, g + 1)
            for hb in range(2):
                for tt in range(TT):
                    mm = pe.matmul(pb[hb][:, tok(tt)], TTI[hb][:, tok(tt)], TI[hb][:, tok(tt)], start=True, stop=True)
            mm.then_inc(solved, 1)
            pe.wait_ge(solved_copied, g + 1)
            for hb, rows, ch in heads_of(j):
                gh = tiles(NGH[hb])
                for tt in range(TT):
                    pe.matmul(pb[2][rows, tok(tt)], gh[:, tt, 0:HD], MT[hb][:, tok(tt)], start=True, stop=True)
                for tt in range(TT):
                    pe.matmul(pb[3][rows, tok(tt)], VTOK[:, tt, ch], XS[hb][:, tok(tt)], start=True, stop=False)
                    pe.matmul(pb[3][rows, tok(tt)], gh[:, tt, HD:P], MT[hb][:, tok(tt)], start=False, stop=True)
                for half in range(2):
                    tr = slice(HD * half, HD * half + HD)
                    for tt in range(TT):
                        o = slice(tt * HD, (tt + 1) * HD)
                        hc = slice(tt * P + HD * hb, tt * P + HD * hb + HD)
                        pe.matmul(pb[4 + 2 * half][rows, o], gh[tr, tt, 0:HD], TOK[tr, 1, hc], start=True, stop=True)
                        pe.matmul(pb[5 + 2 * half][rows, o], TOK[tr, 2, hc], VTOK[tr, tt, ch], start=True, stop=False)
                        mm = pe.matmul(pb[5 + 2 * half][rows, o], TOK[tr, 1, hc], gh[tr, tt, HD:P], start=False, stop=True)
            mm.then_inc(group_ready, 1)

        def wkv_scalar(act):
            act.wait_ge(kk_ready, 1)
            for g in range(8):
                d, j = g // 4, g % 4
                act.wait_ge(lora_ready, g + 1)
                act.activation(SIG, pb[0][:, :], ACT.Sigmoid, bias=V("w0", 4 * d + j))
                act.activation(AA, pb[1][:, :], ACT.Sigmoid, bias=V("a0", 4 * d + j)).then_inc(rates_ready, 1)
                act.wait_ge(decay_summed, g + 1)
                act.activation(AL_, SIG, ACT.Exp, scale=-DECAY_C)
                act.activation(EX, CUM, ACT.Exp, scale=-DECAY_C)
                act.activation(KA_, CUM, ACT.Exp, scale=DECAY_C).then_inc(decays_ready, 1)
                act.wait_ge(factors_turned, g + 1)
                for i in range(3):
                    ins = act.activation(TOK[:, i, :], pb[i][:, :], ACT.Copy)
                ins.then_inc(factors_by_token, 1)
                for q in range(NLEV * g, NLEV * (g + 1)):
                    act.wait_ge(x_ready, q + 1)
                    act.activation(XS[q % 2], pb[q % 2][:, :], ACT.Copy).then_inc(x_copied, 1)
                act.wait_ge(t_updated, NLEV * (g + 1))
                for hb in range(2):
                    act.activation(tiles(TI[hb])[:, :, 0:HD], tiles(TOK[:, 0, :])[:, :, HD * hb:HD * hb + HD], ACT.Copy)
                act.wait_ge(kv_ready, g + 1)
                for hb in range(2):
                    ins = act.activation(tiles(TI[hb])[:, :, HD:P], tiles(pb[6 + hb][:, 0:TT * HD], HD), ACT.Copy)
                ins.then_inc(rhs_ready, 1)
                act.wait_ge(solved, g + 1)
                for hb in range(2):
                    ins = act.activation(NGH[hb], pb[hb][:, :], ACT.Copy, scale=-1.0)
                ins.then_inc(solved_copied, 1)
                act.wait_ge(group_ready, g + 1)
                for half in range(2):
                    f = FF[:, j, :].rearrange("p (t h v) -> p t h v", h=2, v=HD)[:, :, half, :]
                    ins = act.activation(f, tiles(pb[5 + 2 * half][:, 0:TT * HD], HD), ACT.Copy)
                ins.then_inc(inputs_copied, 1)

        def wkv_gpsimd(pool):
            for g in range(8):
                pool.wait_ge(triangles_ready, g + 1)
                for li, b in enumerate(BLOCK_LEVELS):
                    mask = C("mu" if g < 4 else "ml", LEVELS.index(b) * P, P)
                    for hb in range(2):
                        if li:
                            pool.wait_ge(x_ready, NLEV * g + 2 * li + hb - 1)
                        pool.tensor_tensor(tiles(MB[hb]), tiles(MT[hb]), over(mask, TT), ALU.mult)\
                            .then_inc(level_masked, 1)

        def wkv_vector(dve):
            for d in range(2):
                for j in range(4):
                    wkv_group_vector(dve, d, j, 4 * d + j)
                for s, c in enumerate(chunk_order(d)):
                    st = tiles(WORK[:, 11 + s % 2, 0:4 * HD], HD)
                    cc = slice(c * HD, (c + 1) * HD)
                    decay = along(wstat[:, :, c:c + 1].rearrange("p j o -> p (j o)"), HD)
                    if s == 0:
                        dve.wait_ge(inputs_copied, 4 * d + 4)
                        dve.tensor_tensor(st, FF[:, :, cc], decay, ALU.mult)
                    else:
                        dve.wait_ge(step_ready, (NCH - 1) * d + s)
                        for hb in range(2):
                            rows = slice(HD * hb, HD * hb + HD)
                            if s < NCH - 1:
                                dve.tensor_tensor(st[rows, :, :], FF[rows, :, cc], tiles(pb[2 + hb][rows, 0:4 * HD], HD),
                                                  ALU.add)
                            y = H[rows, 4:8, cc]
                            dve.tensor_tensor(y, y, tiles(pb[hb][rows, 0:4 * HD], HD), ALU.add)
                        if s < NCH - 1:
                            dve.drain()
                            dve.tensor_tensor(st, st, decay, ALU.mult)
                    dve.drain().then_inc(state_ready, 1)

        def wkv_group_vector(dve, d, j, g):
            strict, incl = C("su" if d == 0 else "sl"), C("iu" if d == 0 else "il")
            one, one_t = (C("ml", 0, P), C("mu", 0, P)) if d == 0 else (C("mu", 0, P), C("ml", 0, P))
            step = 1 if d == 0 else -1
            dve.wait_ge(rates_ready, g + 1)
            dve.tensor_tensor_scan(CUM[:, ::step], C("reset"), SIG[:, ::step], 0.0, ALU.mult, ALU.add)
            dve.drain()
            dve.tensor_tensor(SIG, CUM, SIG, ALU.subtract).then_inc(decay_summed, 1)
            dve.tensor_tensor(BE_, KK[:, j, :], AA, ALU.mult)
            dve.drain()
            dve.tensor_scalar(AA, AA, V("ka", j), omka[:, j:j + 1], ALU.mult, ALU.add)
            dve.drain()
            dve.tensor_tensor(AA, AA, BIG[:, K_ + j, :], ALU.mult)
            dve.drain()
            dve.wait_ge(decays_ready, g + 1)
            dve.tensor_tensor(RR[:, j, :], BIG[:, R_ + j, :], EX, ALU.mult)
            dve.tensor_copy(wstat[:, j, :], EX[:, (CHUNK - 1 if d == 0 else 0)::CHUNK])
            dve.tensor_tensor(AL_, AL_, KK[:, j, :], ALU.mult)
            dve.tensor_tensor(BE_, BE_, KA_, ALU.mult)
            dve.drain()
            dve.tensor_tensor(KA_, KA_, AA, ALU.mult).then_inc(factors_ready, 1)
            dve.wait_ge(within_ready, g + 1)
            for hb in range(2):
                dve.tensor_tensor(tiles(MT[hb]), tiles(pb[4 + hb][:, :]), over(strict, TT), ALU.mult)
                dve.tensor_tensor(tiles(TI[hb]), tiles(pb[6 + hb][:, :]), over(one, TT), ALU.mult)
            dve.drain().then_inc(triangles_ready, 1)
            for hb in range(2):
                dve.tensor_tensor(tiles(TTI[hb]), tiles(MT[hb]), over(one_t, TT), ALU.mult)
            dve.drain()
            for hb in range(2):
                for x in (TI[hb], TTI[hb]):
                    dve.tensor_tensor(tiles(x), over(C("ident"), TT), tiles(x), ALU.subtract)
            dve.drain().then_inc(t_started, 1)
            for q in range(NLEV * g, NLEV * (g + 1)):
                hb = q % 2
                dve.wait_ge(z_ready, q + 1)
                dve.tensor_tensor(TI[hb], TI[hb], pb[2 + hb][:, :], ALU.subtract)
                dve.tensor_tensor(TTI[hb], TTI[hb], pb[4 + hb][:, :], ALU.subtract).then_inc(t_updated, 1)
            dve.wait_ge(mixes_ready, g + 1)
            for hb in range(2):
                dve.tensor_tensor(tiles(MB[hb]), tiles(pb[hb][:, :]), over(strict, TT), ALU.mult)
                dve.tensor_tensor(tiles(XS[hb]), tiles(pb[2 + hb][:, :]), over(incl, TT), ALU.mult)
                ins = dve.tensor_tensor(tiles(MT[hb]), tiles(pb[4 + hb][:, :]), over(incl, TT), ALU.mult)
            ins.then_inc(mixes_masked, 1)
            dve.wait_ge(group_ready, g + 1)
            dve.tensor_tensor(RR[:, j, :], RR[:, j, :], pb[2][:, :], ALU.add)
            if d == 0:
                dve.tensor_copy(H[:, 4 + j, :], pb[3][:, :])
            else:
                dve.tensor_tensor(H[:, 4 + j, :], H[:, 4 + j, :], pb[3][:, :], ALU.add)
            for half in range(2):
                e = EIT[:, j, :].rearrange("p (t h k) -> p t h k", h=2, k=HD)[:, :, half, :]
                dve.tensor_tensor(e, tiles(pb[4 + 2 * half][:, 0:TT * HD], HD), over(C("ident64"), TT), ALU.add)

        y_summed, y_centred, y_squared = sem("output_summed"), sem("output_centred"), sem("output_squared")
        var_summed, y_rooted = sem("output_squares_summed"), sem("output_deviation_ready")
        bonus_summed, out_gate_ready = sem("bonus_summed"), sem("output_gate_ready")

        def wkv_readout_tensor(pe):
            pe.wait_ge(state_ready, 2 * NCH)
            for j in range(4):
                pe.matmul(pb[j][:, :], C("blk"), H[:, 4 + j, :], start=True, stop=True).then_inc(y_summed, 1)
            for j in range(4):
                mm = pe.matmul(pb[4 + j][:, :], S("g2", 0, P, j * P, P), BIG[:, GL, :], start=True, stop=True)
            mm.then_inc(out_gate_ready, 1)
            for j in range(4):
                pe.wait_ge(y_squared, j + 1)
                pe.matmul(pb[j][:, :], C("blk"), WORK[:, j, :], start=True, stop=True).then_inc(var_summed, 1)
            for j in range(4):
                pe.wait_ge(y_rooted, j + 1)
                pe.matmul(pb[j][:, :], C("blk"), WORK[:, 4 + j, :], start=True, stop=True).then_inc(bonus_summed, 1)

        def wkv_readout_scalar(act):
            for j in range(4):
                act.wait_ge(y_centred, j + 1)
                act.activation(WORK[:, j, :], H[:, 4 + j, :], ACT.Square).then_inc(y_squared, 1)
            for j in range(4):
                act.wait_ge(var_summed, j + 1)
                act.activation(WORK[:, j, :], pb[j][:, :], ACT.Sqrt, bias=epsb[:, 2:3], scale=1.0 / HD)\
                   .then_inc(y_rooted, 1)

        def wkv_readout_vector(dve):
            for j in range(4):
                dve.scalar_tensor_tensor(out=WORK[:, 4 + j, :], in0=BIG[:, R_ + j, :], scalar=V("rk", j),
                                         in1=BIG[:, K_ + j, :], op0=ALU.mult, op1=ALU.mult)
                dve.wait_ge(y_summed, j + 1)
                dve.scalar_tensor_tensor(out=H[:, 4 + j, :], in0=pb[j][:, :], scalar=-1.0 / HD, in1=H[:, 4 + j, :],
                                         op0=ALU.mult, op1=ALU.add).then_inc(y_centred, 1)
            for j in range(4):
                dve.wait_ge(y_rooted, j + 1)
                dve.reciprocal(WORK[:, j, :], WORK[:, j, :])
            dve.drain()
            for j in range(4):
                dve.scalar_tensor_tensor(out=H[:, 4 + j, :], in0=H[:, 4 + j, :], scalar=V("gnw", j), in1=WORK[:, j, :],
                                         op0=ALU.mult, op1=ALU.mult)
            dve.drain()
            for j in range(4):
                dve.wait_ge(bonus_summed, j + 1)
                dve.tensor_tensor(WORK[:, j, :], BIG[:, V_ + j, :], pb[j][:, :], ALU.mult)
            dve.drain()
            for j in range(4):
                dve.scalar_tensor_tensor(out=H[:, 4 + j, :], in0=H[:, 4 + j, :], scalar=V("gnb", j), in1=WORK[:, j, :],
                                         op0=ALU.add, op1=ALU.add)
            dve.drain()
            dve.wait_ge(out_gate_ready, 1)
            for j in range(4):
                dve.tensor_tensor(H[:, 4 + j, :], H[:, 4 + j, :], pb[4 + j][:, :], ALU.mult)
            dve.drain().then_inc(mixer_ready, 1)

        MVTOK = WORK[:, 0:4, :]
        ROWS = 64
        IGR, LFR, BCR, MMR, AR, RBR = (WORK[0:ROWS, 4 + i, :] for i in range(6))
        ACOL = WORK[:, 10, 0:TT * ROWS].rearrange("p (t r) -> p t r", r=ROWS)
        TMP1, LOGS, RD = WORK[0:ROWS, 11, :], WORK[0:ROWS, 12, :], WORK[:, 13, :]
        WGT = [WORK[:, 14:18, :], WORK[:, 22:26, :]]
        DEN, EM = [WORK[:, 18, :], WORK[:, 19, :]], [WORK[:, 26, :], WORK[:, 27, :]]
        SELROW = WORK[0:ROWS, 20:22, :].rearrange("p a (b c) -> p (a b) c", c=P)
        conv_ready, conv_silu = sem("convolution_ready"), sem("convolution_silu")
        mv_turned, mv_ready = sem("mlstm_values_transposed"), sem("mlstm_values_by_token_ready")
        gates_summed, gates_biased, gates_logged = sem("mlstm_gates_gathered"), sem("mlstm_gates_biased"), sem("mlstm_gates_logged")
        stabilised = sem("mlstm_stabiliser_ready")
        acol_turned, acol_ready = sem("mlstm_key_terms_transposed"), sem("mlstm_key_terms_ready")
        rows_spread, qk_ready = sem("mlstm_query_terms_spread"), sem("mlstm_scores_ready")
        rd_ready, exps_ready = sem("mlstm_diagonal_masked"), sem("mlstm_weights_exponential")
        weights_ready, sums_ready = sem("mlstm_weights_ready"), sem("mlstm_sums_ready")
        den_ready, unit_done = sem("mlstm_denominator_ready"), sem("mlstm_unit_done")

        def place_of(d, tile):
            return tile if d == 0 else (1, 0, 3, 2)[tile]

        def later_runs(d, si):
            later = [t for t in range(TT) if place_of(d, t) > place_of(d, si)]
            runs = []
            for t in later:
                if runs and runs[-1][1] == t:
                    runs[-1][1] = t + 1
                else:
                    runs.append([t, t + 1])
            return runs

        UNITS = [(d, h) for h in range(4) for d in range(2)]

        def mlstm_vector(dve):
            all_copied(dve, 2, 0)
            for i in range(8):
                dve.tensor_scalar(WORK[:, 20 + i, :], BIG[:, 5 + i, :], V("cw", 8 + i), V("cb", i), ALU.mult, ALU.add)
            dve.drain()
            add_neighbours(dve, [(BIG[:, 5 + i, :], WORK[:, 20 + i, :], V("cw", i), V("cw", 16 + i)) for i in range(8)])
            dve.drain().then_inc(conv_ready, 1)
            dve.wait_ge(gates_biased, 1)
            dve.tensor_scalar(LFR, pb[5][0:ROWS, :], vec[0:ROWS, VO["bf"][0]:VO["bf"][0] + 1], 0.0, ALU.add, ALU.min)
            dve.wait_ge(gates_logged, 1)
            dve.drain()
            dve.tensor_tensor(LFR, LFR, LOGS, ALU.subtract)
            dve.memset(RD[0:ROWS, :], 1.0)
            dve.drain()
            ones = RD[0:32, :]
            lf, ig, bc, mm = (x[0:32, :] for x in (LFR, IGR, BCR, MMR))
            dve.tensor_tensor_scan(bc, ones, lf, 0.0, ALU.mult, ALU.add)
            dve.tensor_tensor_scan(mm, lf, ig, 0.0, ALU.add, ALU.max)
            ones = RD[32:64, 0:TC]
            c, l = ([x[32:64, a:b] for x in (LFR, IGR, BCR, MMR)] for a, b in (CTX, LAT))
            dve.tensor_tensor_scan(c[2][:, ::-1], ones, c[0][:, ::-1], 0.0, ALU.mult, ALU.add)
            dve.tensor_tensor_scan(c[3][:, ::-1], c[0][:, ::-1], c[1][:, ::-1], 0.0, ALU.add, ALU.max)
            dve.drain()
            dve.tensor_tensor_scan(l[2][:, ::-1], ones, l[0][:, ::-1], c[2][:, 0:1], ALU.mult, ALU.add)
            dve.tensor_tensor_scan(l[3][:, ::-1], l[0][:, ::-1], l[1][:, ::-1], c[3][:, 0:1], ALU.add, ALU.max)
            dve.drain()
            dve.tensor_tensor(AR, IGR, BCR, ALU.subtract)
            dve.tensor_tensor(RBR, BCR, MMR, ALU.subtract)
            dve.wait_ge(conv_silu, 8)
            for d in range(2):
                dve.tensor_copy(SELROW[:, 4 * d:4 * d + 4, :], along(C("ident", 32 * d, 4)[0:ROWS, :], P))
            dve.drain().then_inc(stabilised, 1)
            for u in range(len(UNITS) + 1):
                if u < len(UNITS):
                    d, h = UNITS[u]
                    dve.wait_ge(rows_spread, u + 1)
                    dve.tensor_tensor(tiles(RD), tiles(pb[0][:, :]), over(C("nu" if d == 0 else "nl"), TT), ALU.add)\
                       .then_inc(rd_ready, 1)
                    dve.wait_ge(exps_ready, u + 1)
                    dve.wait_ge(qk_ready, u + 1)
                    for si in range(TT):
                        for a, b in [[si, si + 1]] + later_runs(d, si):
                            w = WGT[u % 2][:, si, a * P:b * P]
                            ins = dve.scalar_tensor_tensor(out=w, in0=pb[2 + si][:, a * P:b * P], scalar=P ** -0.5, in1=w,
                                                           op0=ALU.mult, op1=ALU.mult)
                    ins.then_inc(weights_ready, 1)
                if u:
                    d, h = UNITS[u - 1]
                    den = DEN[(u - 1) % 2]
                    dve.wait_ge(den_ready, u)
                    dve.tensor_tensor(den, den, EM[(u - 1) % 2], ALU.max)
                    dve.drain()
                    dve.reciprocal(den, den)
                    dve.drain()
                    if d == 0:
                        dve.tensor_tensor(H[:, 4 + h, :], den, pb[6][:, :], ALU.mult).then_inc(unit_done, 1)
                    else:
                        dve.tensor_tensor(den, den, pb[6][:, :], ALU.mult)
                        dve.drain()
                        dve.tensor_tensor(H[:, 4 + h, :], H[:, 4 + h, :], den, ALU.add).then_inc(unit_done, 1)

        def mlstm_scalar(act):
            act.wait_ge(conv_ready, 1)
            for i in range(8):
                act.activation(BIG[:, 5 + i, :], WORK[:, 20 + i, :], ACT.Silu).then_inc(conv_silu, 1)
            act.wait_ge(gates_summed, 1)
            act.activation(IGR, pb[4][0:ROWS, :], ACT.Identity, bias=vec[0:ROWS, VO["bi"][0]:VO["bi"][0] + 1])
            act.activation(TMP1, pb[5][0:ROWS, :], ACT.Abs, bias=vec[0:ROWS, VO["bf"][0]:VO["bf"][0] + 1])\
               .then_inc(gates_biased, 1)
            act.drain()
            act.activation(TMP1, TMP1, ACT.Exp, scale=-1.0)
            act.drain()
            act.activation(LOGS, TMP1, ACT.Ln, bias=1.0).then_inc(gates_logged, 1)
            act.wait_ge(mv_turned, 1)
            for tt in range(TT):
                ins = act.activation(MVTOK[:, tt, :], pb[tt][:, :], ACT.Copy)
            ins.then_inc(mv_ready, 1)
            act.wait_ge(acol_turned, 1)
            act.activation(ACOL, tiles(pb[0][:, 0:TT * ROWS], ROWS), ACT.Copy).then_inc(acol_ready, 1)
            act.drain()
            for u in range(len(UNITS) + 1):
                if u < len(UNITS):
                    d, h = UNITS[u]
                    row = 32 * d + h
                    act.wait_ge(rows_spread, u + 1)
                    if u >= 2:
                        act.wait_ge(unit_done, u - 1)
                    act.activation(EM[u % 2], pb[1][:, :], ACT.Exp, scale=-1.0)
                    act.wait_ge(rd_ready, u + 1)
                    for si in range(TT):
                        s = slice(si * P, (si + 1) * P)
                        ins = act.activation(WGT[u % 2][:, si, s], RD[:, s], ACT.Exp, bias=ACOL[:, si, row:row + 1])
                        for a, b in later_runs(d, si):
                            ins = act.activation(WGT[u % 2][:, si, a * P:b * P], pb[0][:, a * P:b * P], ACT.Exp,
                                                 bias=ACOL[:, si, row:row + 1])
                    ins.then_inc(exps_ready, 1)
                if u:
                    act.wait_ge(sums_ready, u)
                    act.activation(DEN[(u - 1) % 2], pb[7][:, :], ACT.Abs).then_inc(den_ready, 1)

        def mlstm_tensor(pe):
            pe.wait_ge(conv_ready, 1)
            pe.matmul(pb[4][0:ROWS, :], C("sel_i"), BIG[:, 29, :], start=True, stop=True)
            pe.matmul(pb[5][0:ROWS, :], C("sel_f"), BIG[:, 29, :], start=True, stop=True).then_inc(gates_summed, 1)
            turn_values(pe, BIG[:, 13:17, :], 4, 0).then_inc(mv_turned, 1)
            pe.wait_ge(mv_ready, 1)
            pe.wait_ge(stabilised, 1)
            for tt in range(TT):
                mm = pe.transpose(pb[0][:, tt * ROWS:(tt + 1) * ROWS], AR[:, tt * P:(tt + 1) * P],
                                  C("ident")[0:ROWS, 0:ROWS])
            mm.then_inc(acol_turned, 1)
            pe.wait_ge(acol_ready, 1)
            pe.wait_ge(conv_silu, 8)
            for u in range(len(UNITS) + 1):
                if u < len(UNITS):
                    d, h = UNITS[u]
                    if u:
                        pe.wait_ge(weights_ready, u)
                    sel = SELROW[:, 4 * d + h, :]
                    pe.matmul(pb[0][:, :], sel, RBR, start=True, stop=True)
                    pe.matmul(pb[1][:, :], sel, MMR, start=True, stop=True).then_inc(rows_spread, 1)
                    for si in range(TT):
                        for a, b in [[si, si + 1]] + later_runs(d, si):
                            mm = pe.matmul(pb[2 + si][:, a * P:b * P], BIG[:, 9 + h, si * P:(si + 1) * P],
                                           BIG[:, 5 + h, a * P:b * P], start=True, stop=True)
                    mm.then_inc(qk_ready, 1)
                if u:
                    d, h = UNITS[u - 1]
                    pe.wait_ge(weights_ready, u)
                    if u >= 2:
                        pe.wait_ge(unit_done, u - 1)
                    for t in range(TT):
                        earlier = [s for s in range(TT) if place_of(d, s) <= place_of(d, t)]
                        for bank in (6, 7):
                            for s in earlier:
                                mm = pe.matmul(pb[bank][:, t * P:(t + 1) * P],
                                               MVTOK[:, s, h * P:(h + 1) * P] if bank == 6 else C("ones"),
                                               WGT[(u - 1) % 2][:, s, t * P:(t + 1) * P], start=s == earlier[0],
                                               stop=s == earlier[-1])
                    mm.then_inc(sums_ready, 1)

        READOUTS = [(4, 17, 21, ALL, "mn"), (0, None, 20, LAT, "gln")]
        gates_ready, out_gated = sem("readout_gates_ready"), sem("readout_heads_gated")
        out_squared, out_summed, out_rooted = (sem(f"readout_{x}") for x in ("squared", "summed", "rms_ready"))

        def readout_scalar(act, k):
            h0, o0, z0, (a, b), _ = READOUTS[k]
            if o0 is not None:
                for h in range(4):
                    act.activation(BIG[:, o0 + h, a:b], BIG[:, o0 + h, a:b], ACT.Sigmoid)
            for i in range(KT):
                ins = act.activation(BIG[:, z0 + i, a:b], BIG[:, z0 + i, a:b], ACT.Silu)
            ins.then_inc(gates_ready, 1)
            act.wait_ge(out_gated, k + 1)
            for h in range(4):
                act.activation(WORK[:, h, a:b], H[:, h0 + h, a:b], ACT.Square).then_inc(out_squared, 1)
            for h in range(4):
                act.wait_ge(out_summed, 4 * k + h + 1)
                act.activation(WORK[:, h, a:b], pb[h][:, a:b], ACT.Sqrt, bias=epsb[:, 0:1], scale=1.0 / P)\
                   .then_inc(out_rooted, 1)

        def readout_tensor(pe, k):
            a, b = READOUTS[k][3]
            for h in range(4):
                pe.wait_ge(out_squared, 4 * k + h + 1)
                pe.matmul(pb[h][:, a:b], C("ones"), WORK[:, h, a:b], start=True, stop=True).then_inc(out_summed, 1)

        def readout_vector(dve, k):
            h0, o0, z0, (a, b), gain = READOUTS[k]
            dve.wait_ge(gates_ready, k + 1)
            dve.drain()
            if o0 is not None:
                for h in range(4):
                    dve.tensor_tensor(H[:, h0 + h, a:b], H[:, h0 + h, a:b], BIG[:, o0 + h, a:b], ALU.mult)
            dve.drain().then_inc(out_gated, 1)
            for h in range(4):
                dve.wait_ge(out_rooted, 4 * k + h + 1)
                dve.reciprocal(WORK[:, h, a:b], WORK[:, h, a:b])
            dve.drain()
            for h in range(4):
                dve.scalar_tensor_tensor(out=H[:, h0 + h, a:b], in0=H[:, h0 + h, a:b], scalar=V(gain, h),
                                         in1=WORK[:, h, a:b], op0=ALU.mult, op1=ALU.mult)
            dve.drain()
            for i in range(KT):
                dve.tensor_tensor(H[:, i, a:b], H[:, i, a:b], BIG[:, z0 + i, a:b], ALU.mult)
            dve.drain().then_inc(mixer_ready, 1)

        GVTOK = WORK[:, 0:4, :]
        LGT, BSUM, TMP2, ONES_ROW = WORK[:, 4, :], WORK[:, 5, :], WORK[:, 6, :], WORK[:, 7, :]
        QC = WORK[:, 8, :]
        QL = WORK[:, 9:13, :].rearrange("p a (b t) -> p (a b) t", t=TC)
        PART = WORK[:, 13:17, :]
        NEAR, FAR, CTXA = WORK[:, 17, 0:TC], WORK[:, 17, TC:TC + P], WORK[:, 18, :]
        GLA_LEVELS = LEVELS + (P,)
        gv_turned, gv_ready = sem("gla_values_transposed"), sem("gla_values_by_token_ready")
        forget_ready, forget_logged = sem("gla_gate_product"), sem("gla_gate_logged")
        spans_ready, spans_exp, spans_used = sem("gla_log_decays_ready"), sem("gla_decays_ready"), sem("gla_factors_ready")
        pairs_ready, near_ready, far_ready = sem("gla_scores_ready"), sem("gla_near_scores_masked"), sem("gla_far_scores_copied")
        gla_mixed, gla_added = sem("gla_values_mixed"), sem("gla_output_added")

        def halves(ap, b):
            return ap.rearrange("p (n h b) -> p n h b", h=2, b=b)

        def gla_tensor(pe):
            pe.wait_ge(mixed_copied, units_before(4))
            turn_values(pe, BIG[:, 4:8, :], 4, 0).then_inc(gv_turned, 1)
            pe.wait_ge(gv_ready, 1)
            for g in range(4):
                d, j = g // 2, g % 2
                early, late = (2, 3) if d == 0 else (3, 2)
                low = slice(32 * d, 32 * d + 16)
                pe.matmul(pb[7][:, :], S("wg", 32 * d, 32 * d + 16, j * P, P), BIG[low, 28, :], start=True, stop=True)\
                  .then_inc(forget_ready, 1)
                pe.wait_ge(spans_used, g + 1)
                for hb in range(2):
                    u, h, rows = 2 * g + hb, 2 * j + hb, slice(HD * hb, HD * hb + HD)
                    for li in range(len(LEVELS)):
                        for i in range(2):
                            x = QL[rows, li, i * P:(i + 1) * P]
                            o = (li % 2) * TC + i * P
                            pe.matmul(pb[li // 2][:, o:o + P], x, x, start=True, stop=True)
                    for i in range(2):
                        s = slice(TC + i * P, TC + (i + 1) * P)
                        pe.matmul(pb[3][:, s], BIG[rows, 2 + j, s], BIG[rows, j, s], start=True, stop=True)
                    e, l = (slice((x - 2) * P, (x - 1) * P) for x in (early, late))
                    pe.matmul(pb[4][:, 0:P], QL[rows, 7, e], QL[rows, 7, l], start=True, stop=True)
                    for s in range(2):
                        mm = pe.matmul(pb[5][:, s * TC:(s + 1) * TC], QC[rows, s * P:(s + 1) * P], QC[rows, TC:T],
                                       start=True, stop=True)
                    mm.then_inc(pairs_ready, 1)
                    pe.wait_ge(near_ready, u + 1)
                    pe.wait_ge(far_ready, u + 1)
                    if u:
                        pe.wait_ge(gla_added, u)
                    hc = slice(h * P, (h + 1) * P)
                    for t in (2, 3):
                        terms = [(2 + (t - 2), NEAR[:, (t - 2) * P:(t - 1) * P])]
                        terms += [(early, FAR)] if t == late else []
                        terms += [(s, CTXA[:, s * TC + (t - 2) * P:s * TC + (t - 1) * P]) for s in range(2)]
                        for i, (s, a) in enumerate(terms):
                            mm = pe.matmul(pb[6][:, (t - 2) * P:(t - 1) * P], GVTOK[:, s, hc], a, start=i == 0,
                                           stop=i == len(terms) - 1)
                    mm.then_inc(gla_mixed, 1)

        def gla_scalar(act):
            act.wait_ge(gv_turned, 1)
            for tt in range(TT):
                ins = act.activation(GVTOK[:, tt, :], pb[tt][:, :], ACT.Copy)
            ins.then_inc(gv_ready, 1)
            for g in range(4):
                act.wait_ge(forget_ready, g + 1)
                act.activation(TMP2, pb[7][:, :], ACT.Abs, bias=V("bg", g))
                act.drain()
                act.activation(TMP2, TMP2, ACT.Exp, scale=-1.0)
                act.drain()
                act.activation(TMP2, TMP2, ACT.Ln, bias=1.0).then_inc(forget_logged, 1)
                act.wait_ge(spans_ready, g + 1)
                act.activation(QC, QC, ACT.Exp, scale=1.0 / 16)
                act.activation(QL, QL, ACT.Exp, scale=1.0 / 16).then_inc(spans_exp, 1)
                for u in (2 * g, 2 * g + 1):
                    act.wait_ge(pairs_ready, u + 1)
                    act.activation(CTXA, pb[5][:, :], ACT.Copy)
                    act.activation(FAR, pb[4][:, 0:P], ACT.Copy).then_inc(far_ready, 1)

        def gla_vector(dve):
            dve.memset(ONES_ROW, 1.0)
            for g in range(4):
                d, j = g // 2, g % 2
                hk, hq = (0, 1) if d == 0 else (1, 0)
                mask = lambda li: C("mu" if d == 0 else "ml", li * P, P)
                dve.wait_ge(forget_logged, g + 1)
                dve.tensor_scalar(LGT, pb[7][:, :], V("bg", g), 0.0, ALU.add, ALU.min)
                dve.drain()
                dve.tensor_tensor(LGT, LGT, TMP2, ALU.subtract)
                dve.drain()
                if d == 0:
                    dve.tensor_tensor_scan(BSUM, ONES_ROW, LGT, 0.0, ALU.mult, ALU.add)
                else:
                    dve.tensor_tensor_scan(BSUM[:, 0:TC][:, ::-1], ONES_ROW[:, 0:TC], LGT[:, 0:TC][:, ::-1], 0.0,
                                           ALU.mult, ALU.add)
                    dve.drain()
                    dve.tensor_tensor_scan(BSUM[:, TC:T][:, ::-1], ONES_ROW[:, 0:TC], LGT[:, TC:T][:, ::-1],
                                           BSUM[:, 0:1], ALU.mult, ALU.add)
                dve.drain()
                ref = BSUM[:, TC - 1:TC] if d == 0 else BSUM[:, 0:1]
                dve.tensor_scalar(QC[:, 0:TC], BSUM[:, 0:TC], -1.0, ref, ALU.mult, ALU.add)
                dve.tensor_scalar(QC[:, TC:T], BSUM[:, TC:T], ref, None, ALU.subtract)
                for li, b in enumerate(GLA_LEVELS):
                    src, dst = halves(BSUM[:, TC:T], b), halves(QL[:, li, :], b)
                    r = b - 1 if d == 0 else 0
                    refs = src[:, :, hk, r:r + 1].to_broadcast([P, TC // (2 * b), b])
                    dve.tensor_tensor(dst[:, :, hq, :], src[:, :, hq, :], refs, ALU.subtract)
                    dve.tensor_tensor(dst[:, :, hk, :], refs, src[:, :, hk, :], ALU.subtract)
                dve.drain().then_inc(spans_ready, 1)
                dve.wait_ge(spans_exp, g + 1)
                dve.tensor_tensor(QC[:, 0:TC], QC[:, 0:TC], BIG[:, 2 + j, 0:TC], ALU.mult)
                dve.tensor_tensor(QC[:, TC:T], QC[:, TC:T], BIG[:, j, TC:T], ALU.mult)
                for li, b in enumerate(GLA_LEVELS):
                    dst = halves(QL[:, li, :], b)
                    for half, src in ((hq, BIG[:, j, TC:T]), (hk, BIG[:, 2 + j, TC:T])):
                        dve.tensor_tensor(dst[:, :, half, :], dst[:, :, half, :], halves(src, b)[:, :, half, :], ALU.mult)
                dve.drain().then_inc(spans_used, 1)
                for hb in range(2):
                    u, h = 2 * g + hb, 2 * j + hb
                    dve.wait_ge(pairs_ready, u + 1)
                    for li in range(len(LEVELS) + 1):
                        m = mask(li) if li < len(LEVELS) else C("ident")
                        o = (li % 2) * TC
                        dve.tensor_tensor(tiles(PART[:, li // 2, o:o + TC]), tiles(pb[li // 2][:, o:o + TC]), over(m, 2),
                                          ALU.mult)
                    dve.drain()
                    dve.tensor_tensor(PART[:, 0, :], PART[:, 0, :], PART[:, 1, :], ALU.add)
                    dve.tensor_tensor(PART[:, 2, :], PART[:, 2, :], PART[:, 3, :], ALU.add)
                    dve.drain()
                    dve.tensor_tensor(PART[:, 0, :], PART[:, 0, :], PART[:, 2, :], ALU.add)
                    dve.drain()
                    dve.tensor_tensor(NEAR, PART[:, 0, 0:TC], PART[:, 0, TC:T], ALU.add).then_inc(near_ready, 1)
                    dve.wait_ge(gla_mixed, u + 1)
                    if d == 0:
                        dve.tensor_copy(H[:, h, TC:T], pb[6][:, 0:TC]).then_inc(gla_added, 1)
                    else:
                        dve.tensor_tensor(H[:, h, TC:T], H[:, h, TC:T], pb[6][:, 0:TC], ALU.add).then_inc(gla_added, 1)

        block = ctx.enter_context(nc.Block())

        @block.tensor
        def _(pe):
            pe.wait_ge(loaded, 16 * 4)
            mod_tensor(pe, 0)
            norm_tensor(pe, 0)
            ffn_tensor(pe, 0)
            norm_tensor(pe, 1)
            linear_tensor(pe, 0)
            even_heads_tensor(pe)
            attend_tensor(pe, 0)
            wkv_features_tensor(pe)
            wkv_tensor(pe)
            wkv_readout_tensor(pe)
            residual_tensor(pe, 0)
            norm_tensor(pe, 2)
            ffn_tensor(pe, 1)
            mod_tensor(pe, 1)
            norm_tensor(pe, 3)
            ffn_tensor(pe, 2)
            norm_tensor(pe, 4)
            linear_tensor(pe, 1)
            odd_heads_tensor(pe)
            attend_tensor(pe, 1)
            residual_tensor(pe, 1)
            norm_tensor(pe, 5)
            ffn_tensor(pe, 3)
            gain_norm_tensor(pe, 0)
            mod_tensor(pe, 2)
            norm_tensor(pe, 6)
            linear_tensor(pe, 2)
            mla_heads_tensor(pe)
            attend_tensor(pe, 2)
            mlstm_tensor(pe)
            readout_tensor(pe, 0)
            residual_tensor(pe, 2)
            mod_tensor(pe, 3)
            norm_tensor(pe, 7)
            linear_tensor(pe, 3)
            na_heads_tensor(pe)
            attend_tensor(pe, 3)
            gla_tensor(pe)
            readout_tensor(pe, 1)
            residual_tensor(pe, 3)
            gain_norm_tensor(pe, 1)

        @block.vector
        def _(dve):
            setup_vector(dve)
            mod_vector(dve, 0)
            norm_vector(dve, 0)
            ffn_vector(dve, 0)
            norm_vector(dve, 1)
            linear_vector(dve, 0)
            even_heads_vector(dve)
            attend_vector(dve, 0)
            wkv_features_vector(dve)
            wkv_vector(dve)
            wkv_readout_vector(dve)
            residual_vector(dve, 0)
            norm_vector(dve, 2)
            ffn_vector(dve, 1)
            mod_vector(dve, 1)
            norm_vector(dve, 3)
            ffn_vector(dve, 2)
            norm_vector(dve, 4)
            linear_vector(dve, 1)
            odd_heads_vector(dve)
            attend_vector(dve, 1)
            residual_vector(dve, 1)
            norm_vector(dve, 5)
            ffn_vector(dve, 3)
            gain_norm_vector(dve, 0)
            mod_vector(dve, 2)
            norm_vector(dve, 6)
            linear_vector(dve, 2)
            mla_heads_vector(dve)
            attend_vector(dve, 2)
            mlstm_vector(dve)
            readout_vector(dve, 0)
            residual_vector(dve, 2)
            mod_vector(dve, 3)
            norm_vector(dve, 7)
            linear_vector(dve, 3)
            attend_vector(dve, 3)
            gla_vector(dve)
            readout_vector(dve, 1)
            residual_vector(dve, 3)
            gain_norm_vector(dve, 1)

        @block.scalar
        def _(act):
            setup_scalar(act)
            mod_scalar(act, 0)
            norm_scalar(act, 0)
            ffn_scalar(act, 0)
            norm_scalar(act, 1, ffn_added, 4 + 1)
            linear_scalar(act, 0)
            even_heads_scalar(act)
            attend_scalar(act, 0)
            wkv_features_scalar(act)
            wkv_scalar(act)
            wkv_readout_scalar(act)
            norm_scalar(act, 2, mixer_added, 4 + 1)
            ffn_scalar(act, 1)
            mod_scalar(act, 1)
            norm_scalar(act, 3, ffn_added, 4 + KT + 1)
            ffn_scalar(act, 2)
            norm_scalar(act, 4, ffn_added, 4 + 2 * KT + 1)
            linear_scalar(act, 1)
            odd_heads_scalar(act)
            attend_scalar(act, 1)
            norm_scalar(act, 5, mixer_added, 4 + KT + 1)
            ffn_scalar(act, 3)
            gain_norm_scalar(act, 0, ffn_added, 4 + 3 * KT + 1)
            mod_scalar(act, 2)
            act.wait_ge(ctx2_loaded, 16)
            norm_scalar(act, 6, scaled, GAIN_NORMS[0][2] * KT + 1)
            linear_scalar(act, 2)
            mla_heads_scalar(act)
            attend_scalar(act, 2)
            mlstm_scalar(act)
            readout_scalar(act, 0)
            mod_scalar(act, 3)
            norm_scalar(act, 7, mixer_added, 4 + 2 * KT + 1)
            linear_scalar(act, 3)
            na_heads_scalar(act)
            attend_scalar(act, 3)
            gla_scalar(act)
            readout_scalar(act, 1)
            gain_norm_scalar(act, 1, mixer_added, 4 + 3 * KT + 1)

        @block.gpsimd
        def _(pool):
            wkv_gpsimd(pool)
            pool.wait_ge(scaled, 5 * KT)
            pool.dma_start(X[:, :, 0:TC], ctx2).then_inc(ctx2_loaded, 16)
            na_heads_gpsimd(pool)

        @block.sync
        def _(sp):
            sp.dma_start(vec[:, :], vecs).then_inc(loaded, 16)
            sp.dma_start(X[:, :, :], xin).then_inc(loaded, 16)
            sp.dma_start(cst[:, :], consts).then_inc(loaded, 16)
            sp.dma_start(smallw[:, :], small).then_inc(loaded, 16)

            def load(words, n, row, i=None):
                if n >= RING or i is not None:
                    free = max(n - RING + 1, 0)
                    sp.wait_ge(slab_done, free if i is None else i * RING + free)
                src = stream_k if words == D else stream_f
                src = src[row] if i is None else src[bass.ds(i * RING + row, 1), :, :].rearrange("o p c -> (o p) c")
                sp.dma_start(ring[:, n % RING, 0:words], src).then_inc(slot_full[n % RING], 16)

            runs = []
            for _, words, count in SLABS:
                if runs and runs[-1][0] == words:
                    runs[-1][1] += count
                else:
                    runs.append([words, count])
            n, rows = 0, {D: 0, SLOT: 0}
            for words, count in runs:
                row, done = rows[words], 0
                while done < count and n + done < RING:
                    load(words, n + done, row + done)
                    done += 1
                turns = (count - done) // RING
                if turns:
                    with sp.Fori(0, turns) as i:
                        for k in range(RING):
                            load(words, n + done + k, row + done + k, i)
                    done += turns * RING
                for k in range(done, count):
                    load(words, n + k, row + k)
                n += count
                rows[words] += count
            sp.wait_ge(scaled, 10 * KT)
            sp.dma_start(out, X[:, :, TC:T]).then_inc(stored, 16)
            sp.wait_ge(stored, 16)


def shape_constants():
    p, f = np.arange(P)[:, None], np.arange(P)[None, :]
    c = {"ident": p == f, "ones": np.ones((P, P)), "blk": p // HD == f // HD, "ident64": p % 64 == np.arange(64)[None, :]}
    rot = np.zeros((P, P))
    for i in range(0, P, 2):
        rot[i + 1, i], rot[i, i + 1] = -1, 1
    rotm = np.zeros((P, P))
    for base in (0, 16, 64, 80):
        for i in range(base, base + 8):
            rotm[i + 8, i], rotm[i, i + 8] = -1, 1
    c |= {"rot": rot, "rotm": rotm}
    sel_i, sel_f = np.zeros((P, 64)), np.zeros((P, 64))
    for d in range(2):
        for h in range(4):
            sel_i[32 + 8 * d + h, 32 * d + h] = 1
            sel_f[32 + 8 * d + 4 + h, 32 * d + h] = 1
    c |= {"sel_i": sel_i, "sel_f": sel_f}
    up = [(p // (2 * b) == f // (2 * b)) & (p % (2 * b) < b) & (f % (2 * b) >= b) for b in LEVELS]
    chunk = p // CHUNK == f // CHUNK
    c |= {"mu": np.concatenate(up, 1), "ml": np.concatenate([u.T for u in up], 1), "su": chunk & (p < f),
          "sl": chunk & (p > f), "iu": chunk & (p <= f), "il": chunk & (p >= f),
          "nu": np.where(p <= f, 0, NEG), "nl": np.where(p >= f, 0, NEG)}
    t = np.arange(TC)
    row, col = (t // GRID_W).astype(np.float32), (t % GRID_W).astype(np.float32)
    inv = np.float32(10000.0) ** (-np.arange(16, dtype=np.float32) / np.float32(16))
    ang = np.concatenate([row[:, None] * inv, col[:, None] * inv], 1).T
    pair = np.arange(P) % HD // 2
    c |= {"cosa": np.cos(ang)[pair], "sina": np.sin(ang)[pair]}
    inv = np.float32(1.0) / np.float32(10000.0) ** (np.arange(8, dtype=np.float32) / np.float32(8))
    ang = np.concatenate([row[:, None] * inv, col[:, None] * inv], 1).T
    r32 = np.arange(32)
    ang = ang[r32 // 16 * 8 + r32 % 8]
    for name, bases in (("me", (64,)), ("mo", (0,)), ("mk", (0, 64))):
        cos, sin = np.ones((P, TC), np.float32), np.zeros((P, TC), np.float32)
        for b in bases:
            cos[b:b + 32], sin[b:b + 32] = np.cos(ang), np.sin(ang)
        c["cos" + name], c["sin" + name] = cos, sin
    q, k = np.arange(TC)[:, None], np.arange(TC)[None, :]
    halves = lambda m: m.reshape(2, P, TC).transpose(1, 0, 2).reshape(P, 2 * TC)
    c["wmask"] = halves(np.where((np.abs(k - q) <= 128) & (k >= 128), 0, NEG))
    c["padkeys"] = p + 1
    start = np.clip(q % GRID_W - 8, 0, GRID_W - 16)
    inside = (k % GRID_W >= start) & (k % GRID_W < start + 16)
    c["namask"] = halves(np.where(inside, 0, NEG))
    c["reset"] = np.broadcast_to(np.arange(T)[None, :] % CHUNK != 0, (P, T))
    out = np.concatenate([np.asarray(c[n], np.float32) for n, _ in CONSTS], 1)
    assert out.shape == (P, offsets(CONSTS)[1])
    return np.ascontiguousarray(out)


def lay_out(a):
    heads = lambda order: np.concatenate([np.arange(h * HD, h * HD + HD) for h in order])
    even = heads([h for t in range(4) for h in (t, 4 + t)])
    odd = heads([h for q in range(2) for j in range(4) for h in (8 * q + j, 8 * q + 4 + j)])
    slabs_k, slabs_f = [], []

    def square(w):
        n = w.shape[1] // P
        slabs_k.append(w.reshape(KT, P, n, P).transpose(2, 1, 0, 3).reshape(n, P, D))

    def ffn(w_in, w_out):
        both = w_in.reshape(D, 2, FT, P).transpose(0, 2, 1, 3).reshape(D, 2 * DFF)
        square(both)
        w = w_out.reshape(2, HALF_FT, P, KT, P).transpose(3, 0, 2, 1, 4)
        slabs_f.append(w.reshape(2 * KT, P, SLOT))

    def padded(w, cols):
        out = np.zeros((w.shape[0], len(cols)), np.float32)
        keep = np.flatnonzero(cols >= 0)
        out[:, keep] = w[:, cols[keep]]
        return out

    square(a["w_mod"][0])
    ffn(a["ffn_in"][0, 0], a["ffn_out"][0, 0])
    w = a["even_w_in"][0]
    square(np.concatenate([w[:, even], w[:, 512:]], 1))
    w = a["even_w_out"][0]
    square(np.concatenate([w[even], w[512:]], 0))
    ffn(a["ffn_in"][0, 1], a["ffn_out"][0, 1])
    square(a["w_mod"][1])
    ffn(a["ffn_in"][1, 0], a["ffn_out"][1, 0])
    w = a["odd_w_in"][0]
    square(np.concatenate([w[:, odd], w[:, 1024:]], 1))
    square(a["odd_w_out"][0][odd])
    ffn(a["ffn_in"][1, 1], a["ffn_out"][1, 1])

    square(a["l0_w_mod_2"])
    none = lambda n: np.full(n, -1)
    c = np.arange(a["l0_w_in_2"].shape[1])
    krope, gates = c[640:672], c[2720:2736]
    square(padded(a["l0_w_in_2"], np.concatenate([c[0:640], c[672:2720], c[2736:3760], krope, gates, none(16), krope,
                                                  none(32)])))
    uq = np.zeros((4, P, D), np.float32)
    for h in range(8):
        q = np.arange(96 * h, 96 * h + 96)
        cols = np.concatenate([q, none(32)] if h % 2 == 0 else [q[64:], none(32), q[:64]])
        w = padded(a["l0_mla_w_uq_2"], cols).reshape(3, P, P).transpose(1, 0, 2).reshape(P, 3 * P)
        uq[h // 2, :, h % 2 * 3 * P:(h % 2 + 1) * 3 * P] = w
    slabs_k.append(uq)
    ukv = a["l0_mla_w_ukv_2"].reshape(2, P, 4, 2, 2, HD)
    slabs_k.append(ukv.transpose(4, 1, 2, 0, 3, 5).reshape(2, P, D))
    square(a["l0_w_out_2"])
    square(a["l1_w_mod_2"])
    c = np.arange(a["l1_w_in_2"].shape[1])
    square(padded(a["l1_w_in_2"], np.concatenate([c[0:1024], c[1056:3616], c[1024:1040], none(16), c[1040:1056],
                                                  none(80)])))
    square(a["l1_w_out_2"])

    col = lambda v: np.asarray(v).reshape(-1, P).T
    def gate_rows(v):
        out = np.zeros((P, 1), np.float32)
        out[0:4, 0], out[32:36, 0] = v[0], v[1]
        return out

    pair = lambda lat, ctx: np.stack([col(ctx), col(lat)], 2).reshape(P, 2 * KT)
    v = {"c": pair(a["c"][0], a["c_ctx"]), "bmod0": col(a["b_mod"][0]), "bmod1": col(a["b_mod"][1]),
         "qgain": np.concatenate([a["q_gain"][0]] * 2)[:, None], "kgain": np.concatenate([a["k_gain"][0]] * 2)[:, None],
         "mu": col(a["rwkv_mu"][0]), "w0": col(a["rwkv_w0"][0]), "a0": col(a["rwkv_a0"][0]), "kk": col(a["rwkv_k_k"][0]),
         "ka": col(a["rwkv_k_a"][0]), "rk": col(a["rwkv_r_k"][0]), "gnw": col(a["rwkv_gn_w"][0]),
         "gnb": col(a["rwkv_gn_b"][0]), "sink": np.broadcast_to(a["sink"][0][None, :], (P, 16)),
         "fgain": col(a["final_gain"]), "c2": pair(a["c_2"][0], a["c_ctx_2"]), "n0": col(a["l0_norm_2"]),
         "bm0": col(a["l0_b_mod_2"]), "qn": col(a["l0_mla_q_norm_2"]), "kvn": col(a["l0_mla_kv_norm_2"]),
         "cw": col(a["l0_mlstm_conv_w_2"]), "cb": col(a["l0_mlstm_conv_b_2"]), "bi": gate_rows(a["l0_mlstm_b_i_2"]),
         "bf": gate_rows(a["l0_mlstm_b_f_2"]), "mn": col(a["l0_mlstm_norm_2"]), "n1": col(a["l1_norm_2"]),
         "bm1": col(a["l1_b_mod_2"]), "bg": col(a["l1_gla_b_gate_2"]), "gln": col(a["l1_gla_norm_2"]),
         "fn": col(a["final_norm_2"])}
    wg = np.zeros((P, 256), np.float32)
    wg[0:16], wg[32:48] = a["l1_gla_w_gate_2"][0], a["l1_gla_w_gate_2"][1]
    small = np.concatenate([a["rwkv_w2"][0].reshape(P, 512), a["rwkv_a2"][0].reshape(P, 512), a["rwkv_g2"][0], wg], 1)
    tok = lambda x: x[0].T.reshape(KT, P, TC).transpose(1, 0, 2)
    q, k = np.arange(TC)[:, None], np.arange(TC)[None, :]
    bias = a["l1_na_rpb_2"][:, k // GRID_W - q // GRID_W + 7, np.clip(k % GRID_W - q % GRID_W + 15, 0, 30)]
    bias = np.stack([bias[2 * t + b, (qt - 2) * P:(qt - 1) * P] for t, b, qt in attention_units("na")], 1)
    return {"xin": np.concatenate([tok(a["ctx"]), tok(a["x"])], 2), "ctx2": tok(a["ctx_2"]),
            "stream_k": np.concatenate(slabs_k, 0), "stream_f": np.concatenate(slabs_f, 0),
            "vecs": np.concatenate([v[n] for n, _ in VECS], 1), "consts": shape_constants(), "small": small,
            "nabias": bias.reshape(P, -1)}


INPUTS = ["xin", "ctx2", "stream_k", "stream_f", "vecs", "consts", "small", "nabias"]


def kernel(**inputs):
    import concourse.bacc as bacc
    from concourse.bass_utils import run_bass_kernel_spmd

    laid = lay_out({n: np.asarray(x) for n, x in inputs.items()})
    nc = bacc.Bacc("TRN2", target_bir_lowering=False, num_devices=1)
    arrays, args = {}, []
    for name in INPUTS:
        arrays[name] = np.ascontiguousarray(laid[name])
        args.append(nc.dram_tensor(name, arrays[name].shape, F32, kind="ExternalInput").ap())
    result = nc.dram_tensor("result", (P, KT, TC), F32, kind="ExternalOutput").ap()
    build(nc, *args, result)
    r = run_bass_kernel_spmd(nc, [arrays], core_ids=[0]).results[0]["result"]
    return np.ascontiguousarray(r.transpose(2, 1, 0).reshape(1, TC, D))
```

```python
from contextlib import ExitStack

import numpy as np

import concourse.bass as bass
from concourse import mybir

F32 = mybir.dt.float32
ALU = mybir.AluOpType
ACT = mybir.ActivationFunctionType
AX = mybir.AxisListType

P = 128
D = 1024
KT = D // P
TC = 256
T = 2 * TC
TT = T // P
DFF = 2816
FT = DFF // P
GRID_W = 64
HD = 64
EPS, GN_EPS = 1e-6, 64e-5
NEG = -1e30
DECAY_C = float(np.exp(-0.5))
RING = 4
OUT_PARTS = (8, 7, 7)
LEVELS = (1, 2, 4, 8, 16, 32, 64)
CHUNK = 64
NCH = T // CHUNK
BLOCK_LEVELS = (2, 4, 8, 16, 32)
CTX, LAT, ALL = (0, TC), (TC, T), (0, T)

VECS = [("c", 16), ("c2", 16), ("bmod0", 72), ("bmod1", 72), ("bm0", 24), ("bm1", 24), ("qgain", 1), ("kgain", 1), ("mu", 30), ("w0", 8), ("a0", 8),
        ("kk", 4), ("ka", 4), ("rk", 4), ("gnw", 4), ("gnb", 4), ("sink", 16), ("fgain", 8),
        ("n0", 8), ("qn", 3), ("kvn", 2), ("cw", 24), ("cb", 8), ("bi", 1), ("bf", 1), ("mn", 4),
        ("n1", 8), ("bg", 4), ("gln", 4), ("fn", 8)]
CONSTS = [("ident", P), ("ones", P), ("blk", P), ("rot", P), ("rotm", P), ("ident64", 64), ("sel_i", 64),
          ("sel_f", 64), ("mu", 7 * P), ("ml", 7 * P), ("su", P), ("sl", P), ("iu", P), ("il", P),
          ("nu", P), ("nl", P), ("cosa", TC), ("sina", TC), ("cosme", TC), ("sinme", TC), ("cosmo", TC),
          ("sinmo", TC), ("cosmk", TC), ("sinmk", TC), ("wmask", 2 * TC), ("namask", 2 * TC), ("reset", T), ("padkeys", 1)]
SMALL = [("w2", 512), ("a2", 512), ("g2", 512), ("wg", 256)]


def offsets(table):
    at, out = 0, {}
    for name, n in table:
        out[name] = (at, n)
        at += n
    return out, at


MOD_BATCHES = [(0, 28), (28, 72), (72, 116), (116, 160), (160, 192)]
MOD_SCALES = {1: None, 4: None, 7: None, 10: None, 13: None, 16: None, 19: "n0", 22: "n1"}
MOD_HALF_GATES = (2, 8, 11, 17)
FFN_RUNS = [[(11, 0)], [(11, 0)], [(7, 0), (4, 1)], [(8, 1), (3, None)]]


def ffn_slabs(f):
    lo, hi = MOD_BATCHES[f + 1]
    return [(f"ffn_in{f}", 2 * FT + hi - lo), (f"ffn_out{f}", len(OUT_PARTS) * KT)]


SLABS = [("mods", MOD_BATCHES[0][1]), *ffn_slabs(0), ("even_in", 21), ("even_out", KT), *ffn_slabs(1), *ffn_slabs(2),
         ("odd_in", 12), ("odd_out", KT), *ffn_slabs(3), ("l0_in", 30), ("mla_up", 6), ("l0_out", KT), ("l1_in", 29),
         ("l1_out", KT)]
SLAB_AT, N_SLABS = offsets(SLABS)
NORMS = [(ALL, 0, KT, 0, 0), (ALL, 3 * KT, 4 * KT, 0, 1), (ALL, 6 * KT, 7 * KT, 4, 2),
         (ALL, 72, 72 + KT, 0, 3), (ALL, 72 + 3 * KT, 72 + 4 * KT, 0, 4), (LAT, 72 + 6 * KT, 72 + 7 * KT, 4, 5),
         (ALL, 144, 144 + KT, 2, 7), (ALL, 168, 168 + KT, 4, 8)]
GAIN_NORMS = [("fgain", 0, 6), ("fn", 4, 9)]
FFNS = [(ALL, 2 * KT), (ALL, 8 * KT), (ALL, 72 + 2 * KT), (LAT, 72 + 8 * KT)]
LINEARS = [("even_in", 21, 1), ("odd_in", 12, 4), ("l0_in", 30, 6), ("l1_in", 29, 7)]
RESIDUALS = [("even_out", ALL, 5 * KT), ("odd_out", LAT, 72 + 5 * KT), ("l0_out", ALL, 144 + 2 * KT),
             ("l1_out", LAT, 168 + 2 * KT)]
ATTENTIONS = ("even", "odd", "mla", "na")


def linear_copies_before(p, who):
    return 2 + sum((n + 1 - who) // 2 for _, n, _ in LINEARS[:p])


def attention_units(which):
    if which == "even":
        return [(t, b, qt) for t in range(4) for qt in range(TT) for b in range(2)]
    if which == "odd":
        return [(t, b, qt) for t in range(8) for qt in (2, 3) for b in range(2)]
    if which == "mla":
        return [(t, b, qt) for t in range(4) for qt in range(TT) for b in range(2)]
    return [(t, b, qt) for t in range(4) for qt in (2, 3) for b in range(2)]


def units_before(a):
    return sum(len(attention_units(which)) for which in ATTENTIONS[:a])


def build(nc, xin, ctx2, stream_k, stream_f, vecs, consts, small, nabias, out):
    VO, NV = offsets(VECS)
    CO, NCST = offsets(CONSTS)
    SO, NS = offsets(SMALL)
    with ExitStack() as ctx:
        def sb(name, shape):
            return ctx.enter_context(nc.sbuf_tensor(name, shape, F32))

        def sem(name):
            return ctx.enter_context(nc.semaphore(name))

        X = sb("residual_stream", [P, KT, T])
        H = sb("mixer_io", [P, KT, T])
        BIG = sb("projections", [P, 30, T])
        WORK = sb("work", [P, 28, T])
        SPARE = sb("spare_tiles", [P, 2, T])
        ring = sb("weight_ring", [P, RING, D])
        vec = sb("vectors", [P, NV])
        cst = sb("constants", [P, NCST])
        smallw = sb("small_weights", [P, NS])
        MODS = sb("modulation", [P, 192, 2])
        conds = sb("silu_conditions", [P, 2, 2 * KT])
        stat = sb("row_statistics", [P, 3, 5])
        wstat = sb("wkv_vectors", [P, 2, 4, NCH])
        omka = sb("one_minus_ka", [P, 4])
        mu_rest = sb("one_minus_mus", [P, 15])
        epsb = sb("epsilons", [P, 4])
        pb = [ctx.enter_context(nc.psum_tensor(f"bank{i}", [P, 512], F32)) for i in range(8)]

        def V(name, i=0, n=1):
            return vec[:, VO[name][0] + i:VO[name][0] + i + n]

        def C(name, i=0, n=None):
            o, w = CO[name]
            return cst[:, o + i:o + i + (w if n is None else n)]

        def S(name, p0, p1, i, n):
            o = SO[name][0]
            return smallw[p0:p1, o + i:o + i + n]

        def tiles(ap, n=P):
            return ap.rearrange("p (a n) -> p a n", n=n)

        def over(ap, n):
            return ap.unsqueeze(1).to_broadcast([ap.shape[0], n, ap.shape[1]])

        def along(ap, n):
            return ap.unsqueeze(2).to_broadcast([ap.shape[0], ap.shape[1], n])

        def segments(cols):
            return [(s, a, b) for s, (a, b) in enumerate((CTX, LAT)) if a >= cols[0] and b <= cols[1]]

        loaded = sem("inputs_loaded")
        prepared = sem("vectors_prepared")
        ctx2_loaded = sem("ctx2_loaded")
        nab_loaded = sem("na_bias_loaded")
        stored = sem("output_stored")
        slot_full = [sem(f"slot_full{i}") for i in range(RING)]
        slab_done = sem("slab_multiplied")
        conds_ready = sem("silu_of_condition_ready")
        mods_ready = sem("modulation_ready")
        squared = sem("tile_squared")
        summed = sem("squares_summed")
        rooted = sem("rms_ready")
        scaled = sem("tile_scaled")
        modulated = sem("tile_modulated")
        copied = [sem("tile_copied_by_scalar"), sem("tile_copied_by_vector")]
        gated = sem("gate_tile_silu")
        hidden = sem("hidden_tile_ready")
        ffn_added = sem("ffn_tile_added")
        mixer_added = sem("mixer_tile_added")
        heads_ready = sem("heads_ready")
        values_ready = sem("values_by_token_ready")
        scores_ready = sem("scores_ready")
        max_ready = sem("row_max_ready")
        probs_ready = sem("probs_ready")
        probs_scaled = sem("probs_scaled")
        probs_turned = sem("probs_transposed")
        turned_copied = sem("transposed_probs_copied")
        mixed = sem("values_mixed")
        mixed_copied = sem("mixed_values_copied")
        mixer_ready = sem("mixer_output_ready")

        def take(pe, n, i=None, per=0):
            full = 16 * (n // RING + 1)
            pe.wait_ge(slot_full[n % RING], full if i is None else i * (16 * per // RING) + full)
            return ring[:, n % RING, :]

        def setup_scalar(act):
            act.sem_inc(copied[0], 2)
            act.sem_inc(gated, 2)
            act.wait_ge(loaded, 16 * 4)
            act.wait_ge(prepared, 1)

        def setup_vector(dve):
            dve.sem_inc(copied[1], 2)
            dve.sem_inc(hidden, 2)
            dve.sem_inc(ffn_added, 4)
            dve.sem_inc(mixer_added, 4)
            dve.memset(epsb[:, 0:1], EPS)
            dve.memset(epsb[:, 1:2], HD * EPS)
            dve.memset(epsb[:, 2:3], GN_EPS).then_inc(prepared, 1)
            dve.wait_ge(loaded, 16 * 4)
            dve.tensor_scalar(omka[:, :], V("ka", 0, 4), -1.0, 1.0, ALU.mult, ALU.add)
            dve.tensor_tensor(mu_rest[:, :], V("mu", 0, 15), V("mu", 15, 15), ALU.add)
            dve.drain()
            dve.tensor_scalar(mu_rest[:, :], mu_rest[:, :], -1.0, 1.0, ALU.mult, ALU.add)

        def mods_scalar(act):
            act.activation(conds[:, :, :].rearrange("p c k -> p (c k)"), V("c", 0, 4 * KT), ACT.Silu).then_inc(conds_ready, 1)

        def mod_product(pe, w, kt, cond, column):
            return pe.matmul(pb[7][:, column], w[:, kt * P:(kt + 1) * P], conds[:, cond, 2 * kt:2 * kt + 2],
                             start=kt == 0, stop=kt == KT - 1)

        def mods_tensor(pe):
            pe.wait_ge(conds_ready, 1)
            with pe.Fori(0, MOD_BATCHES[0][1] // RING) as i:
                for k in range(RING):
                    w = take(pe, SLAB_AT["mods"][0] + k, i, RING)
                    for kt in range(KT):
                        mm = mod_product(pe, w, kt, 0, bass.ds(i * (2 * RING) + 2 * k, 2))
                    mm.then_inc(slab_done, 1)

        def mods_vector(dve, b, done):
            lo, hi = MOD_BATCHES[b]
            dve.wait_ge(slab_done, done)
            dve.tensor_tensor(MODS[:, lo:hi, :], pb[7][:, 0:2 * (hi - lo)].rearrange("p (m s) -> p m s", s=2),
                              along(V("bmod0", lo, hi - lo), 2), ALU.add)
            dve.drain()
            for q in range(lo // KT, hi // KT):
                group = MODS[:, q * KT:(q + 1) * KT, :]
                if q in MOD_SCALES:
                    dve.tensor_scalar(group, group, 1.0, None, ALU.add)
                    if MOD_SCALES[q] is not None:
                        dve.drain()
                        dve.tensor_tensor(group, group, along(V(MOD_SCALES[q], 0, KT), 2), ALU.mult)
                if q in MOD_HALF_GATES:
                    dve.tensor_scalar(group, group, 0.5, None, ALU.mult)
            dve.drain().then_inc(mods_ready, 1)

        SQ = WORK[:, 20:28, :]

        def square_tiles(act, cols, x_ready, x0):
            a, b = cols
            for kt in range(KT):
                if x_ready is not None:
                    act.wait_ge(x_ready, x0 + kt)
                act.activation(SQ[:, kt, a:b], X[:, kt, a:b], ACT.Square).then_inc(squared, 1)

        def root(act, cols, bank, place):
            a, b = cols
            act.wait_ge(summed, place + 1)
            act.activation(WORK[:, 0, a:b], pb[bank][:, a:b], ACT.Sqrt, bias=epsb[:, 0:1], scale=1.0 / D)\
               .then_inc(rooted, 1)

        def norm_scalar(act, n, x_ready=None, x0=0):
            cols, shift, scale, bank, place = NORMS[n]
            square_tiles(act, cols, x_ready, x0)
            root(act, cols, bank, place)
            act.wait_ge(mods_ready, (1, 2, 2, 3, 3, 4, 4, 5)[n])
            for kt in range(KT):
                act.wait_ge(scaled, place * KT + kt + 1)
                for s, p, q in segments(cols):
                    ins = act.activation(H[:, kt, p:q], H[:, kt, p:q], ACT.Identity,
                                         bias=MODS[:, shift + kt, s:s + 1], scale=MODS[:, scale + kt, s:s + 1])
                ins.then_inc(modulated, 1)

        def sum_squares(pe, cols, bank, place):
            a, b = cols
            for kt in range(KT):
                pe.wait_ge(squared, place * KT + kt + 1)
                mm = pe.matmul(pb[bank][:, a:b], C("ones"), SQ[:, kt, a:b], start=kt == 0, stop=kt == KT - 1)
            mm.then_inc(summed, 1)

        def norm_tensor(pe, n):
            sum_squares(pe, NORMS[n][0], NORMS[n][3], NORMS[n][4])

        def norm_vector(dve, n):
            (a, b), _, _, bank, place = NORMS[n]
            dve.wait_ge(rooted, place + 1)
            dve.reciprocal(pb[bank + 1][:, a:b], WORK[:, 0, a:b])
            dve.drain()
            for kt in range(KT):
                dve.tensor_tensor(H[:, kt, a:b], X[:, kt, a:b], pb[bank + 1][:, a:b], ALU.mult).then_inc(scaled, 1)

        def gain_norm_scalar(act, g, x_ready, x0):
            _, bank, place = GAIN_NORMS[g]
            square_tiles(act, LAT, x_ready, x0)
            root(act, LAT, bank, place)

        def gain_norm_tensor(pe, g):
            sum_squares(pe, LAT, *GAIN_NORMS[g][1:])

        def gain_norm_vector(dve, g):
            gain, bank, place = GAIN_NORMS[g]
            a, b = LAT
            dve.wait_ge(rooted, place + 1)
            dve.reciprocal(pb[bank + 1][:, a:b], WORK[:, 0, a:b])
            dve.drain()
            for kt in range(KT):
                dve.scalar_tensor_tensor(out=X[:, kt, a:b], in0=X[:, kt, a:b], scalar=V(gain, kt),
                                         in1=pb[bank + 1][:, a:b], op0=ALU.mult, op1=ALU.mult).then_inc(scaled, 1)

        def linear_tensor(pe, p):
            stage, n, norm = LINEARS[p]
            n0 = SLAB_AT[stage][0]

            def product(m, i=None):
                w = take(pe, n0 + m, i, RING)
                c = linear_copies_before(p, m % 2) - 2 + m // 2 + 1
                pe.wait_ge(copied[m % 2], c if i is None else i * 2 + c)
                for kt in range(KT):
                    if m == 0:
                        pe.wait_ge(modulated, norm * KT + kt + 1)
                    mm = pe.matmul(pb[m % 4][:, :], w[:, kt * P:(kt + 1) * P], H[:, kt, :], start=kt == 0,
                                   stop=kt == KT - 1)
                mm.then_inc(slab_done, 1)

            with pe.Fori(0, n // 4) as i:
                for k in range(4):
                    product(k, i)
            for m in range(n // 4 * 4, n):
                product(m)

        def linear_copies(eng, copy, p, who):
            stage, n, _ = LINEARS[p]

            def one(m, i=None):
                d = SLAB_AT[stage][0] + m + 1
                eng.wait_ge(slab_done, d if i is None else i * 4 + d)
                dst = BIG[:, m, :] if i is None else BIG[:, bass.ds(i * 4 + m, 1), :].rearrange("p o t -> p (o t)")
                copy(dst, pb[m % 4][:, :]).then_inc(copied[who], 1)

            with eng.Fori(0, n // 4) as i:
                for k in range(who, 4, 2):
                    one(k, i)
            for m in range(n // 4 * 4, n):
                if m % 2 == who:
                    one(m)

        def linear_scalar(act, p):
            linear_copies(act, lambda d, s: act.activation(d, s, ACT.Copy), p, 0)

        def linear_vector(dve, p):
            linear_copies(dve, dve.tensor_copy, p, 1)

        def all_copied(eng, p, who):
            eng.wait_ge(copied[who], linear_copies_before(p + 1, who))

        def add_tiles(dve, cols, gate, slabs_each, n0, bank0, added):
            with dve.Fori(0, KT // 4) as i:
                for k in range(4):
                    dve.wait_ge(slab_done, i * (4 * slabs_each) + (n0 + slabs_each * (k + 1)))
                    for s, p, q in segments(cols):
                        x = X[:, bass.ds(i * 4 + k, 1), p:q].rearrange("p o t -> p (o t)")
                        g = MODS[:, bass.ds(i * 4 + (gate + k), 1), s:s + 1].rearrange("p o t -> p (o t)")
                        ins = dve.scalar_tensor_tensor(out=x, in0=pb[bank0 + k][:, p:q], scalar=g, in1=x,
                                                       op0=ALU.mult, op1=ALU.add)
                    ins.then_inc(added, 1)

        def residual_tensor(pe, r):
            stage, (a, b), _ = RESIDUALS[r]
            pe.wait_ge(mixer_ready, r + 1)
            with pe.Fori(0, KT // 4) as i:
                for k in range(4):
                    w = take(pe, SLAB_AT[stage][0] + k, i, 4)
                    pe.wait_ge(mixer_added, i * 4 + (r * KT + k + 1))
                    for kt in range(KT):
                        mm = pe.matmul(pb[k][:, a:b], w[:, kt * P:(kt + 1) * P], H[:, kt, a:b], start=kt == 0,
                                       stop=kt == KT - 1)
                    mm.then_inc(slab_done, 1)

        def residual_vector(dve, r):
            stage, cols, gate = RESIDUALS[r]
            add_tiles(dve, cols, gate, 1, SLAB_AT[stage][0], 0, mixer_added)

        def ffn_turns(f):
            n, t, out = SLAB_AT[f"ffn_in{f}"][0], f * FT, []
            for turns, cond in FFN_RUNS[f]:
                per = 4 if cond is None else 8
                out.append((turns, cond, per, n, t))
                n, t = n + per * turns, t + 2 * turns
            return out

        def ffn_tensor(pe, f):
            a, b = FFNS[f][0]
            norm, m0 = (0, 2, 3, 5)[f], 0
            pe.wait_ge(mods_ready, f + 1)
            for turns, cond, per, n0, t0 in ffn_turns(f):
                with pe.Fori(0, turns) as i:
                    for k in range(4):
                        w = take(pe, n0 + k * per // 4, i, per)
                        pe.wait_ge(hidden if k % 2 else gated, i * 2 + (t0 + k // 2 + 1))
                        for kt in range(KT):
                            if k == 0:
                                pe.wait_ge(modulated, norm * KT + kt + 1)
                            mm = pe.matmul(pb[k][:, a:b], w[:, kt * P:(kt + 1) * P], H[:, kt, a:b], start=kt == 0,
                                           stop=kt == KT - 1)
                        mm.then_inc(slab_done, 1)
                        if cond is not None:
                            w = take(pe, n0 + 2 * k + 1, i, per)
                            for kt in range(KT):
                                mm = mod_product(pe, w, kt, cond, bass.ds(i * 8 + (m0 + 2 * k), 2))
                            mm.then_inc(slab_done, 1)
                m0 += 8 * turns
            n0 = SLAB_AT[f"ffn_out{f}"][0]
            pe.wait_ge(hidden, 2 + (f + 1) * FT)
            pe.wait_ge(mods_ready, f + 2)
            with pe.Fori(0, KT // 4) as i:
                for k in range(4):
                    pe.wait_ge(ffn_added, i * 4 + (f * KT + k + 1))
                    t = 0
                    for part, n in enumerate(OUT_PARTS):
                        w = take(pe, n0 + len(OUT_PARTS) * k + part, i, 4 * len(OUT_PARTS))
                        for q in range(n):
                            mm = pe.matmul(pb[4 + k][:, a:b], w[:, q * P:(q + 1) * P], BIG[:, t, a:b], start=t == 0,
                                           stop=t == FT - 1)
                            t += 1
                        mm.then_inc(slab_done, 1)

        def ffn_scalar(act, f):
            a, b = FFNS[f][0]
            for turns, _, per, n0, t0 in ffn_turns(f):
                with act.Fori(0, turns) as i:
                    for j in range(2):
                        act.wait_ge(slab_done, i * per + (n0 + j * per // 2 + 1))
                        act.wait_ge(hidden, i * 2 + (t0 + j + 1))
                        act.activation(WORK[:, j, a:b], pb[2 * j][:, a:b], ACT.Silu).then_inc(gated, 1)

        def ffn_vector(dve, f):
            (a, b), gate = FFNS[f]
            for turns, _, per, n0, t0 in ffn_turns(f):
                with dve.Fori(0, turns) as i:
                    for j in range(2):
                        dve.wait_ge(slab_done, i * per + (n0 + j * per // 2 + per // 4 + 1))
                        dve.wait_ge(gated, i * 2 + (2 + t0 + j + 1))
                        h = BIG[:, bass.ds(i * 2 + (t0 - f * FT + j), 1), a:b].rearrange("p o t -> p (o t)")
                        dve.tensor_tensor(h, WORK[:, j, a:b], pb[2 * j + 1][:, a:b], ALU.mult).then_inc(hidden, 1)
            mods_vector(dve, f + 1, SLAB_AT[f"ffn_out{f}"][0])
            add_tiles(dve, (a, b), gate, len(OUT_PARTS), SLAB_AT[f"ffn_out{f}"][0], 4, ffn_added)

        def attention_operands(which, t, b, qt):
            q0, nk = qt * P, (TC if qt < 2 else T)
            rows = slice(HD * b, HD * b + HD)
            if which == "even":
                pairs = [(BIG[rows, t, q0:q0 + P], BIG[rows, 4, 0:nk])]
                return pairs, nk, H[rows, t, q0:q0 + P], HD * b
            if which == "odd":
                pairs = [(BIG[rows, t, q0:q0 + P], BIG[rows, 8 + t // 4, 0:nk])]
                return pairs, nk, H[rows, t, q0:q0 + P], t // 4 * P + HD * b
            if which == "mla":
                rope = slice(64 * (1 - b), 64 * (1 - b) + 32)
                pairs = [(WORK[rows, 2 * t + b, q0:q0 + P], WORK[rows, 8 + t, 0:nk]),
                         (WORK[rope, 2 * t + b, q0:q0 + P], BIG[rope, 29, 0:nk])]
                return pairs, nk, H[rows, t, q0:q0 + P], t * P + HD * b
            pairs = [(BIG[rows, 8 + t, q0:q0 + P], BIG[rows, 12 + t, 0:nk])]
            return pairs, nk, H[rows, 4 + t, q0:q0 + P], t * P + HD * b

        score_bank = (pb[0], pb[1], pb[6])
        PROBS = WORK[:, 24:27, :]

        def attend_tensor(pe, a):
            which, u0 = ATTENTIONS[a], units_before(a)
            units = attention_units(which)
            n = len(units)
            pe.wait_ge(heads_ready, a + 1)
            pe.wait_ge(values_ready, a + 1)
            for it in range(n + 3):
                if it < n:
                    pairs, nk, _, _ = attention_operands(which, *units[it])
                    if it >= 3:
                        pe.wait_ge(probs_ready, u0 + it - 2)
                    for i, (q, k) in enumerate(pairs):
                        mm = pe.matmul(score_bank[it % 3][:, 0:nk], q, k, start=i == 0, stop=i == len(pairs) - 1)
                    mm.then_inc(scores_ready, 1)
                u = it - 2
                if 0 <= u < n:
                    nk = attention_operands(which, *units[u])[1]
                    pe.wait_ge(probs_scaled, u0 + u + 1)
                    if u >= 2:
                        pe.wait_ge(turned_copied, u0 + u - 1)
                    for i in range(nk // P):
                        mm = pe.transpose(pb[2 + u % 2][:, i * P:(i + 1) * P], PROBS[:, u % 3, i * P:(i + 1) * P],
                                          C("ident"))
                    mm.then_inc(probs_turned, 1)
                u = it - 3
                if 0 <= u < n:
                    _, nk, _, ch = attention_operands(which, *units[u])
                    b = units[u][1]
                    pe.wait_ge(turned_copied, u0 + u + 1)
                    if u >= 2:
                        pe.wait_ge(mixed_copied, u0 + u - 1)
                    for i in range(nk // P):
                        mm = pe.matmul(pb[4 + u % 2][HD * b:HD * b + HD, 0:P], WORK[:, 12 + i, ch:ch + HD],
                                       WORK[:, 22 + u % 2, i * P:(i + 1) * P], start=i == 0, stop=i == nk // P - 1)
                    mm.then_inc(mixed, 1)

        def attend_vector(dve, a):
            which, u0 = ATTENTIONS[a], units_before(a)
            units = attention_units(which)
            n = len(units)
            if which == "na":
                dve.wait_ge(nab_loaded, 16)
            for it in range(n + 4):
                if it < n:
                    t, b, qt = units[it]
                    nk = attention_operands(which, t, b, qt)[1]
                    sc, st = score_bank[it % 3], stat[:, it % 3, :]
                    dve.wait_ge(scores_ready, u0 + it + 1)
                    if which in ("odd", "na"):
                        mask = C("wmask" if which == "odd" else "namask", (qt - 2) * TC, TC)
                        dve.tensor_tensor(sc[:, TC:T], sc[:, TC:T], mask, ALU.add)
                        dve.drain()
                    if which == "na":
                        bias = WORK[:, 0:8, :].rearrange("p a (b k) -> p (a b) k", k=TC)[:, it, :]
                        dve.tensor_tensor(sc[:, TC:T], sc[:, TC:T], bias, ALU.add)
                        dve.drain()
                    ins = dve.tensor_reduce(st[:, 0:1], sc[:, 0:nk], AX.X, ALU.max, negate=True)
                    if which == "odd":
                        dve.drain()
                        sink = V("sink", 8 * (t // 4) + 4 * b + t % 4)
                        ins = dve.scalar_tensor_tensor(out=st[:, 0:1], in0=sink, scalar=-1.0, in1=st[:, 0:1],
                                                       op0=ALU.mult, op1=ALU.min)
                        if qt == 3:
                            dve.drain()
                            ins = dve.tensor_scalar(st[:, 0:1], st[:, 0:1], 0.0, None, ALU.min)
                    ins.then_inc(max_ready, 1)
                u = it - 1
                if 0 <= u < n:
                    nk = attention_operands(which, *units[u])[1]
                    st, probs = stat[:, u % 3, :], PROBS[:, u % 3, 0:nk]
                    dve.wait_ge(probs_ready, u0 + u + 1)
                    if which == "odd":
                        dve.tensor_tensor(st[:, 1:2], st[:, 1:2], st[:, 2:3], ALU.add)
                        dve.drain()
                        if units[u][2] == 3:
                            dve.scalar_tensor_tensor(out=st[:, 1:2], in0=C("padkeys"), scalar=st[:, 4:5],
                                                     in1=st[:, 1:2], op0=ALU.mult, op1=ALU.add)
                            dve.drain()
                    dve.reciprocal(st[:, 3:4], st[:, 1:2])
                    dve.drain()
                    dve.tensor_scalar(probs, probs, st[:, 3:4], None, ALU.mult).then_inc(probs_scaled, 1)
                u = it - 4
                if 0 <= u < n:
                    b = units[u][1]
                    o = attention_operands(which, *units[u])[2]
                    dve.wait_ge(mixed, u0 + u + 1)
                    dve.tensor_copy(o, pb[4 + u % 2][HD * b:HD * b + HD, 0:P]).then_inc(mixed_copied, 1)
            if which == "odd":
                dve.drain().then_inc(mixer_ready, 1)

        def attend_scalar(act, a):
            which, u0 = ATTENTIONS[a], units_before(a)
            units = attention_units(which)
            n = len(units)
            for it in range(n + 2):
                if it < n:
                    t, b, qt = units[it]
                    nk = attention_operands(which, t, b, qt)[1]
                    st = stat[:, it % 3, :]
                    act.wait_ge(max_ready, u0 + it + 1)
                    if it >= 3:
                        act.wait_ge(probs_turned, u0 + it - 2)
                    if which == "odd":
                        act.activation(st[:, 2:3], V("sink", 8 * (t // 4) + 4 * b + t % 4), ACT.Exp, bias=st[:, 0:1])
                        if qt == 3:
                            act.activation(st[:, 4:5], st[:, 0:1], ACT.Exp)
                    act.activation(PROBS[:, it % 3, 0:nk], score_bank[it % 3][:, 0:nk], ACT.Exp, bias=st[:, 0:1],
                                   accum_out=st[:, 1:2]).then_inc(probs_ready, 1)
                u = it - 2
                if 0 <= u < n:
                    nk = attention_operands(which, *units[u])[1]
                    act.wait_ge(probs_turned, u0 + u + 1)
                    if u >= 2:
                        act.wait_ge(mixed, u0 + u - 1)
                    act.activation(WORK[:, 22 + u % 2, 0:nk], pb[2 + u % 2][:, 0:nk], ACT.Copy)\
                       .then_inc(turned_copied, 1)

        qk_squared, qk_summed, qk_rooted = sem("head_squared"), sem("head_squares_summed"), sem("head_rms_ready")
        qk_normed, qk_turned = sem("head_normed"), sem("head_rotated_half_ready")
        values_turned = sem("values_transposed")
        q_turned, q_rotated, k_turned = sem("query_half_ready"), sem("queries_rotated"), sem("key_half_ready")
        low_squared, low_summed, low_rooted = sem("low_rank_squared"), sem("low_rank_summed"), sem("low_rank_rms_ready")
        low_normed = sem("low_rank_normed")
        q_copied, k_copied, v_copied = sem("mla_query_copied"), sem("mla_key_copied"), sem("mla_value_copied")
        mq_turned, mq_rotated, mk_turned = sem("mla_query_half_ready"), sem("mla_queries_rotated"), sem("mla_key_half_ready")

        def rotate(dve, jobs, scale, scratch, turned):
            for i, (x, bank, cos, sin) in enumerate(jobs):
                tmp = scratch[:, i, :]
                dve.scalar_tensor_tensor(out=tmp[:, 0:TC], in0=x[:, TC:T], scalar=scale, in1=C(cos), op0=ALU.mult,
                                         op1=ALU.mult)
                dve.wait_ge(turned, i + 1)
                dve.scalar_tensor_tensor(out=tmp[:, TC:T], in0=bank[:, TC:T], scalar=scale, in1=C(sin), op0=ALU.mult,
                                         op1=ALU.mult)
            dve.drain()
            for i, (x, _, _, _) in enumerate(jobs):
                dve.tensor_tensor(x[:, TC:T], scratch[:, i, 0:TC], scratch[:, i, TC:T], ALU.add)

        def turn_values(pe, src, n, bank0):
            for tt in range(TT):
                for j in range(n):
                    mm = pe.transpose(pb[bank0 + tt][:, j * P:(j + 1) * P], src[:, j, tt * P:(tt + 1) * P], C("ident"))
            return mm

        def even_heads_scalar(act):
            all_copied(act, 0, 1)
            act.drain()
            for i in range(5):
                act.activation(WORK[:, i, :], BIG[:, i, :], ACT.Square).then_inc(qk_squared, 1)
            for i in range(5):
                act.wait_ge(qk_summed, i + 1)
                act.activation(WORK[:, i, :], pb[i][:, :], ACT.Sqrt, bias=epsb[:, 1:2] if i < 4 else epsb[:, 0:1],
                               scale=1.0 if i < 4 else 1.0 / HD).then_inc(qk_rooted, 1)
            act.wait_ge(values_turned, 1)
            act.activation(WORK[:, 12:16, 0:P], tiles(pb[5][:, :]), ACT.Copy).then_inc(values_ready, 1)

        def even_heads_tensor(pe):
            all_copied(pe, 0, 0)
            all_copied(pe, 0, 1)
            for i in range(5):
                pe.wait_ge(qk_squared, i + 1)
                pe.matmul(pb[i][:, :], C("blk"), WORK[:, i, :], start=True, stop=True).then_inc(qk_summed, 1)
            for tt in range(TT):
                mm = pe.transpose(pb[5][:, tt * P:(tt + 1) * P], BIG[:, 5, tt * P:(tt + 1) * P], C("ident"))
            mm.then_inc(values_turned, 1)
            for i in range(5):
                pe.wait_ge(qk_normed, i + 1)
                pe.matmul(pb[i][:, TC:T], C("rot"), BIG[:, i, TC:T], start=True, stop=True).then_inc(qk_turned, 1)

        def even_heads_vector(dve):
            for i in range(5):
                dve.wait_ge(qk_rooted, i + 1)
                dve.reciprocal(pb[i][:, :], WORK[:, i, :])
                dve.drain()
                dve.scalar_tensor_tensor(out=BIG[:, i, :], in0=BIG[:, i, :], scalar=V("qgain" if i < 4 else "kgain"),
                                         in1=pb[i][:, :], op0=ALU.mult, op1=ALU.mult).then_inc(qk_normed, 1)
            dve.drain()
            rotate(dve, [(BIG[:, i, :], pb[i], "cosa", "sina") for i in range(5)], 1.0, WORK[:, 0:5, :], qk_turned)
            dve.drain().then_inc(heads_ready, 1)

        def odd_heads_tensor(pe):
            all_copied(pe, 1, 0)
            all_copied(pe, 1, 1)
            for i in range(8):
                pe.matmul(pb[i][:, TC:T], C("rot"), BIG[:, i, TC:T], start=True, stop=True).then_inc(q_turned, 1)
            pe.wait_ge(q_rotated, 1)
            for i in range(2):
                pe.matmul(pb[i][:, TC:T], C("rot"), BIG[:, 8 + i, TC:T], start=True, stop=True).then_inc(k_turned, 1)
            turn_values(pe, BIG[:, 10:12, :], 2, 2).then_inc(values_turned, 1)

        def odd_heads_vector(dve):
            all_copied(dve, 1, 0)
            rotate(dve, [(BIG[:, i, :], pb[i], "cosa", "sina") for i in range(8)], HD ** -0.5, WORK[:, 0:8, :], q_turned)
            dve.drain().then_inc(q_rotated, 1)
            rotate(dve, [(BIG[:, 8 + i, :], pb[i], "cosa", "sina") for i in range(2)], 1.0, WORK[:, 0:2, :], k_turned)
            dve.drain().then_inc(heads_ready, 1)

        def odd_heads_scalar(act):
            act.wait_ge(values_turned, 2)
            for tt in range(TT):
                ins = act.activation(WORK[:, 12 + tt, 0:2 * P], pb[2 + tt][:, 0:2 * P], ACT.Copy)
            ins.then_inc(values_ready, 1)

        UP0 = SLAB_AT["mla_up"][0]

        def mla_heads_scalar(act):
            all_copied(act, 2, 1)
            act.drain()
            for i in range(5):
                act.activation(WORK[:, i, :], BIG[:, i, :], ACT.Square).then_inc(low_squared, 1)
            for i, n in enumerate((3, 2)):
                act.wait_ge(low_summed, i + 1)
                act.activation(WORK[:, 5 + i, :], pb[i][:, :], ACT.Sqrt, bias=epsb[:, 0:1], scale=1.0 / (n * P))\
                   .then_inc(low_rooted, 1)
            act.wait_ge(low_normed, 5)
            for h in range(8):
                act.wait_ge(slab_done, UP0 + h // 2 + 1)
                act.activation(WORK[:, h, :], pb[h][:, :], ACT.Copy, scale=96 ** -0.5).then_inc(q_copied, 1)
            act.wait_ge(slab_done, UP0 + 5)
            for t in range(4):
                act.activation(WORK[:, 8 + t, :], pb[t][:, :], ACT.Copy).then_inc(k_copied, 1)
            act.wait_ge(values_turned, 3)
            for tt in range(TT):
                ins = act.activation(WORK[:, 12 + tt, :], pb[4 + tt][:, :], ACT.Copy)
            ins.then_inc(values_ready, 1)

        def mla_heads_tensor(pe):
            all_copied(pe, 2, 0)
            all_copied(pe, 2, 1)
            for i in range(5):
                bank, first, last = (0, 0, 2) if i < 3 else (1, 3, 4)
                pe.wait_ge(low_squared, i + 1)
                mm = pe.matmul(pb[bank][:, :], C("ones"), WORK[:, i, :], start=i == first, stop=i == last)
                if i == last:
                    mm.then_inc(low_summed, 1)
            pe.wait_ge(low_normed, 3)
            for n in range(4):
                w = take(pe, UP0 + n)
                if n == 3:
                    pe.wait_ge(low_normed, 5)
                for j in range(2):
                    for i in range(3):
                        mm = pe.matmul(pb[2 * n + j][:, :], w[:, (3 * j + i) * P:(3 * j + i + 1) * P], BIG[:, i, :],
                                       start=i == 0, stop=i == 2)
                mm.then_inc(slab_done, 1)
            for n in range(2):
                w = take(pe, UP0 + 4 + n)
                pe.wait_ge(q_copied, 4 * n + 4)
                for t in range(4):
                    for i in range(2):
                        mm = pe.matmul(pb[4 * n + t][:, :], w[:, (2 * t + i) * P:(2 * t + i + 1) * P], BIG[:, 3 + i, :],
                                       start=i == 0, stop=i == 1)
                mm.then_inc(slab_done, 1)
            for h in range(8):
                pe.wait_ge(*((k_copied, h + 1) if h < 4 else (v_copied, h - 3)))
                pe.matmul(pb[h][:, TC:T], C("rotm"), WORK[:, h, TC:T], start=True, stop=True).then_inc(mq_turned, 1)
            pe.wait_ge(mq_rotated, 1)
            pe.matmul(pb[0][:, TC:T], C("rotm"), BIG[:, 29, TC:T], start=True, stop=True).then_inc(mk_turned, 1)
            turn_values(pe, WORK[:, 16:20, :], 4, 4).then_inc(values_turned, 1)

        def mla_heads_vector(dve):
            for i in range(2):
                dve.wait_ge(low_rooted, i + 1)
                dve.reciprocal(pb[6 + i][:, :], WORK[:, 5 + i, :])
            dve.drain()
            for i in range(5):
                dve.scalar_tensor_tensor(out=BIG[:, i, :], in0=BIG[:, i, :], scalar=V("qn", i) if i < 3 else V("kvn", i - 3),
                                         in1=pb[6 + i // 3][:, :], op0=ALU.mult, op1=ALU.mult).then_inc(low_normed, 1)
            dve.wait_ge(slab_done, UP0 + 6)
            for t in range(4):
                dve.tensor_copy(WORK[:, 16 + t, :], pb[4 + t][:, :]).then_inc(v_copied, 1)
            dve.wait_ge(q_copied, 8)
            rotate(dve, [(WORK[:, h, :], pb[h], "cosmo" if h % 2 else "cosme", "sinmo" if h % 2 else "sinme")
                         for h in range(8)], 1.0, WORK[:, 20:28, :], mq_turned)
            dve.drain().then_inc(mq_rotated, 1)
            rotate(dve, [(BIG[:, 29, :], pb[0], "cosmk", "sinmk")], 1.0, WORK[:, 20:21, :], mk_turned)
            dve.drain().then_inc(heads_ready, 1)

        def na_heads_gpsimd(pool):
            pool.wait_ge(modulated, 8 * KT)
            pool.dma_start(WORK[:, 0:8, :].rearrange("p a b -> p (a b)"), nabias).then_inc(nab_loaded, 16)

        def na_heads_tensor(pe):
            all_copied(pe, 3, 0)
            all_copied(pe, 3, 1)
            turn_values(pe, BIG[:, 16:20, :], 4, 0).then_inc(values_turned, 1)

        def na_heads_scalar(act):
            all_copied(act, 3, 1)
            act.drain()
            for i in (0, 1, 8, 9, 10, 11):
                ins = act.activation(BIG[:, i, TC:T], BIG[:, i, TC:T], ACT.Copy, scale=HD ** -0.5)
            ins.then_inc(heads_ready, 1)
            act.wait_ge(values_turned, 4)
            for tt in range(TT):
                ins = act.activation(WORK[:, 12 + tt, :], pb[tt][:, :], ACT.Copy)
            ins.then_inc(values_ready, 1)

        def add_neighbours(dve, jobs):
            for x, y, before, after in jobs:
                for a, b in (CTX, LAT):
                    dve.scalar_tensor_tensor(out=y[:, a + 1:b], in0=x[:, a:b - 1], scalar=before, in1=y[:, a + 1:b],
                                             op0=ALU.mult, op1=ALU.add)
            dve.drain()
            for x, y, before, after in jobs:
                for a, b in (CTX, LAT):
                    dve.scalar_tensor_tensor(out=y[:, a:b - 1], in0=x[:, a + 1:b], scalar=after, in1=y[:, a:b - 1],
                                             op0=ALU.mult, op1=ALU.add)
            dve.drain()

        R_, K_, V_, WL, AL, GL = 5, 9, 13, 17, 18, 19
        KK = BIG[:, 0:4, :]
        EIT, FF = BIG[:, 20:24, :], BIG[:, 24:28, :]
        RR = WORK[:, 0:4, :]
        VTOK = WORK[:, 4:8, :]
        TOK = WORK[:, 8:11, :]
        SIG, CUM, AA, EX = (WORK[:, 11 + i, :] for i in range(4))
        FACTORS = [[WORK[:, 15 + i, :] for i in range(3)], [SPARE[:, 0, :], SPARE[:, 1, :], BIG[:, 4, :]]]
        STATE = [tiles(WORK[:, 18 + i, 0:4 * HD], HD) for i in range(2)]
        MT, MB, TI, TTI, XS = ([WORK[:, 18 + 5 * hb + i, :] for hb in range(2)] for i in range(5))
        NGH = [BIG[:, 28 + hb, :] for hb in range(2)]
        shifted, ranks_ready = sem("tokens_shifted"), sem("low_ranks_ready")
        kk_squared, kk_summed, kk_rooted, kk_ready = (sem(f"removal_key_{x}") for x in ("squared", "summed", "rms", "ready"))
        v_turned = sem("rwkv_values_transposed")
        lora_ready, rates_ready = sem("decay_and_rate_products"), sem("decay_and_rate_ready")
        decay_summed, decays_ready = sem("log_decays_summed"), sem("decays_ready")
        factors_ready = sem("alpha_beta_kappa_rho_ready")
        factors_turned, factors_by_token = sem("factors_transposed"), sem("factors_by_token_ready")
        within_ready, triangles_ready = sem("alpha_beta_products"), sem("triangles_masked")
        t_started, level_masked = sem("inverse_started"), sem("level_mask_applied")
        x_ready, x_copied = sem("off_block_product_ready"), sem("off_block_product_copied")
        z_ready, t_updated = sem("inverse_update_ready"), sem("inverse_updated")
        mixes_ready, mixes_masked = sem("kappa_rho_products"), sem("kappa_rho_masked")
        kv_ready, rhs_ready = sem("kappa_alpha_values_ready"), sem("right_sides_ready")
        solved, solved_copied = sem("right_sides_solved"), sem("solutions_copied")
        group_ready, group_added, inputs_copied = sem("group_products"), sem("group_added"), sem("state_inputs_copied")
        step_ready, state_ready = sem("state_products"), sem("state_ready")

        def wkv_features_vector(dve):
            all_copied(dve, 0, 0)
            for i in range(15):
                x, y = BIG[:, 6 + i, :], BIG[:, 5 + i, :]
                dve.tensor_scalar(y, x, mu_rest[:, i:i + 1], None, ALU.mult)
                dve.drain()
                add_neighbours(dve, [(x, y, V("mu", i), V("mu", 15 + i))])
            for j in range(4):
                dve.tensor_scalar(KK[:, j, :], BIG[:, K_ + j, :], V("kk", j), None, ALU.mult)
            dve.drain().then_inc(shifted, 1)
            dve.wait_ge(v_turned, 1)
            for tt in range(TT):
                dve.tensor_copy(VTOK[:, tt, :], pb[4 + tt][:, :])
            for j in range(4):
                dve.wait_ge(kk_rooted, j + 1)
                dve.reciprocal(WORK[:, 8 + j, :], WORK[:, 8 + j, :])
            dve.drain()
            for j in range(4):
                dve.tensor_tensor(KK[:, j, :], KK[:, j, :], WORK[:, 8 + j, :], ALU.mult)
            dve.drain().then_inc(kk_ready, 1)

        def wkv_features_scalar(act):
            act.wait_ge(shifted, 1)
            for j in range(4):
                act.activation(WORK[:, 8 + j, :], KK[:, j, :], ACT.Square).then_inc(kk_squared, 1)
            act.activation(BIG[:, WL, :], BIG[:, WL, :], ACT.Tanh)
            act.activation(BIG[:, GL, :], BIG[:, GL, :], ACT.Sigmoid).then_inc(ranks_ready, 1)
            for j in range(4):
                act.wait_ge(kk_summed, j + 1)
                act.activation(WORK[:, 8 + j, :], pb[j][:, :], ACT.Sqrt, bias=epsb[:, 0:1]).then_inc(kk_rooted, 1)

        def wkv_features_tensor(pe):
            pe.wait_ge(shifted, 1)
            turn_values(pe, BIG[:, V_:V_ + 4, :], 4, 4).then_inc(v_turned, 1)
            for j in range(4):
                pe.wait_ge(kk_squared, j + 1)
                pe.matmul(pb[j][:, :], C("blk"), WORK[:, 8 + j, :], start=True, stop=True).then_inc(kk_summed, 1)

        NLEV = 2 * len(BLOCK_LEVELS)

        def chunk_order(d):
            return list(range(NCH)) if d == 0 else [3, 2, 1, 0, 7, 6, 5, 4]

        def heads_of(j):
            return [(hb, slice(HD * hb, HD * hb + HD), slice(j * P + hb * HD, j * P + hb * HD + HD)) for hb in (0, 1)]

        def tok(i):
            return slice(i * P, (i + 1) * P)

        def wkv_tensor(pe):
            pe.wait_ge(ranks_ready, 1)
            pe.wait_ge(kk_ready, 1)
            wkv_low_ranks(pe, 0)
            for d in range(2):
                for j in range(4):
                    wkv_group_tensor(pe, d, j, 4 * d + j)
                for s, c in enumerate(chunk_order(d)):
                    if s:
                        st = STATE[(s - 1) % 2]
                        pe.wait_ge(state_ready, NCH * d + s)
                        for j in range(4):
                            for hb, rows, _ in heads_of(j):
                                o = slice(j * HD, (j + 1) * HD)
                                cc = slice(c * HD, (c + 1) * HD)
                                mm = pe.matmul(pb[hb][rows, o], st[rows, j, :], RR[rows, j, cc], start=True, stop=True)
                                if s < NCH - 1:
                                    mm = pe.matmul(pb[2 + hb][rows, o], EIT[rows, j, cc], st[rows, j, :], start=True,
                                                   stop=True)
                        mm.then_inc(step_ready, 1)

        def wkv_low_ranks(pe, g):
            low, j = slice(HD * (g // 4), HD * (g // 4) + HD), g % 4
            pe.matmul(pb[6][:, :], S("w2", low.start, low.stop, j * P, P), BIG[low, WL, :], start=True, stop=True)
            pe.matmul(pb[7][:, :], S("a2", low.start, low.stop, j * P, P), BIG[low, AL, :], start=True, stop=True)\
              .then_inc(lora_ready, 1)

        def wkv_group_tensor(pe, d, j, g):
            AL_, BE_, KA_ = FACTORS[g % 2]
            pe.wait_ge(factors_ready, g + 1)
            if g:
                pe.wait_ge(inputs_copied, g)
                pe.wait_ge(group_added, g)
            for i, x in enumerate((AL_, BE_, KA_)):
                for tt in range(TT):
                    mm = pe.transpose(pb[i][:, tok(tt)], x[:, tok(tt)], C("ident"))
            mm.then_inc(factors_turned, 1)
            for hb, rows, _ in heads_of(j):
                for tt in range(TT):
                    pe.matmul(pb[4 + hb][:, tok(tt)], BE_[rows, tok(tt)], AL_[rows, tok(tt)], start=True, stop=True)
                for tt in range(TT):
                    mm = pe.matmul(pb[6 + hb][:, tok(tt)], AL_[rows, tok(tt)], BE_[rows, tok(tt)], start=True, stop=True)
            mm.then_inc(within_ready, 1)
            pe.wait_ge(factors_by_token, g + 1)
            pe.wait_ge(t_started, g + 1)
            for li in range(len(BLOCK_LEVELS)):
                for hb in range(2):
                    q = NLEV * g + 2 * li + hb
                    pe.wait_ge(level_masked, q + 1)
                    if li:
                        pe.wait_ge(t_updated, q - 1)
                    for tt in range(TT):
                        mm = pe.matmul(pb[hb][:, tok(tt)], MB[hb][:, tok(tt)], TI[hb][:, tok(tt)], start=True, stop=True)
                    mm.then_inc(x_ready, 1)
                if li == 0 and g < 7:
                    wkv_low_ranks(pe, g + 1)
                for hb in range(2):
                    q = NLEV * g + 2 * li + hb
                    pe.wait_ge(x_copied, q + 1)
                    for tt in range(TT):
                        pe.matmul(pb[2 + hb][:, tok(tt)], TTI[hb][:, tok(tt)], XS[hb][:, tok(tt)], start=True, stop=True)
                    for tt in range(TT):
                        mm = pe.matmul(pb[4 + hb][:, tok(tt)], XS[hb][:, tok(tt)], TTI[hb][:, tok(tt)], start=True,
                                       stop=True)
                    mm.then_inc(z_ready, 1)
            pe.wait_ge(t_updated, NLEV * (g + 1))
            for hb, rows, _ in heads_of(j):
                for tt in range(TT):
                    pe.matmul(pb[hb][:, tok(tt)], KA_[rows, tok(tt)], AL_[rows, tok(tt)], start=True, stop=True)
                for tt in range(TT):
                    pe.matmul(pb[2 + hb][:, tok(tt)], KA_[rows, tok(tt)], RR[rows, j, tok(tt)], start=True, stop=True)
                for tt in range(TT):
                    mm = pe.matmul(pb[4 + hb][:, tok(tt)], BE_[rows, tok(tt)], RR[rows, j, tok(tt)], start=True, stop=True)
            mm.then_inc(mixes_ready, 1)
            pe.wait_ge(mixes_masked, g + 1)
            if g < 7:
                pe.wait_ge(rates_ready, g + 2)
            for hb, _, ch in heads_of(j):
                for tt in range(TT):
                    mm = pe.matmul(pb[6 + hb][:, tt * HD:(tt + 1) * HD], MB[hb][:, tok(tt)], VTOK[:, tt, ch], start=True,
                                   stop=True)
            mm.then_inc(kv_ready, 1)
            pe.wait_ge(rhs_ready, g + 1)
            for hb in range(2):
                for tt in range(TT):
                    mm = pe.matmul(pb[hb][:, tok(tt)], TTI[hb][:, tok(tt)], TI[hb][:, tok(tt)], start=True, stop=True)
            mm.then_inc(solved, 1)
            pe.wait_ge(solved_copied, g + 1)
            for hb, rows, ch in heads_of(j):
                gh = tiles(NGH[hb])
                for tt in range(TT):
                    pe.matmul(pb[2][rows, tok(tt)], gh[:, tt, 0:HD], MT[hb][:, tok(tt)], start=True, stop=True)
                for tt in range(TT):
                    pe.matmul(pb[3][rows, tok(tt)], VTOK[:, tt, ch], XS[hb][:, tok(tt)], start=True, stop=False)
                    pe.matmul(pb[3][rows, tok(tt)], gh[:, tt, HD:P], MT[hb][:, tok(tt)], start=False, stop=True)
                for half in range(2):
                    tr = slice(HD * half, HD * half + HD)
                    for tt in range(TT):
                        o = slice(tt * HD, (tt + 1) * HD)
                        hc = slice(tt * P + HD * hb, tt * P + HD * hb + HD)
                        pe.matmul(pb[4 + 2 * half][rows, o], gh[tr, tt, 0:HD], TOK[tr, 1, hc], start=True, stop=True)
                        pe.matmul(pb[5 + 2 * half][rows, o], TOK[tr, 2, hc], VTOK[tr, tt, ch], start=True, stop=False)
                        mm = pe.matmul(pb[5 + 2 * half][rows, o], TOK[tr, 1, hc], gh[tr, tt, HD:P], start=False, stop=True)
            mm.then_inc(group_ready, 1)

        def wkv_scalar(act):
            act.wait_ge(kk_ready, 1)

            def rates(g):
                act.wait_ge(lora_ready, g + 1)
                act.activation(SIG, pb[6][:, :], ACT.Sigmoid, bias=V("w0", g))
                act.activation(AA, pb[7][:, :], ACT.Sigmoid, bias=V("a0", g)).then_inc(rates_ready, 1)

            def decays(g):
                AL_, _, KA_ = FACTORS[g % 2]
                act.wait_ge(decay_summed, g + 1)
                act.activation(AL_, SIG, ACT.Exp, scale=-DECAY_C)
                act.activation(EX, CUM, ACT.Exp, scale=-DECAY_C)
                act.activation(KA_, CUM, ACT.Exp, scale=DECAY_C).then_inc(decays_ready, 1)

            rates(0)
            decays(0)
            for g in range(8):
                j = g % 4
                act.wait_ge(factors_turned, g + 1)
                for i in range(3):
                    ins = act.activation(TOK[:, i, :], pb[i][:, :], ACT.Copy)
                ins.then_inc(factors_by_token, 1)
                for li in range(len(BLOCK_LEVELS)):
                    for hb in range(2):
                        act.wait_ge(x_ready, NLEV * g + 2 * li + hb + 1)
                        act.activation(XS[hb], pb[hb][:, :], ACT.Copy).then_inc(x_copied, 1)
                    if g < 7 and li == 0:
                        rates(g + 1)
                    if g < 7 and li == 2:
                        decays(g + 1)
                act.wait_ge(t_updated, NLEV * (g + 1))
                for hb in range(2):
                    act.activation(tiles(TI[hb])[:, :, 0:HD], tiles(TOK[:, 0, :])[:, :, HD * hb:HD * hb + HD], ACT.Copy)
                act.wait_ge(kv_ready, g + 1)
                for hb in range(2):
                    ins = act.activation(tiles(TI[hb])[:, :, HD:P], tiles(pb[6 + hb][:, 0:TT * HD], HD), ACT.Copy)
                ins.then_inc(rhs_ready, 1)
                act.wait_ge(solved, g + 1)
                for hb in range(2):
                    ins = act.activation(NGH[hb], pb[hb][:, :], ACT.Copy, scale=-1.0)
                ins.then_inc(solved_copied, 1)
                act.wait_ge(group_ready, g + 1)
                for half in range(2):
                    f = FF[:, j, :].rearrange("p (t h v) -> p t h v", h=2, v=HD)[:, :, half, :]
                    ins = act.activation(f, tiles(pb[5 + 2 * half][:, 0:TT * HD], HD), ACT.Copy)
                ins.then_inc(inputs_copied, 1)

        def wkv_gpsimd(pool):
            wkv_factors(pool, 0)
            for g in range(8):
                pool.wait_ge(triangles_ready, g + 1)
                for li, b in enumerate(BLOCK_LEVELS):
                    mask = C("mu" if g < 4 else "ml", LEVELS.index(b) * P, P)
                    for hb in range(2):
                        if li:
                            pool.wait_ge(x_ready, NLEV * g + 2 * li + hb - 1)
                        pool.tensor_tensor(tiles(MB[hb]), tiles(MT[hb]), over(mask, TT), ALU.mult)\
                            .then_inc(level_masked, 1)
                if g < 7:
                    wkv_factors(pool, g + 1)

        def wkv_factors(pool, g):
            d, j = g // 4, g % 4
            AL_, BE_, KA_ = FACTORS[g % 2]
            if g == 0:
                pool.wait_ge(kk_ready, 1)
            pool.wait_ge(rates_ready, g + 1)
            pool.tensor_tensor(BE_, KK[:, j, :], AA, ALU.mult)
            pool.drain()
            pool.tensor_scalar(AA, AA, V("ka", j), omka[:, j:j + 1], ALU.mult, ALU.add)
            pool.drain()
            pool.tensor_tensor(AA, AA, BIG[:, K_ + j, :], ALU.mult)
            pool.drain()
            pool.wait_ge(decays_ready, g + 1)
            pool.tensor_tensor(AL_, AL_, KK[:, j, :], ALU.mult)
            pool.tensor_tensor(BE_, BE_, KA_, ALU.mult)
            pool.drain()
            pool.tensor_tensor(KA_, KA_, AA, ALU.mult)
            pool.tensor_copy(wstat[:, d, j, :], EX[:, (CHUNK - 1 if d == 0 else 0)::CHUNK])
            if g == 4:
                pool.wait_ge(state_ready, NCH)
            pool.tensor_tensor(RR[:, j, :], BIG[:, R_ + j, :], EX, ALU.mult).then_inc(factors_ready, 1)

        def wkv_vector(dve):
            wkv_decay_sums(dve, 0)
            for d in range(2):
                for j in range(4):
                    wkv_group_vector(dve, d, j, 4 * d + j)
                for s, c in enumerate(chunk_order(d)):
                    st = STATE[s % 2]
                    cc = slice(c * HD, (c + 1) * HD)
                    decay = along(wstat[:, d, :, c:c + 1].rearrange("p j o -> p (j o)"), HD)
                    if s == 0:
                        dve.wait_ge(inputs_copied, 4 * d + 4)
                        dve.tensor_tensor(st, FF[:, :, cc], decay, ALU.mult)
                    else:
                        dve.wait_ge(step_ready, (NCH - 1) * d + s)
                        for hb in range(2):
                            rows = slice(HD * hb, HD * hb + HD)
                            if s < NCH - 1:
                                dve.tensor_tensor(st[rows, :, :], FF[rows, :, cc], tiles(pb[2 + hb][rows, 0:4 * HD], HD),
                                                  ALU.add)
                            y = H[rows, 4:8, cc]
                            dve.tensor_tensor(y, y, tiles(pb[hb][rows, 0:4 * HD], HD), ALU.add)
                        if s < NCH - 1:
                            dve.drain()
                            dve.tensor_tensor(st, st, decay, ALU.mult)
                    dve.drain().then_inc(state_ready, 1)

        def wkv_decay_sums(dve, g):
            step = 1 if g < 4 else -1
            dve.wait_ge(rates_ready, g + 1)
            dve.tensor_tensor_scan(CUM[:, ::step], C("reset"), SIG[:, ::step], 0.0, ALU.mult, ALU.add)
            dve.drain()
            dve.tensor_tensor(SIG, CUM, SIG, ALU.subtract).then_inc(decay_summed, 1)

        def wkv_group_vector(dve, d, j, g):
            strict, incl = C("su" if d == 0 else "sl"), C("iu" if d == 0 else "il")
            one, one_t = (C("ml", 0, P), C("mu", 0, P)) if d == 0 else (C("mu", 0, P), C("ml", 0, P))
            dve.wait_ge(within_ready, g + 1)
            for hb in range(2):
                dve.tensor_tensor(tiles(MT[hb]), tiles(pb[4 + hb][:, :]), over(strict, TT), ALU.mult)
                dve.tensor_tensor(tiles(TI[hb]), tiles(pb[6 + hb][:, :]), over(one, TT), ALU.mult)
            dve.drain().then_inc(triangles_ready, 1)
            for hb in range(2):
                dve.tensor_tensor(tiles(TTI[hb]), tiles(MT[hb]), over(one_t, TT), ALU.mult)
            dve.drain()
            for hb in range(2):
                for x in (TI[hb], TTI[hb]):
                    dve.tensor_tensor(tiles(x), over(C("ident"), TT), tiles(x), ALU.subtract)
            dve.drain().then_inc(t_started, 1)
            for li in range(len(BLOCK_LEVELS)):
                for hb in range(2):
                    dve.wait_ge(z_ready, NLEV * g + 2 * li + hb + 1)
                    dve.tensor_tensor(TI[hb], TI[hb], pb[2 + hb][:, :], ALU.subtract)
                    dve.tensor_tensor(TTI[hb], TTI[hb], pb[4 + hb][:, :], ALU.subtract).then_inc(t_updated, 1)
                if g < 7 and li == 1:
                    wkv_decay_sums(dve, g + 1)
            dve.wait_ge(mixes_ready, g + 1)
            for hb in range(2):
                dve.tensor_tensor(tiles(MB[hb]), tiles(pb[hb][:, :]), over(strict, TT), ALU.mult)
                dve.tensor_tensor(tiles(XS[hb]), tiles(pb[2 + hb][:, :]), over(incl, TT), ALU.mult)
                ins = dve.tensor_tensor(tiles(MT[hb]), tiles(pb[4 + hb][:, :]), over(incl, TT), ALU.mult)
            ins.then_inc(mixes_masked, 1)
            dve.wait_ge(group_ready, g + 1)
            dve.tensor_tensor(RR[:, j, :], RR[:, j, :], pb[2][:, :], ALU.add)
            if d == 0:
                dve.tensor_copy(H[:, 4 + j, :], pb[3][:, :])
            else:
                dve.tensor_tensor(H[:, 4 + j, :], H[:, 4 + j, :], pb[3][:, :], ALU.add)
            for half in range(2):
                e = EIT[:, j, :].rearrange("p (t h k) -> p t h k", h=2, k=HD)[:, :, half, :]
                ins = dve.tensor_tensor(e, tiles(pb[4 + 2 * half][:, 0:TT * HD], HD), over(C("ident64"), TT), ALU.add)
            ins.then_inc(group_added, 1)

        y_summed, y_centred, y_squared = sem("output_summed"), sem("output_centred"), sem("output_squared")
        var_summed, y_rooted = sem("output_squares_summed"), sem("output_deviation_ready")
        bonus_summed, out_gate_ready = sem("bonus_summed"), sem("output_gate_ready")

        def wkv_readout_tensor(pe):
            pe.wait_ge(state_ready, 2 * NCH)
            for j in range(4):
                pe.matmul(pb[j][:, :], C("blk"), H[:, 4 + j, :], start=True, stop=True).then_inc(y_summed, 1)
            for j in range(4):
                mm = pe.matmul(pb[4 + j][:, :], S("g2", 0, P, j * P, P), BIG[:, GL, :], start=True, stop=True)
            mm.then_inc(out_gate_ready, 1)
            for j in range(4):
                pe.wait_ge(y_squared, j + 1)
                pe.matmul(pb[j][:, :], C("blk"), WORK[:, j, :], start=True, stop=True).then_inc(var_summed, 1)
            for j in range(4):
                pe.wait_ge(y_rooted, j + 1)
                pe.matmul(pb[j][:, :], C("blk"), WORK[:, 4 + j, :], start=True, stop=True).then_inc(bonus_summed, 1)

        def wkv_readout_scalar(act):
            for j in range(4):
                act.wait_ge(y_centred, j + 1)
                act.activation(WORK[:, j, :], H[:, 4 + j, :], ACT.Square).then_inc(y_squared, 1)
            for j in range(4):
                act.wait_ge(var_summed, j + 1)
                act.activation(WORK[:, j, :], pb[j][:, :], ACT.Sqrt, bias=epsb[:, 2:3], scale=1.0 / HD)\
                   .then_inc(y_rooted, 1)

        def wkv_readout_vector(dve):
            for j in range(4):
                dve.scalar_tensor_tensor(out=WORK[:, 4 + j, :], in0=BIG[:, R_ + j, :], scalar=V("rk", j),
                                         in1=BIG[:, K_ + j, :], op0=ALU.mult, op1=ALU.mult)
                dve.wait_ge(y_summed, j + 1)
                dve.scalar_tensor_tensor(out=H[:, 4 + j, :], in0=pb[j][:, :], scalar=-1.0 / HD, in1=H[:, 4 + j, :],
                                         op0=ALU.mult, op1=ALU.add).then_inc(y_centred, 1)
            for j in range(4):
                dve.wait_ge(y_rooted, j + 1)
                dve.reciprocal(WORK[:, j, :], WORK[:, j, :])
            dve.drain()
            for j in range(4):
                dve.scalar_tensor_tensor(out=H[:, 4 + j, :], in0=H[:, 4 + j, :], scalar=V("gnw", j), in1=WORK[:, j, :],
                                         op0=ALU.mult, op1=ALU.mult)
            dve.drain()
            for j in range(4):
                dve.wait_ge(bonus_summed, j + 1)
                dve.tensor_tensor(WORK[:, j, :], BIG[:, V_ + j, :], pb[j][:, :], ALU.mult)
            dve.drain()
            for j in range(4):
                dve.scalar_tensor_tensor(out=H[:, 4 + j, :], in0=H[:, 4 + j, :], scalar=V("gnb", j), in1=WORK[:, j, :],
                                         op0=ALU.add, op1=ALU.add)
            dve.drain()
            dve.wait_ge(out_gate_ready, 1)
            for j in range(4):
                dve.tensor_tensor(H[:, 4 + j, :], H[:, 4 + j, :], pb[4 + j][:, :], ALU.mult)
            dve.drain().then_inc(mixer_ready, 1)

        MVTOK = WORK[:, 0:4, :]
        ROWS = 64
        IGR, LFR, BCR, MMR, AR, RBR = (WORK[0:ROWS, 4 + i, :] for i in range(6))
        ACOL = WORK[:, 10, 0:TT * ROWS].rearrange("p (t r) -> p t r", r=ROWS)
        TMP1, LOGS, RD = WORK[0:ROWS, 11, :], WORK[0:ROWS, 12, :], WORK[:, 13, :]
        WGT = [WORK[:, 14:18, :], WORK[:, 22:26, :]]
        DEN, EM = [WORK[:, 18, :], WORK[:, 19, :]], [WORK[:, 26, :], WORK[:, 27, :]]
        SELROW = WORK[0:ROWS, 20:22, :].rearrange("p a (b c) -> p (a b) c", c=P)
        conv_ready, conv_silu = sem("convolution_ready"), sem("convolution_silu")
        mv_turned, mv_ready = sem("mlstm_values_transposed"), sem("mlstm_values_by_token_ready")
        gates_summed, gates_biased, gates_logged = sem("mlstm_gates_gathered"), sem("mlstm_gates_biased"), sem("mlstm_gates_logged")
        stabilised = sem("mlstm_stabiliser_ready")
        acol_turned, acol_ready = sem("mlstm_key_terms_transposed"), sem("mlstm_key_terms_ready")
        rows_spread, qk_ready = sem("mlstm_query_terms_spread"), sem("mlstm_scores_ready")
        rd_ready, exps_ready = sem("mlstm_diagonal_masked"), sem("mlstm_weights_exponential")
        weights_ready, sums_ready = sem("mlstm_weights_ready"), sem("mlstm_sums_ready")
        den_ready, unit_done = sem("mlstm_denominator_ready"), sem("mlstm_unit_done")

        def place_of(d, tile):
            return tile if d == 0 else (1, 0, 3, 2)[tile]

        def later_runs(d, si):
            later = [t for t in range(TT) if place_of(d, t) > place_of(d, si)]
            runs = []
            for t in later:
                if runs and runs[-1][1] == t:
                    runs[-1][1] = t + 1
                else:
                    runs.append([t, t + 1])
            return runs

        UNITS = [(d, h) for h in range(4) for d in range(2)]

        def mlstm_vector(dve):
            all_copied(dve, 2, 0)
            for i in range(8):
                dve.tensor_scalar(WORK[:, 20 + i, :], BIG[:, 5 + i, :], V("cw", 8 + i), V("cb", i), ALU.mult, ALU.add)
            dve.drain()
            add_neighbours(dve, [(BIG[:, 5 + i, :], WORK[:, 20 + i, :], V("cw", i), V("cw", 16 + i)) for i in range(8)])
            dve.drain().then_inc(conv_ready, 1)
            dve.wait_ge(gates_biased, 1)
            dve.tensor_scalar(LFR, pb[5][0:ROWS, :], vec[0:ROWS, VO["bf"][0]:VO["bf"][0] + 1], 0.0, ALU.add, ALU.min)
            dve.wait_ge(gates_logged, 1)
            dve.drain()
            dve.tensor_tensor(LFR, LFR, LOGS, ALU.subtract)
            dve.memset(RD[0:ROWS, :], 1.0)
            dve.drain()
            ones = RD[0:32, :]
            lf, ig, bc, mm = (x[0:32, :] for x in (LFR, IGR, BCR, MMR))
            dve.tensor_tensor_scan(bc, ones, lf, 0.0, ALU.mult, ALU.add)
            dve.tensor_tensor_scan(mm, lf, ig, 0.0, ALU.add, ALU.max)
            ones = RD[32:64, 0:TC]
            c, l = ([x[32:64, a:b] for x in (LFR, IGR, BCR, MMR)] for a, b in (CTX, LAT))
            dve.tensor_tensor_scan(c[2][:, ::-1], ones, c[0][:, ::-1], 0.0, ALU.mult, ALU.add)
            dve.tensor_tensor_scan(c[3][:, ::-1], c[0][:, ::-1], c[1][:, ::-1], 0.0, ALU.add, ALU.max)
            dve.drain()
            dve.tensor_tensor_scan(l[2][:, ::-1], ones, l[0][:, ::-1], c[2][:, 0:1], ALU.mult, ALU.add)
            dve.tensor_tensor_scan(l[3][:, ::-1], l[0][:, ::-1], l[1][:, ::-1], c[3][:, 0:1], ALU.add, ALU.max)
            dve.drain()
            dve.tensor_tensor(AR, IGR, BCR, ALU.subtract)
            dve.tensor_tensor(RBR, BCR, MMR, ALU.subtract)
            dve.wait_ge(conv_silu, 8)
            for d in range(2):
                dve.tensor_copy(SELROW[:, 4 * d:4 * d + 4, :], along(C("ident", 32 * d, 4)[0:ROWS, :], P))
            dve.drain().then_inc(stabilised, 1)
            for u in range(len(UNITS) + 1):
                if u < len(UNITS):
                    d, h = UNITS[u]
                    dve.wait_ge(rows_spread, u + 1)
                    dve.tensor_tensor(tiles(RD), tiles(pb[0][:, :]), over(C("nu" if d == 0 else "nl"), TT), ALU.add)\
                       .then_inc(rd_ready, 1)
                    dve.wait_ge(exps_ready, u + 1)
                    dve.wait_ge(qk_ready, u + 1)
                    for si in range(TT):
                        for a, b in [[si, si + 1]] + later_runs(d, si):
                            w = WGT[u % 2][:, si, a * P:b * P]
                            ins = dve.scalar_tensor_tensor(out=w, in0=pb[2 + si][:, a * P:b * P], scalar=P ** -0.5, in1=w,
                                                           op0=ALU.mult, op1=ALU.mult)
                    ins.then_inc(weights_ready, 1)
                if u:
                    d, h = UNITS[u - 1]
                    den = DEN[(u - 1) % 2]
                    dve.wait_ge(den_ready, u)
                    dve.tensor_tensor(den, den, EM[(u - 1) % 2], ALU.max)
                    dve.drain()
                    dve.reciprocal(den, den)
                    dve.drain()
                    if d == 0:
                        dve.tensor_tensor(H[:, 4 + h, :], den, pb[6][:, :], ALU.mult).then_inc(unit_done, 1)
                    else:
                        dve.tensor_tensor(den, den, pb[6][:, :], ALU.mult)
                        dve.drain()
                        dve.tensor_tensor(H[:, 4 + h, :], H[:, 4 + h, :], den, ALU.add).then_inc(unit_done, 1)

        def mlstm_scalar(act):
            act.wait_ge(conv_ready, 1)
            for i in range(8):
                act.activation(BIG[:, 5 + i, :], WORK[:, 20 + i, :], ACT.Silu).then_inc(conv_silu, 1)
            act.wait_ge(gates_summed, 1)
            act.activation(IGR, pb[4][0:ROWS, :], ACT.Identity, bias=vec[0:ROWS, VO["bi"][0]:VO["bi"][0] + 1])
            act.activation(TMP1, pb[5][0:ROWS, :], ACT.Abs, bias=vec[0:ROWS, VO["bf"][0]:VO["bf"][0] + 1])\
               .then_inc(gates_biased, 1)
            act.drain()
            act.activation(TMP1, TMP1, ACT.Exp, scale=-1.0)
            act.drain()
            act.activation(LOGS, TMP1, ACT.Ln, bias=1.0).then_inc(gates_logged, 1)
            act.wait_ge(mv_turned, 1)
            for tt in range(TT):
                ins = act.activation(MVTOK[:, tt, :], pb[tt][:, :], ACT.Copy)
            ins.then_inc(mv_ready, 1)
            act.wait_ge(acol_turned, 1)
            act.activation(ACOL, tiles(pb[0][:, 0:TT * ROWS], ROWS), ACT.Copy).then_inc(acol_ready, 1)
            act.drain()
            for u in range(len(UNITS) + 1):
                if u < len(UNITS):
                    d, h = UNITS[u]
                    row = 32 * d + h
                    act.wait_ge(rows_spread, u + 1)
                    if u >= 2:
                        act.wait_ge(unit_done, u - 1)
                    act.activation(EM[u % 2], pb[1][:, :], ACT.Exp, scale=-1.0)
                    act.wait_ge(rd_ready, u + 1)
                    for si in range(TT):
                        s = slice(si * P, (si + 1) * P)
                        ins = act.activation(WGT[u % 2][:, si, s], RD[:, s], ACT.Exp, bias=ACOL[:, si, row:row + 1])
                        for a, b in later_runs(d, si):
                            ins = act.activation(WGT[u % 2][:, si, a * P:b * P], pb[0][:, a * P:b * P], ACT.Exp,
                                                 bias=ACOL[:, si, row:row + 1])
                    ins.then_inc(exps_ready, 1)
                if u:
                    act.wait_ge(sums_ready, u)
                    act.activation(DEN[(u - 1) % 2], pb[7][:, :], ACT.Abs).then_inc(den_ready, 1)

        def mlstm_tensor(pe):
            pe.wait_ge(conv_ready, 1)
            pe.matmul(pb[4][0:ROWS, :], C("sel_i"), BIG[:, 29, :], start=True, stop=True)
            pe.matmul(pb[5][0:ROWS, :], C("sel_f"), BIG[:, 29, :], start=True, stop=True).then_inc(gates_summed, 1)
            turn_values(pe, BIG[:, 13:17, :], 4, 0).then_inc(mv_turned, 1)
            pe.wait_ge(mv_ready, 1)
            pe.wait_ge(stabilised, 1)
            for tt in range(TT):
                mm = pe.transpose(pb[0][:, tt * ROWS:(tt + 1) * ROWS], AR[:, tt * P:(tt + 1) * P],
                                  C("ident")[0:ROWS, 0:ROWS])
            mm.then_inc(acol_turned, 1)
            pe.wait_ge(acol_ready, 1)
            pe.wait_ge(conv_silu, 8)
            for u in range(len(UNITS) + 1):
                if u < len(UNITS):
                    d, h = UNITS[u]
                    if u:
                        pe.wait_ge(weights_ready, u)
                    sel = SELROW[:, 4 * d + h, :]
                    pe.matmul(pb[0][:, :], sel, RBR, start=True, stop=True)
                    pe.matmul(pb[1][:, :], sel, MMR, start=True, stop=True).then_inc(rows_spread, 1)
                    for si in range(TT):
                        for a, b in [[si, si + 1]] + later_runs(d, si):
                            mm = pe.matmul(pb[2 + si][:, a * P:b * P], BIG[:, 9 + h, si * P:(si + 1) * P],
                                           BIG[:, 5 + h, a * P:b * P], start=True, stop=True)
                    mm.then_inc(qk_ready, 1)
                if u:
                    d, h = UNITS[u - 1]
                    pe.wait_ge(weights_ready, u)
                    if u >= 2:
                        pe.wait_ge(unit_done, u - 1)
                    for t in range(TT):
                        earlier = [s for s in range(TT) if place_of(d, s) <= place_of(d, t)]
                        for bank in (6, 7):
                            for s in earlier:
                                mm = pe.matmul(pb[bank][:, t * P:(t + 1) * P],
                                               MVTOK[:, s, h * P:(h + 1) * P] if bank == 6 else C("ones"),
                                               WGT[(u - 1) % 2][:, s, t * P:(t + 1) * P], start=s == earlier[0],
                                               stop=s == earlier[-1])
                    mm.then_inc(sums_ready, 1)

        READOUTS = [(4, 17, 21, ALL, "mn"), (0, None, 20, LAT, "gln")]
        gates_ready, out_gated = sem("readout_gates_ready"), sem("readout_heads_gated")
        out_squared, out_summed, out_rooted = (sem(f"readout_{x}") for x in ("squared", "summed", "rms_ready"))

        def readout_scalar(act, k):
            h0, o0, z0, (a, b), _ = READOUTS[k]
            if o0 is not None:
                for h in range(4):
                    act.activation(BIG[:, o0 + h, a:b], BIG[:, o0 + h, a:b], ACT.Sigmoid)
            for i in range(KT):
                ins = act.activation(BIG[:, z0 + i, a:b], BIG[:, z0 + i, a:b], ACT.Silu)
            ins.then_inc(gates_ready, 1)
            act.wait_ge(out_gated, k + 1)
            for h in range(4):
                act.activation(WORK[:, h, a:b], H[:, h0 + h, a:b], ACT.Square).then_inc(out_squared, 1)
            for h in range(4):
                act.wait_ge(out_summed, 4 * k + h + 1)
                act.activation(WORK[:, h, a:b], pb[h][:, a:b], ACT.Sqrt, bias=epsb[:, 0:1], scale=1.0 / P)\
                   .then_inc(out_rooted, 1)

        def readout_tensor(pe, k):
            a, b = READOUTS[k][3]
            for h in range(4):
                pe.wait_ge(out_squared, 4 * k + h + 1)
                pe.matmul(pb[h][:, a:b], C("ones"), WORK[:, h, a:b], start=True, stop=True).then_inc(out_summed, 1)

        def readout_vector(dve, k):
            h0, o0, z0, (a, b), gain = READOUTS[k]
            dve.wait_ge(gates_ready, k + 1)
            dve.drain()
            if o0 is not None:
                for h in range(4):
                    dve.tensor_tensor(H[:, h0 + h, a:b], H[:, h0 + h, a:b], BIG[:, o0 + h, a:b], ALU.mult)
            dve.drain().then_inc(out_gated, 1)
            for h in range(4):
                dve.wait_ge(out_rooted, 4 * k + h + 1)
                dve.reciprocal(WORK[:, h, a:b], WORK[:, h, a:b])
            dve.drain()
            for h in range(4):
                dve.scalar_tensor_tensor(out=H[:, h0 + h, a:b], in0=H[:, h0 + h, a:b], scalar=V(gain, h),
                                         in1=WORK[:, h, a:b], op0=ALU.mult, op1=ALU.mult)
            dve.drain()
            for i in range(KT):
                dve.tensor_tensor(H[:, i, a:b], H[:, i, a:b], BIG[:, z0 + i, a:b], ALU.mult)
            dve.drain().then_inc(mixer_ready, 1)

        GVTOK = WORK[:, 0:4, :]
        LGT, BSUM, TMP2, ONES_ROW = WORK[:, 4, :], WORK[:, 5, :], WORK[:, 6, :], WORK[:, 7, :]
        QC2 = [WORK[:, 8, :], WORK[:, 20, :]]
        QL2 = [WORK[:, a:a + 4, :].rearrange("p a (b t) -> p (a b) t", t=TC) for a in (9, 21)]
        PART = WORK[:, 13:17, :]
        NEAR2, FAR2 = [WORK[:, a, 0:TC] for a in (17, 26)], [WORK[:, a, TC:TC + P] for a in (17, 26)]
        CTXA2 = [WORK[:, a, :] for a in (18, 25)]
        GLA_LEVELS = LEVELS + (P,)
        gv_turned, gv_ready = sem("gla_values_transposed"), sem("gla_values_by_token_ready")
        forget_ready, forget_logged = sem("gla_gate_product"), sem("gla_gate_logged")
        spans_ready, spans_exp, spans_used = sem("gla_log_decays_ready"), sem("gla_decays_ready"), sem("gla_factors_ready")
        pairs_ready, pairs_read, far_summed = sem("gla_scores_ready"), sem("gla_scores_masked"), sem("gla_far_scores_ready")
        near_ready, far_ready = sem("gla_near_scores_masked"), sem("gla_far_scores_copied")
        gla_mixed, gla_added = sem("gla_values_mixed"), sem("gla_output_added")

        def halves(ap, b):
            return ap.rearrange("p (n h b) -> p n h b", h=2, b=b)

        def gla_tensor(pe):
            pe.wait_ge(mixed_copied, units_before(4))
            turn_values(pe, BIG[:, 4:8, :], 4, 0).then_inc(gv_turned, 1)
            pe.wait_ge(gv_ready, 1)

            def forget(g):
                low = slice(32 * (g // 2), 32 * (g // 2) + 16)
                pe.matmul(pb[7][:, :], S("wg", low.start, low.stop, g % 2 * P, P), BIG[low, 28, :], start=True, stop=True)\
                  .then_inc(forget_ready, 1)

            def pairs(u):
                g, hb = u // 2, u % 2
                d, j, rows = g // 2, g % 2, slice(HD * hb, HD * hb + HD)
                QC, QL = QC2[g % 2], QL2[g % 2]
                if hb == 0:
                    pe.wait_ge(spans_used, g + 1)
                    if g < 3:
                        forget(g + 1)
                for li in range(len(LEVELS) + 1):
                    if u and li % 2 == 0:
                        pe.wait_ge(pairs_read, 4 * (u - 1) + li // 2 + 1)
                    for i in range(2):
                        o = (li % 2) * TC + i * P
                        k = q = QL[rows, min(li, len(LEVELS) - 1), i * P:(i + 1) * P]
                        if li == len(LEVELS):
                            k, q = (BIG[rows, t + j, TC + i * P:TC + (i + 1) * P] for t in (2, 0))
                        mm = pe.matmul(pb[li // 2][:, o:o + P], k, q, start=True, stop=True)
                    if li % 2:
                        mm.then_inc(pairs_ready, 1)
                if u:
                    pe.wait_ge(far_ready, u)
                e, l = (slice(x * P, (x + 1) * P) for x in ((0, 1) if d == 0 else (1, 0)))
                pe.matmul(pb[4][:, 0:P], QL[rows, 7, e], QL[rows, 7, l], start=True, stop=True)
                for s in range(2):
                    mm = pe.matmul(pb[5][:, s * TC:(s + 1) * TC], QC[rows, s * P:(s + 1) * P], QC[rows, TC:T],
                                   start=True, stop=True)
                mm.then_inc(far_summed, 1)

            forget(0)
            pairs(0)
            for u in range(8):
                early, late = (2, 3) if u < 4 else (3, 2)
                h = u % 4
                hc, NEAR, FAR, CTXA = slice(h * P, (h + 1) * P), NEAR2[u % 2], FAR2[u % 2], CTXA2[u % 2]
                if u < 7:
                    pairs(u + 1)
                pe.wait_ge(near_ready, u + 1)
                pe.wait_ge(far_ready, u + 1)
                if u:
                    pe.wait_ge(gla_added, u)
                for t in (2, 3):
                    terms = [(2 + (t - 2), NEAR[:, (t - 2) * P:(t - 1) * P])]
                    terms += [(early, FAR)] if t == late else []
                    terms += [(s, CTXA[:, s * TC + (t - 2) * P:s * TC + (t - 1) * P]) for s in range(2)]
                    for i, (s, a) in enumerate(terms):
                        mm = pe.matmul(pb[6][:, (t - 2) * P:(t - 1) * P], GVTOK[:, s, hc], a, start=i == 0,
                                       stop=i == len(terms) - 1)
                mm.then_inc(gla_mixed, 1)

        def gla_scalar(act):
            act.wait_ge(gv_turned, 1)
            for tt in range(TT):
                ins = act.activation(GVTOK[:, tt, :], pb[tt][:, :], ACT.Copy)
            ins.then_inc(gv_ready, 1)

            def log_gate(g):
                act.wait_ge(forget_ready, g + 1)
                if g:
                    act.wait_ge(spans_ready, g)
                act.activation(TMP2, pb[7][:, :], ACT.Abs, bias=V("bg", g))
                act.drain()
                act.activation(TMP2, TMP2, ACT.Exp, scale=-1.0)
                act.drain()
                act.activation(TMP2, TMP2, ACT.Ln, bias=1.0).then_inc(forget_logged, 1)

            def decays(g):
                act.wait_ge(spans_ready, g + 1)
                act.activation(QC2[g % 2], QC2[g % 2], ACT.Exp, scale=1.0 / 16)
                act.activation(QL2[g % 2], QL2[g % 2], ACT.Exp, scale=1.0 / 16).then_inc(spans_exp, 1)

            def far(u):
                act.wait_ge(far_summed, u + 1)
                act.activation(CTXA2[u % 2], pb[5][:, :], ACT.Copy)
                act.activation(FAR2[u % 2], pb[4][:, 0:P], ACT.Copy).then_inc(far_ready, 1)

            log_gate(0)
            decays(0)
            for g in range(4):
                far(2 * g)
                if g < 3:
                    log_gate(g + 1)
                    decays(g + 1)
                far(2 * g + 1)

        def gla_vector(dve):
            dve.memset(ONES_ROW, 1.0)

            def log_spans(g):
                d, j = g // 2, g % 2
                hk, hq = (0, 1) if d == 0 else (1, 0)
                QC, QL = QC2[g % 2], QL2[g % 2]
                dve.wait_ge(forget_logged, g + 1)
                dve.tensor_scalar(LGT, pb[7][:, :], V("bg", g), 0.0, ALU.add, ALU.min)
                dve.drain()
                dve.tensor_tensor(LGT, LGT, TMP2, ALU.subtract)
                dve.drain()
                if d == 0:
                    dve.tensor_tensor_scan(BSUM, ONES_ROW, LGT, 0.0, ALU.mult, ALU.add)
                else:
                    dve.tensor_tensor_scan(BSUM[:, 0:TC][:, ::-1], ONES_ROW[:, 0:TC], LGT[:, 0:TC][:, ::-1], 0.0,
                                           ALU.mult, ALU.add)
                    dve.drain()
                    dve.tensor_tensor_scan(BSUM[:, TC:T][:, ::-1], ONES_ROW[:, 0:TC], LGT[:, TC:T][:, ::-1],
                                           BSUM[:, 0:1], ALU.mult, ALU.add)
                dve.drain()
                ref = BSUM[:, TC - 1:TC] if d == 0 else BSUM[:, 0:1]
                dve.tensor_scalar(QC[:, 0:TC], BSUM[:, 0:TC], -1.0, ref, ALU.mult, ALU.add)
                dve.tensor_scalar(QC[:, TC:T], BSUM[:, TC:T], ref, None, ALU.subtract)
                for li, b in enumerate(GLA_LEVELS):
                    src, dst = halves(BSUM[:, TC:T], b), halves(QL[:, li, :], b)
                    r = b - 1 if d == 0 else 0
                    refs = src[:, :, hk, r:r + 1].to_broadcast([P, TC // (2 * b), b])
                    dve.tensor_tensor(dst[:, :, hq, :], src[:, :, hq, :], refs, ALU.subtract)
                    dve.tensor_tensor(dst[:, :, hk, :], refs, src[:, :, hk, :], ALU.subtract)
                dve.drain().then_inc(spans_ready, 1)

            def factors(g):
                d, j = g // 2, g % 2
                hk, hq = (0, 1) if d == 0 else (1, 0)
                QC, QL = QC2[g % 2], QL2[g % 2]
                dve.wait_ge(spans_exp, g + 1)
                dve.tensor_tensor(QC[:, 0:TC], QC[:, 0:TC], BIG[:, 2 + j, 0:TC], ALU.mult)
                dve.tensor_tensor(QC[:, TC:T], QC[:, TC:T], BIG[:, j, TC:T], ALU.mult)
                for li, b in enumerate(GLA_LEVELS):
                    dst = halves(QL[:, li, :], b)
                    for half, src in ((hq, BIG[:, j, TC:T]), (hk, BIG[:, 2 + j, TC:T])):
                        dve.tensor_tensor(dst[:, :, half, :], dst[:, :, half, :], halves(src, b)[:, :, half, :], ALU.mult)
                dve.drain().then_inc(spans_used, 1)

            def near(u):
                mask = lambda li: C("mu" if u < 4 else "ml", li * P, P)
                dve.drain()
                for li in range(len(LEVELS) + 1):
                    if li % 2 == 0:
                        dve.wait_ge(pairs_ready, 4 * u + li // 2 + 1)
                    m = mask(li) if li < len(LEVELS) else C("ident")
                    o = (li % 2) * TC
                    ins = dve.tensor_tensor(tiles(PART[:, li // 2, o:o + TC]), tiles(pb[li // 2][:, o:o + TC]), over(m, 2),
                                            ALU.mult)
                    if li % 2:
                        ins.then_inc(pairs_read, 1)
                dve.drain()
                dve.tensor_tensor(PART[:, 0, :], PART[:, 0, :], PART[:, 1, :], ALU.add)
                dve.tensor_tensor(PART[:, 2, :], PART[:, 2, :], PART[:, 3, :], ALU.add)
                dve.drain()
                dve.tensor_tensor(PART[:, 0, :], PART[:, 0, :], PART[:, 2, :], ALU.add)
                dve.drain()
                dve.tensor_tensor(NEAR2[u % 2], PART[:, 0, 0:TC], PART[:, 0, TC:T], ALU.add).then_inc(near_ready, 1)

            def add_output(u):
                y = H[:, u % 4, TC:T]
                dve.wait_ge(gla_mixed, u + 1)
                if u < 4:
                    dve.tensor_copy(y, pb[6][:, 0:TC]).then_inc(gla_added, 1)
                else:
                    dve.tensor_tensor(y, y, pb[6][:, 0:TC], ALU.add).then_inc(gla_added, 1)

            log_spans(0)
            factors(0)
            for u in range(8):
                near(u)
                if u < 6:
                    (factors if u % 2 else log_spans)(u // 2 + 1)
                if u:
                    add_output(u - 1)
            add_output(7)

        block = ctx.enter_context(nc.Block())

        @block.tensor
        def _(pe):
            pe.wait_ge(loaded, 16 * 4)
            mods_tensor(pe)
            norm_tensor(pe, 0)
            ffn_tensor(pe, 0)
            norm_tensor(pe, 1)
            linear_tensor(pe, 0)
            even_heads_tensor(pe)
            attend_tensor(pe, 0)
            wkv_features_tensor(pe)
            wkv_tensor(pe)
            wkv_readout_tensor(pe)
            residual_tensor(pe, 0)
            norm_tensor(pe, 2)
            ffn_tensor(pe, 1)
            norm_tensor(pe, 3)
            ffn_tensor(pe, 2)
            norm_tensor(pe, 4)
            linear_tensor(pe, 1)
            odd_heads_tensor(pe)
            attend_tensor(pe, 1)
            residual_tensor(pe, 1)
            norm_tensor(pe, 5)
            ffn_tensor(pe, 3)
            gain_norm_tensor(pe, 0)
            norm_tensor(pe, 6)
            linear_tensor(pe, 2)
            mla_heads_tensor(pe)
            attend_tensor(pe, 2)
            mlstm_tensor(pe)
            readout_tensor(pe, 0)
            residual_tensor(pe, 2)
            norm_tensor(pe, 7)
            linear_tensor(pe, 3)
            na_heads_tensor(pe)
            attend_tensor(pe, 3)
            gla_tensor(pe)
            readout_tensor(pe, 1)
            residual_tensor(pe, 3)
            gain_norm_tensor(pe, 1)

        @block.vector
        def _(dve):
            setup_vector(dve)
            mods_vector(dve, 0, MOD_BATCHES[0][1])
            norm_vector(dve, 0)
            ffn_vector(dve, 0)
            norm_vector(dve, 1)
            linear_vector(dve, 0)
            even_heads_vector(dve)
            attend_vector(dve, 0)
            wkv_features_vector(dve)
            wkv_vector(dve)
            wkv_readout_vector(dve)
            residual_vector(dve, 0)
            norm_vector(dve, 2)
            ffn_vector(dve, 1)
            norm_vector(dve, 3)
            ffn_vector(dve, 2)
            norm_vector(dve, 4)
            linear_vector(dve, 1)
            odd_heads_vector(dve)
            attend_vector(dve, 1)
            residual_vector(dve, 1)
            norm_vector(dve, 5)
            ffn_vector(dve, 3)
            gain_norm_vector(dve, 0)
            norm_vector(dve, 6)
            linear_vector(dve, 2)
            mla_heads_vector(dve)
            attend_vector(dve, 2)
            mlstm_vector(dve)
            readout_vector(dve, 0)
            residual_vector(dve, 2)
            norm_vector(dve, 7)
            linear_vector(dve, 3)
            attend_vector(dve, 3)
            gla_vector(dve)
            readout_vector(dve, 1)
            residual_vector(dve, 3)
            gain_norm_vector(dve, 1)

        @block.scalar
        def _(act):
            setup_scalar(act)
            mods_scalar(act)
            norm_scalar(act, 0)
            ffn_scalar(act, 0)
            norm_scalar(act, 1, ffn_added, 4 + 1)
            linear_scalar(act, 0)
            even_heads_scalar(act)
            attend_scalar(act, 0)
            wkv_features_scalar(act)
            wkv_scalar(act)
            wkv_readout_scalar(act)
            norm_scalar(act, 2, mixer_added, 4 + 1)
            ffn_scalar(act, 1)
            norm_scalar(act, 3, ffn_added, 4 + KT + 1)
            ffn_scalar(act, 2)
            norm_scalar(act, 4, ffn_added, 4 + 2 * KT + 1)
            linear_scalar(act, 1)
            odd_heads_scalar(act)
            attend_scalar(act, 1)
            norm_scalar(act, 5, mixer_added, 4 + KT + 1)
            ffn_scalar(act, 3)
            gain_norm_scalar(act, 0, ffn_added, 4 + 3 * KT + 1)
            act.wait_ge(ctx2_loaded, 16)
            norm_scalar(act, 6, scaled, GAIN_NORMS[0][2] * KT + 1)
            linear_scalar(act, 2)
            mla_heads_scalar(act)
            attend_scalar(act, 2)
            mlstm_scalar(act)
            readout_scalar(act, 0)
            norm_scalar(act, 7, mixer_added, 4 + 2 * KT + 1)
            linear_scalar(act, 3)
            na_heads_scalar(act)
            attend_scalar(act, 3)
            gla_scalar(act)
            readout_scalar(act, 1)
            gain_norm_scalar(act, 1, mixer_added, 4 + 3 * KT + 1)

        @block.gpsimd
        def _(pool):
            wkv_gpsimd(pool)
            pool.wait_ge(scaled, 5 * KT)
            pool.dma_start(X[:, :, 0:TC], ctx2).then_inc(ctx2_loaded, 16)
            na_heads_gpsimd(pool)

        @block.sync
        def _(sp):
            sp.dma_start(vec[:, :], vecs).then_inc(loaded, 16)
            sp.dma_start(X[:, :, :], xin).then_inc(loaded, 16)
            sp.dma_start(cst[:, :], consts).then_inc(loaded, 16)
            sp.dma_start(smallw[:, :], small).then_inc(loaded, 16)

            def load(n, src, i=None, per=0):
                free = n - RING + 1
                if i is not None:
                    sp.wait_ge(slab_done, i * per + free)
                elif free > 0:
                    sp.wait_ge(slab_done, free)
                sp.dma_start(ring[:, n % RING, 0:src.shape[-1]], src).then_inc(slot_full[n % RING], 16)

            n = row = 0
            run = 0
            for stage, count in SLABS + [("ffn_out", 0)]:
                if not stage.startswith("ffn_out"):
                    run += count
                    continue
                first = RING if n == 0 else 0
                for k in range(first):
                    load(k, stream_k[k])
                turns = (run - first) // RING
                with sp.Fori(0, turns) as i:
                    for k in range(first, first + RING):
                        load(n + k, stream_k[bass.ds(i * RING + (row + k), 1), :, :].rearrange("o p c -> (o p) c"), i, RING)
                for k in range(first + turns * RING, run):
                    load(n + k, stream_k[row + k])
                n, row, run = n + run, row + run, 0
                if count:
                    f = int(stage[-1])
                    with sp.Fori(0, KT // 4) as i:
                        for k in range(4):
                            t = 0
                            for part, q in enumerate(OUT_PARTS):
                                w = stream_f[bass.ds(i * 4 + (f * KT + k), 1), :, t * P:(t + q) * P]
                                load(n + len(OUT_PARTS) * k + part, w.rearrange("o p c -> (o p) c"), i, 4 * len(OUT_PARTS))
                                t += q
                    n += count
            sp.wait_ge(scaled, 10 * KT)
            sp.dma_start(out, X[:, :, TC:T]).then_inc(stored, 16)
            sp.wait_ge(stored, 16)


def shape_constants():
    p, f = np.arange(P)[:, None], np.arange(P)[None, :]
    c = {"ident": p == f, "ones": np.ones((P, P)), "blk": p // HD == f // HD, "ident64": p % 64 == np.arange(64)[None, :]}
    rot = np.zeros((P, P))
    for i in range(0, P, 2):
        rot[i + 1, i], rot[i, i + 1] = -1, 1
    rotm = np.zeros((P, P))
    for base in (0, 16, 64, 80):
        for i in range(base, base + 8):
            rotm[i + 8, i], rotm[i, i + 8] = -1, 1
    c |= {"rot": rot, "rotm": rotm}
    sel_i, sel_f = np.zeros((P, 64)), np.zeros((P, 64))
    for d in range(2):
        for h in range(4):
            sel_i[32 + 8 * d + h, 32 * d + h] = 1
            sel_f[32 + 8 * d + 4 + h, 32 * d + h] = 1
    c |= {"sel_i": sel_i, "sel_f": sel_f}
    up = [(p // (2 * b) == f // (2 * b)) & (p % (2 * b) < b) & (f % (2 * b) >= b) for b in LEVELS]
    chunk = p // CHUNK == f // CHUNK
    c |= {"mu": np.concatenate(up, 1), "ml": np.concatenate([u.T for u in up], 1), "su": chunk & (p < f),
          "sl": chunk & (p > f), "iu": chunk & (p <= f), "il": chunk & (p >= f),
          "nu": np.where(p <= f, 0, NEG), "nl": np.where(p >= f, 0, NEG)}
    t = np.arange(TC)
    row, col = (t // GRID_W).astype(np.float32), (t % GRID_W).astype(np.float32)
    inv = np.float32(10000.0) ** (-np.arange(16, dtype=np.float32) / np.float32(16))
    ang = np.concatenate([row[:, None] * inv, col[:, None] * inv], 1).T
    pair = np.arange(P) % HD // 2
    c |= {"cosa": np.cos(ang)[pair], "sina": np.sin(ang)[pair]}
    inv = np.float32(1.0) / np.float32(10000.0) ** (np.arange(8, dtype=np.float32) / np.float32(8))
    ang = np.concatenate([row[:, None] * inv, col[:, None] * inv], 1).T
    r32 = np.arange(32)
    ang = ang[r32 // 16 * 8 + r32 % 8]
    for name, bases in (("me", (64,)), ("mo", (0,)), ("mk", (0, 64))):
        cos, sin = np.ones((P, TC), np.float32), np.zeros((P, TC), np.float32)
        for b in bases:
            cos[b:b + 32], sin[b:b + 32] = np.cos(ang), np.sin(ang)
        c["cos" + name], c["sin" + name] = cos, sin
    q, k = np.arange(TC)[:, None], np.arange(TC)[None, :]
    halves = lambda m: m.reshape(2, P, TC).transpose(1, 0, 2).reshape(P, 2 * TC)
    c["wmask"] = halves(np.where((np.abs(k - q) <= 128) & (k >= 128), 0, NEG))
    c["padkeys"] = p + 1
    start = np.clip(q % GRID_W - 8, 0, GRID_W - 16)
    inside = (k % GRID_W >= start) & (k % GRID_W < start + 16)
    c["namask"] = halves(np.where(inside, 0, NEG))
    c["reset"] = np.broadcast_to(np.arange(T)[None, :] % CHUNK != 0, (P, T))
    out = np.concatenate([np.asarray(c[n], np.float32) for n, _ in CONSTS], 1)
    assert out.shape == (P, offsets(CONSTS)[1])
    return np.ascontiguousarray(out)


def lay_out(a):
    heads = lambda order: np.concatenate([np.arange(h * HD, h * HD + HD) for h in order])
    even = heads([h for t in range(4) for h in (t, 4 + t)])
    odd = heads([h for q in range(2) for j in range(4) for h in (8 * q + j, 8 * q + 4 + j)])
    slabs_k, slabs_f = [], []

    def tiled(w):
        n = w.shape[1] // P
        return w.reshape(KT, P, n, P).transpose(2, 1, 0, 3).reshape(n, P, D)

    def square(w):
        slabs_k.append(tiled(w))

    mods = np.concatenate([tiled(w) for w in (a["w_mod"][0], a["w_mod"][1], a["l0_w_mod_2"], a["l1_w_mod_2"])], 0)

    def ffn(f, w_in, w_out):
        w_in = tiled(w_in.reshape(D, 2, FT, P).transpose(0, 2, 1, 3).reshape(D, 2 * DFF))
        m = mods[slice(*MOD_BATCHES[f + 1])]
        slabs_k.append(np.stack([w_in[:len(m)], m], 1).reshape(-1, P, D))
        slabs_k.append(w_in[len(m):])
        slabs_f.append(w_out.reshape(FT, P, KT, P).transpose(2, 1, 0, 3).reshape(KT, P, DFF))

    def padded(w, cols):
        out = np.zeros((w.shape[0], len(cols)), np.float32)
        keep = np.flatnonzero(cols >= 0)
        out[:, keep] = w[:, cols[keep]]
        return out

    slabs_k.append(mods[:MOD_BATCHES[0][1]])
    ffn(0, a["ffn_in"][0, 0], a["ffn_out"][0, 0])
    w = a["even_w_in"][0]
    square(np.concatenate([w[:, even], w[:, 512:]], 1))
    w = a["even_w_out"][0]
    square(np.concatenate([w[even], w[512:]], 0))
    ffn(1, a["ffn_in"][0, 1], a["ffn_out"][0, 1])
    ffn(2, a["ffn_in"][1, 0], a["ffn_out"][1, 0])
    w = a["odd_w_in"][0]
    square(np.concatenate([w[:, odd], w[:, 1024:]], 1))
    square(a["odd_w_out"][0][odd])
    ffn(3, a["ffn_in"][1, 1], a["ffn_out"][1, 1])

    none = lambda n: np.full(n, -1)
    c = np.arange(a["l0_w_in_2"].shape[1])
    krope, gates = c[640:672], c[2720:2736]
    square(padded(a["l0_w_in_2"], np.concatenate([c[0:640], c[672:2720], c[2736:3760], krope, gates, none(16), krope,
                                                  none(32)])))
    uq = np.zeros((4, P, D), np.float32)
    for h in range(8):
        q = np.arange(96 * h, 96 * h + 96)
        cols = np.concatenate([q, none(32)] if h % 2 == 0 else [q[64:], none(32), q[:64]])
        w = padded(a["l0_mla_w_uq_2"], cols).reshape(3, P, P).transpose(1, 0, 2).reshape(P, 3 * P)
        uq[h // 2, :, h % 2 * 3 * P:(h % 2 + 1) * 3 * P] = w
    slabs_k.append(uq)
    ukv = a["l0_mla_w_ukv_2"].reshape(2, P, 4, 2, 2, HD)
    slabs_k.append(ukv.transpose(4, 1, 2, 0, 3, 5).reshape(2, P, D))
    square(a["l0_w_out_2"])
    c = np.arange(a["l1_w_in_2"].shape[1])
    square(padded(a["l1_w_in_2"], np.concatenate([c[0:1024], c[1056:3616], c[1024:1040], none(16), c[1040:1056],
                                                  none(80)])))
    square(a["l1_w_out_2"])

    col = lambda v: np.asarray(v).reshape(-1, P).T
    def gate_rows(v):
        out = np.zeros((P, 1), np.float32)
        out[0:4, 0], out[32:36, 0] = v[0], v[1]
        return out

    pair = lambda lat, ctx: np.stack([col(ctx), col(lat)], 2).reshape(P, 2 * KT)
    v = {"c": pair(a["c"][0], a["c_ctx"]), "bmod0": col(a["b_mod"][0]), "bmod1": col(a["b_mod"][1]),
         "qgain": np.concatenate([a["q_gain"][0]] * 2)[:, None], "kgain": np.concatenate([a["k_gain"][0]] * 2)[:, None],
         "mu": col(a["rwkv_mu"][0]), "w0": col(a["rwkv_w0"][0]), "a0": col(a["rwkv_a0"][0]), "kk": col(a["rwkv_k_k"][0]),
         "ka": col(a["rwkv_k_a"][0]), "rk": col(a["rwkv_r_k"][0]), "gnw": col(a["rwkv_gn_w"][0]),
         "gnb": col(a["rwkv_gn_b"][0]), "sink": np.broadcast_to(a["sink"][0][None, :], (P, 16)),
         "fgain": col(a["final_gain"]), "c2": pair(a["c_2"][0], a["c_ctx_2"]), "n0": col(a["l0_norm_2"]),
         "bm0": col(a["l0_b_mod_2"]), "qn": col(a["l0_mla_q_norm_2"]), "kvn": col(a["l0_mla_kv_norm_2"]),
         "cw": col(a["l0_mlstm_conv_w_2"]), "cb": col(a["l0_mlstm_conv_b_2"]), "bi": gate_rows(a["l0_mlstm_b_i_2"]),
         "bf": gate_rows(a["l0_mlstm_b_f_2"]), "mn": col(a["l0_mlstm_norm_2"]), "n1": col(a["l1_norm_2"]),
         "bm1": col(a["l1_b_mod_2"]), "bg": col(a["l1_gla_b_gate_2"]), "gln": col(a["l1_gla_norm_2"]),
         "fn": col(a["final_norm_2"])}
    wg = np.zeros((P, 256), np.float32)
    wg[0:16], wg[32:48] = a["l1_gla_w_gate_2"][0], a["l1_gla_w_gate_2"][1]
    small = np.concatenate([a["rwkv_w2"][0].reshape(P, 512), a["rwkv_a2"][0].reshape(P, 512), a["rwkv_g2"][0], wg], 1)
    tok = lambda x: x[0].T.reshape(KT, P, TC).transpose(1, 0, 2)
    q, k = np.arange(TC)[:, None], np.arange(TC)[None, :]
    bias = a["l1_na_rpb_2"][:, k // GRID_W - q // GRID_W + 7, np.clip(k % GRID_W - q % GRID_W + 15, 0, 30)]
    bias = np.stack([bias[2 * t + b, (qt - 2) * P:(qt - 1) * P] for t, b, qt in attention_units("na")], 1)
    return {"xin": np.concatenate([tok(a["ctx"]), tok(a["x"])], 2), "ctx2": tok(a["ctx_2"]),
            "stream_k": np.concatenate(slabs_k, 0), "stream_f": np.concatenate(slabs_f, 0),
            "vecs": np.concatenate([v[n] for n, _ in VECS], 1), "consts": shape_constants(), "small": small,
            "nabias": bias.reshape(P, -1)}


INPUTS = ["xin", "ctx2", "stream_k", "stream_f", "vecs", "consts", "small", "nabias"]


def kernel(**inputs):
    import concourse.bacc as bacc
    from concourse.bass_utils import run_bass_kernel_spmd

    laid = lay_out({n: np.asarray(x) for n, x in inputs.items()})
    nc = bacc.Bacc("TRN2", target_bir_lowering=False, num_devices=1)
    arrays, args = {}, []
    for name in INPUTS:
        arrays[name] = np.ascontiguousarray(laid[name])
        args.append(nc.dram_tensor(name, arrays[name].shape, F32, kind="ExternalInput").ap())
    result = nc.dram_tensor("result", (P, KT, TC), F32, kind="ExternalOutput").ap()
    build(nc, *args, result)
    r = run_bass_kernel_spmd(nc, [arrays], core_ids=[0]).results[0]["result"]
    return np.ascontiguousarray(r.transpose(2, 1, 0).reshape(1, TC, D))
```

```python
from contextlib import ExitStack

import numpy as np

import concourse.bass as bass
from concourse import mybir

F32 = mybir.dt.float32
F32R = mybir.dt.float32r
BF16 = mybir.dt.bfloat16
ALU = mybir.AluOpType
ACT = mybir.ActivationFunctionType
AX = mybir.AxisListType

P = 128
D = 1024
KT = D // P
TC = 256
T = 2 * TC
TT = T // P
DFF = 2816
FT = DFF // P
GRID_W = 64
HD = 64
EPS, GN_EPS = 1e-6, 64e-5
NEG = -1e30
DECAY_C = float(np.exp(-0.5))
RING = 4
OUT_PARTS = (8, 7, 7)
LEVELS = (1, 2, 4, 8, 16, 32, 64)
CHUNK = 64
NCH = T // CHUNK
BLOCK_LEVELS = (2, 4, 8, 16, 32)
CTX, LAT, ALL = (0, TC), (TC, T), (0, T)

VECS = [("c", 16), ("c2", 16), ("bmod0", 72), ("bmod1", 72), ("bm0", 24), ("bm1", 24), ("qgain", 1), ("kgain", 1), ("mu", 30), ("w0", 8), ("a0", 8),
        ("kk", 4), ("ka", 4), ("rk", 4), ("gnw", 4), ("gnb", 4), ("sink", 16), ("fgain", 8),
        ("n0", 8), ("qn", 3), ("kvn", 2), ("cw", 24), ("cb", 8), ("bi", 1), ("bf", 1), ("mn", 4),
        ("n1", 8), ("bg", 4), ("gln", 4), ("fn", 8)]
CONSTS = [("ident", P), ("ones", P), ("blk", P), ("rot", P), ("rotm", P), ("sel_i", 64),
          ("sel_f", 64), ("mu", 7 * P), ("ml", 7 * P), ("su", P), ("sl", P), ("iu", P), ("il", P),
          ("nu", P), ("nl", P), ("cosa", TC), ("sina", TC), ("padkeys", 1)]
TABLES = [("reset", T), ("ident64", HD), ("wmask", 2 * TC), ("cosme", TC), ("sinme", TC), ("cosmo", TC), ("sinmo", TC), ("cosmk", TC),
          ("sinmk", TC), ("namask", 2 * TC)]
SMALL = [("w2", 512), ("a2", 512), ("g2", 512), ("wg", 256)]


def offsets(table):
    at, out = 0, {}
    for name, n in table:
        out[name] = (at, n)
        at += n
    return out, at


MOD_BATCHES = [(0, 20), (20, 64), (64, 108), (108, 152), (152, 192)]
MOD_SCALES = {1: None, 4: None, 7: None, 10: None, 13: None, 16: None, 19: "n0", 22: "n1"}
MOD_HALF_GATES = (2, 8, 11, 17)
FFN_RUNS = [[(11, 0)], [(11, 0)], [(9, 0), (2, 1)], [(11, 1)]]


def ffn_slabs(f):
    return [(f"ffn_in{f}", 4 * FT), (f"ffn_out{f}", len(OUT_PARTS) * KT)]


SLABS = [("mods", MOD_BATCHES[0][1]), *ffn_slabs(0), ("even_in", 21), ("even_out", KT), *ffn_slabs(1), *ffn_slabs(2),
         ("odd_in", 12), ("odd_out", KT), *ffn_slabs(3), ("l0_in", 30), ("mla_up", 6), ("l0_out", KT), ("l1_in", 29),
         ("l1_out", KT)]
SLAB_AT, N_SLABS = offsets(SLABS)
SPLIT_AT, _ = offsets([(stage, 2 * FT if stage.startswith("ffn_in") else n) for stage, n in SLABS
                              if not stage.startswith(("mods", "mla_up"))])
FIRST_SPLITS = [stage for stage in SPLIT_AT if not stage.startswith("ffn_out")]
VECTOR_SPLIT_AT, _ = offsets([(stage, n - 2 if stage in FIRST_SPLITS else n) for stage, (_, n) in SPLIT_AT.items()])
NORMS = [(ALL, 0, KT, 0, 0), (ALL, 3 * KT, 4 * KT, 0, 1), (ALL, 6 * KT, 7 * KT, 4, 2),
         (ALL, 72, 72 + KT, 0, 3), (ALL, 72 + 3 * KT, 72 + 4 * KT, 0, 4), (LAT, 72 + 6 * KT, 72 + 7 * KT, 4, 5),
         (ALL, 144, 144 + KT, 2, 7), (ALL, 168, 168 + KT, 4, 8)]
GAIN_NORMS = [("fgain", 0, 6), ("fn", 4, 9)]
FFNS = [(ALL, 2 * KT), (ALL, 8 * KT), (ALL, 72 + 2 * KT), (LAT, 72 + 8 * KT)]
LINEARS = [("even_in", 21, 1), ("odd_in", 12, 4), ("l0_in", 30, 6), ("l1_in", 29, 7)]
LINEAR_RUNS = [[(5, ALL)], [(2, LAT), (1, ALL)], [(7, ALL)], [(2, ALL), (1, LAT), (2, ALL), (2, LAT)]]
RESIDUALS = [("even_out", ALL, 5 * KT), ("odd_out", LAT, 72 + 5 * KT), ("l0_out", ALL, 144 + 2 * KT),
             ("l1_out", LAT, 168 + 2 * KT)]
ATTENTIONS = ("even", "odd", "mla", "na")


def linear_copies_before(p, who):
    return 2 + sum((n + 1 - who) // 2 for _, n, _ in LINEARS[:p])


def attention_units(which):
    if which == "even":
        return [(t, b, qt) for t in range(4) for qt in range(TT) for b in range(2)]
    if which == "odd":
        return [(t, b, qt) for t in range(8) for qt in (2, 3) for b in range(2)]
    if which == "mla":
        return [(t, b, qt) for t in range(4) for qt in range(TT) for b in range(2)]
    return [(t, b, qt) for t in range(4) for qt in (2, 3) for b in range(2)]


def units_before(a):
    return sum(len(attention_units(which)) for which in ATTENTIONS[:a])


def build(nc, xin, ctx2, stream_k, stream_f, vecs, consts, tables, small, nabias, out):
    VO, NV = offsets(VECS)
    CO, NCST = offsets(CONSTS)
    TO, _ = offsets(TABLES)
    SO, NS = offsets(SMALL)
    with ExitStack() as ctx:
        def sb(name, shape):
            return ctx.enter_context(nc.sbuf_tensor(name, shape, F32))

        def sem(name):
            return ctx.enter_context(nc.semaphore(name))

        X = sb("residual_stream", [P, KT, T])
        with ExitStack() as shared:
            H_HI = shared.enter_context(nc.sbuf_tensor("input_hi", [P, KT, T], F32R))
            HID = shared.enter_context(nc.sbuf_tensor("hidden_hi_lo", [P, 44, T], F32R))
            MODW2 = [shared.enter_context(nc.sbuf_tensor(f"mod_weights_parts{i}", [P, 2, 3, T], BF16)) for i in range(2)]
            H_LO = shared.enter_context(nc.sbuf_tensor("input_lo", [P, KT, T], F32R))
            SPLIT = shared.enter_context(nc.sbuf_tensor("weights_hi_lo", [P, 2, 2, D], F32R))
        H = sb("mixer_io", [P, KT, T])
        BIG = sb("projections", [P, 30, T])
        WORK = sb("work", [P, 28, T])
        SPARE = sb("spare_tiles", [P, 8, T])
        ring = sb("weight_ring", [P, RING, D])
        vec = sb("vectors", [P, NV])
        cst = sb("constants", [P, NCST])
        smallw = sb("small_weights", [P, NS])
        MODS = sb("modulation", [P, 192, 2])
        conds = sb("silu_conditions", [P, 2, 2 * KT])
        cond_parts = ctx.enter_context(nc.sbuf_tensor("condition_parts", [P, 2, 3, 2 * KT], BF16))
        stat = sb("row_statistics", [P, 3, 5])
        wstat = sb("wkv_vectors", [P, 2, 4, NCH])
        omka = sb("one_minus_ka", [P, 4])
        mu_rest = sb("one_minus_mus", [P, 15])
        epsb = sb("epsilons", [P, 4])
        warm = sb("silu_warm", [P, 1])
        pb = [ctx.enter_context(nc.psum_tensor(f"bank{i}", [P, 512], F32)) for i in range(8)]

        def V(name, i=0, n=1):
            return vec[:, VO[name][0] + i:VO[name][0] + i + n]

        def C(name, i=0, n=None):
            o, w = CO[name]
            return cst[:, o + i:o + i + (w if n is None else n)]

        def TAB(name, i=0, n=None):
            first = {"cosme": "cosme", "sinme": "cosme", "cosmo": "cosme", "sinmo": "cosme", "cosmk": "cosme",
                     "sinmk": "cosme", "ident64": "reset"}.get(name, name)
            o, w = TO[name][0] - TO[first][0] + 3 * T, TO[name][1]
            return SPARE[:, :, :].rearrange("p a t -> p (a t)")[:, o + i:o + i + (w if n is None else n)]

        def S(name, p0, p1, i, n):
            o = SO[name][0]
            return smallw[p0:p1, o + i:o + i + n]

        def tiles(ap, n=P):
            return ap.rearrange("p (a n) -> p a n", n=n)

        def over(ap, n):
            return ap.unsqueeze(1).to_broadcast([ap.shape[0], n, ap.shape[1]])

        def along(ap, n):
            return ap.unsqueeze(2).to_broadcast([ap.shape[0], ap.shape[1], n])

        def segments(cols):
            return [(s, a, b) for s, (a, b) in enumerate((CTX, LAT)) if a >= cols[0] and b <= cols[1]]

        vectors_loaded = sem("vectors_loaded")
        loaded = sem("inputs_loaded")
        prepared = sem("vectors_prepared")
        ctx2_loaded = sem("ctx2_loaded")
        nab_loaded = sem("na_bias_loaded")
        stored = sem("output_stored")
        slot_full = [sem(f"slot_full{i}") for i in range(RING)]
        slab_done = sem("slab_multiplied")
        conds_ready, parts_ready = sem("silu_of_condition_ready"), sem("parts_of_condition_ready")
        mods_ready = sem("modulation_ready")
        mod_first, mod_rest, mod_second, mod_third = (sem(f"mod_{x}") for x in ("first_part", "rest", "second_part", "third_part"))
        hi_ready = sem("weights_hi_ready")
        split_ready = sem("weights_lo_ready")
        first_ready = sem("first_weights_lo_ready")
        tables_loaded = sem("tables_loaded")
        squared = sem("tile_squared")
        squares_added = sem("squares_of_tiles_added")
        summed = sem("squares_summed")
        rooted = sem("rms_ready")
        scaled = sem("tile_scaled")
        modulated = sem("tile_modulated")
        input_split = sem("tile_split")
        copied = [sem("tile_copied_by_scalar"), sem("tile_copied_by_vector")]
        gated = sem("gate_tile_silu")
        hidden = sem("hidden_tile_ready")
        hidden_hi = sem("hidden_tile_hi_ready")
        hidden_split = sem("hidden_tile_lo_ready")
        ffn_added = sem("ffn_tile_added")
        mixer_added = sem("mixer_tile_added")
        heads_ready = sem("heads_ready")
        values_ready = sem("values_by_token_ready")
        scores_ready = sem("scores_ready")
        max_ready = sem("row_max_ready")
        probs_ready = sem("probs_ready")
        probs_scaled = sem("probs_scaled")
        probs_turned = sem("probs_transposed")
        turned_copied = sem("transposed_probs_copied")
        mixed = sem("values_mixed")
        mixed_copied = sem("mixed_values_copied")
        mixer_hi, mixer_split = sem("mixer_output_hi_ready"), sem("mixer_output_lo_ready")
        mixer_ready = sem("mixer_output_ready")

        def take(pe, n, i=None, per=0):
            full = 16 * (n // RING + 1)
            pe.wait_ge(slot_full[n % RING], full if i is None else i * (16 * per // RING) + full)
            return ring[:, n % RING, :]

        def split_hi(act, place, n, words=D, i=None, per=0):
            w = take(act, n, i, per)
            act.activation(SPLIT[:, place % 2, 0, 0:words], w[:, 0:words], ACT.Copy).then_inc(hi_ready, 1)

        def split_lo(eng, place, n, count, words=D, ready=split_ready):
            eng.wait_ge(hi_ready, count)
            eng.tensor_tensor(SPLIT[:, place % 2, 1, 0:words], ring[:, n % RING, 0:words],
                              SPLIT[:, place % 2, 0, 0:words].bitcast(F32), ALU.subtract).then_inc(ready, 1)

        def first_slab(stage, k):
            return SLAB_AT[stage][0] + (2 * k if stage.startswith("ffn") else k)

        def first_splits_scalar(act, stage):
            names = list(SPLIT_AT)
            if stage != names[0]:
                last = names[names.index(stage) - 1]
                act.wait_ge(slab_done, sum(SLAB_AT[last]))
            for k in range(2):
                split_hi(act, k, first_slab(stage, k))

        def first_splits_gpsimd(pool, stage):
            for k in range(2):
                split_lo(pool, k, first_slab(stage, k), SPLIT_AT[stage][0] + k + 1, D, first_ready)

        def split_product(pe, out, place, q, x_hi, x_lo, first, last):
            w = slice(q * P, (q + 1) * P)
            pe.matmul(out, SPLIT[:, place % 2, 0, w], x_hi, start=first, stop=False)
            pe.matmul(out, SPLIT[:, place % 2, 0, w], x_lo, start=False, stop=False)
            return pe.matmul(out, SPLIT[:, place % 2, 1, w], x_hi, start=False, stop=last)

        def setup_scalar(act):
            act.sem_inc(copied[0], 2)
            act.sem_inc(gated, 2)
            act.wait_ge(vectors_loaded, 16)
            act.activation(conds[:, :, :].rearrange("p c k -> p (c k)"), V("c", 0, 4 * KT), ACT.Silu).then_inc(conds_ready, 1)

        def inputs_scalar(act):
            act.wait_ge(loaded, 16 * 3)
            act.wait_ge(prepared, 1)

        def setup_vector(dve):
            dve.sem_inc(copied[1], 2)
            dve.sem_inc(split_ready, 2)
            dve.sem_inc(hidden, 2)
            dve.sem_inc(ffn_added, 4)
            dve.sem_inc(mixer_added, 4)
            dve.memset(epsb[:, 0:1], EPS)
            dve.memset(epsb[:, 1:2], HD * EPS)
            dve.memset(epsb[:, 2:3], GN_EPS).then_inc(prepared, 1)
            dve.wait_ge(vectors_loaded, 16)
            dve.tensor_scalar(omka[:, :], V("ka", 0, 4), -1.0, 1.0, ALU.mult, ALU.add)
            dve.tensor_tensor(mu_rest[:, :], V("mu", 0, 15), V("mu", 15, 15), ALU.add)
            dve.drain()
            dve.tensor_scalar(mu_rest[:, :], mu_rest[:, :], -1.0, 1.0, ALU.mult, ALU.add)

        def halves_of(n):
            return [(h, ring[:, n % RING, h * T:(h + 1) * T]) for h in range(2)]

        def counted(i, c, step):
            return c if i is None else i * step + c

        def mod_firsts(act, n, before, i=None, per=0, buf=MODW2[0]):
            take(act, n, i, per)
            if before is not None:
                act.wait_ge(slab_done, counted(i, before + 1, per))
            for h, w in halves_of(n):
                act.activation(buf[:, h, 0, :], w, ACT.Copy).then_inc(mod_first, 1)

        def mod_seconds(act, n, q, i=None, buf=MODW2[0]):
            for h, w in halves_of(n):
                act.wait_ge(mod_rest, counted(i, 2 * q + h + 1, 8))
                act.activation(buf[:, h, 1, :], w, ACT.Copy).then_inc(mod_second, 1)

        def mod_split_scalar(act, n, q, before, i=None, per=0, buf=MODW2[0]):
            mod_firsts(act, n, before, i, per, buf)
            mod_seconds(act, n, q, i, buf)

        def mod_split_vector(dve, n, q, i=None, buf=MODW2[0]):
            for h, w in halves_of(n):
                dve.wait_ge(mod_first, counted(i, 2 * q + h + 1, 8))
                dve.tensor_tensor(w, w, buf[:, h, 0, :], ALU.subtract).then_inc(mod_rest, 1)
            for h, w in halves_of(n):
                dve.wait_ge(mod_second, counted(i, 2 * q + h + 1, 8))
                dve.tensor_tensor(buf[:, h, 2, :], w, buf[:, h, 1, :], ALU.subtract).then_inc(mod_third, 1)

        def mod_product(pe, q, cond, column, i=None, buf=MODW2[0]):
            out = pb[7][:, column:column + 6] if i is None else pb[7][:, bass.ds(i * 24 + column, 6)]
            for kt in range(KT):
                h = kt // (KT // 2)
                if kt % (KT // 2) == 0:
                    pe.wait_ge(mod_third, counted(i, 2 * q + h + 1, 8))
                w = slice(kt % (KT // 2) * P, kt % (KT // 2) * P + P)
                for part in range(3):
                    mm = pe.matmul(out, buf[:, h, part, w], cond_parts[:, cond, :, 2 * kt:2 * kt + 2],
                                   start=kt == part == 0, stop=kt == KT - 1 and part == 2)
            mm.then_inc(slab_done, 1)

        FIRST_MODS = MOD_BATCHES[0][1]

        def mods_scalar(act):
            for n in range(RING):
                mod_split_scalar(act, n, n, n - 2 if n >= 2 else None, buf=MODW2[n % 2])
            with act.Fori(0, FIRST_MODS // RING - 1) as i:
                for n in range(RING, 2 * RING):
                    mod_split_scalar(act, n, n, n - 2, i, RING, MODW2[n % 2])

        def conditions_vector(dve):
            dve.wait_ge(conds_ready, 1)
            for part in range(3):
                x = cond_parts[:, :, part, :]
                dve.tensor_copy(x, conds[:, :, :])
                dve.drain()
                dve.tensor_tensor(conds[:, :, :], conds[:, :, :], x, ALU.subtract)
                dve.drain()
            dve.drain().then_inc(parts_ready, 1)

        def mods_tensor(pe):
            pe.wait_ge(parts_ready, 1)
            for n in range(RING):
                mod_product(pe, n, 0, 6 * n, buf=MODW2[n % 2])
            with pe.Fori(0, FIRST_MODS // RING - 1) as i:
                for n in range(RING, 2 * RING):
                    mod_product(pe, n, 0, 6 * n, i, MODW2[n % 2])

        def first_mods_vector(dve):
            for n in range(RING):
                mod_split_vector(dve, n, n, buf=MODW2[n % 2])
            with dve.Fori(0, FIRST_MODS // RING - 1) as i:
                for n in range(RING, 2 * RING):
                    mod_split_vector(dve, n, n, i, MODW2[n % 2])

        def mods_vector(dve, b, done):
            lo, hi = MOD_BATCHES[b]
            dve.wait_ge(slab_done, done)
            parts = pb[7][:, 0:6 * (hi - lo)].rearrange("p (m c s) -> p m c s", c=3, s=2)
            dve.tensor_tensor(MODS[:, lo:hi, :], parts[:, :, 2, :], along(V("bmod0", lo, hi - lo), 2), ALU.add)
            dve.drain()
            for part in (1, 0):
                dve.tensor_tensor(MODS[:, lo:hi, :], MODS[:, lo:hi, :], parts[:, :, part, :], ALU.add)
                dve.drain()
            for q in range(lo // KT, hi // KT):
                group = MODS[:, q * KT:(q + 1) * KT, :]
                if q in MOD_SCALES:
                    dve.tensor_scalar(group, group, 1.0, None, ALU.add)
                    if MOD_SCALES[q] is not None:
                        dve.drain()
                        dve.tensor_tensor(group, group, along(V(MOD_SCALES[q], 0, KT), 2), ALU.mult)
                if q in MOD_HALF_GATES:
                    dve.tensor_scalar(group, group, 0.5, None, ALU.mult)
            dve.drain().then_inc(mods_ready, 1)

        SQ = WORK[:, 20:28, :]

        def square_tiles(act, cols, x_ready, x0):
            a, b = cols
            for kt in range(KT):
                if x_ready is not None:
                    act.wait_ge(x_ready, x0 + kt)
                act.activation(SQ[:, kt, a:b], X[:, kt, a:b], ACT.Square).then_inc(squared, 1)

        def root(act, cols, bank, place):
            a, b = cols
            act.wait_ge(summed, place + 1)
            act.activation(WORK[:, 0, a:b], pb[bank][:, a:b], ACT.Sqrt, bias=epsb[:, 0:1], scale=1.0 / D)\
               .then_inc(rooted, 1)

        NORMED = WORK[:, 12:20, :]

        def norm_scalar(act, n, stage, x_ready=None, x0=0):
            cols, shift, scale, bank, place = NORMS[n]
            a, b = cols
            square_tiles(act, cols, x_ready, x0)
            root(act, cols, bank, place)
            first_splits_scalar(act, stage)
            act.wait_ge(mods_ready, (1, 2, 2, 3, 4, 4, 5, 5)[n])
            for kt in range(KT):
                act.wait_ge(scaled, place * KT + kt + 1)
                for s, p, q in segments(cols):
                    ins = act.activation(H_HI[:, kt, p:q], NORMED[:, kt, p:q], ACT.Identity,
                                         bias=MODS[:, shift + kt, s:s + 1])
                ins.then_inc(modulated, 1)

        ADDED_PLACES = [place for place in range(len(NORMS) + len(GAIN_NORMS)) if place not in (0, 7)]

        def add_squares_gpsimd(pool, cols, place):
            a, b = cols
            for kt in range(1, KT - 1):
                pool.wait_ge(squared, place * KT + kt + 1)
                pool.tensor_tensor(SQ[:, 0, a:b], SQ[:, 0, a:b], SQ[:, kt, a:b], ALU.add)
                pool.drain()
            pool.drain().then_inc(squares_added, 1)

        def sum_squares(pe, cols, bank, place):
            a, b = cols
            added = place in ADDED_PLACES
            if added:
                pe.wait_ge(squares_added, ADDED_PLACES.index(place) + 1)
                pe.matmul(pb[bank][:, a:b], C("ones"), SQ[:, 0, a:b], start=True, stop=False)
            for kt in range(KT - 1 if added else 0, KT):
                pe.wait_ge(squared, place * KT + kt + 1)
                mm = pe.matmul(pb[bank][:, a:b], C("ones"), SQ[:, kt, a:b], start=kt == 0, stop=kt == KT - 1)
            mm.then_inc(summed, 1)

        def norm_tensor(pe, n):
            sum_squares(pe, NORMS[n][0], NORMS[n][3], NORMS[n][4])

        def norm_vector(dve, n):
            cols, shift, scale, bank, place = NORMS[n]
            a, b = cols
            dve.wait_ge(rooted, place + 1)
            dve.reciprocal(pb[bank + 1][:, a:b], WORK[:, 0, a:b])
            dve.drain()
            for kt in range(KT + 2):
                if kt < KT:
                    for s, p, q in segments(cols):
                        ins = dve.scalar_tensor_tensor(out=NORMED[:, kt, p:q], in0=X[:, kt, p:q],
                                                       scalar=MODS[:, scale + kt, s:s + 1], in1=pb[bank + 1][:, p:q],
                                                       op0=ALU.mult, op1=ALU.mult)
                    ins.then_inc(scaled, 1)
                if kt >= 2:
                    lo = kt - 2
                    dve.wait_ge(modulated, n * KT + lo + 1)
                    for s, p, q in segments(cols):
                        ins = dve.scalar_tensor_tensor(out=H_LO[:, lo, p:q], in0=NORMED[:, lo, p:q],
                                                       scalar=MODS[:, shift + lo, s:s + 1],
                                                       in1=H_HI[:, lo, p:q].bitcast(F32), op0=ALU.add, op1=ALU.subtract)
                    ins.then_inc(input_split, 1)

        def gain_norm_scalar(act, g, x_ready, x0):
            _, bank, place = GAIN_NORMS[g]
            square_tiles(act, LAT, x_ready, x0)
            root(act, LAT, bank, place)

        def gain_norm_tensor(pe, g):
            sum_squares(pe, LAT, *GAIN_NORMS[g][1:])

        def gain_norm_vector(dve, g):
            gain, bank, place = GAIN_NORMS[g]
            a, b = LAT
            dve.wait_ge(rooted, place + 1)
            dve.reciprocal(pb[bank + 1][:, a:b], WORK[:, 0, a:b])
            dve.drain()
            for kt in range(KT):
                dve.scalar_tensor_tensor(out=X[:, kt, a:b], in0=X[:, kt, a:b], scalar=V(gain, kt),
                                         in1=pb[bank + 1][:, a:b], op0=ALU.mult, op1=ALU.mult).then_inc(scaled, 1)

        def linear_tensor(pe, p):
            stage, n, norm = LINEARS[p]

            def product(m, i, run, cols):
                a, b = cols
                c = VECTOR_SPLIT_AT[stage][0] + run + m + 1
                pe.wait_ge(split_ready, c if i is None else i * 4 + c)
                c = linear_copies_before(p, m % 2) - 2 + (run + m) // 2 + 1
                pe.wait_ge(copied[m % 2], c if i is None else i * 2 + c)
                for kt in range(KT):
                    if run + m == 0:
                        pe.wait_ge(input_split, norm * KT + kt + 1)
                    mm = split_product(pe, pb[m % 4][:, a:b], m, kt, H_HI[:, kt, a:b], H_LO[:, kt, a:b], kt == 0,
                                       kt == KT - 1)
                mm.then_inc(slab_done, 1)

            pe.wait_ge(first_ready, 2 * FIRST_SPLITS.index(stage) + 2)
            run = 0
            for turns, cols in LINEAR_RUNS[p]:
                with pe.Fori(0, turns) as i:
                    for k in range(4):
                        product(k, i, run, cols)
                run += 4 * turns
            for m in range(n - run):
                product(m, None, run, ALL)

        def linear_steps(eng, p, step):
            n, run = LINEARS[p][1], 0
            for r, (turns, cols) in enumerate(LINEAR_RUNS[p]):
                last = r == len(LINEAR_RUNS[p]) - 1
                if turns > last:
                    with eng.Fori(0, turns - last) as i:
                        for k in range(4):
                            step(run + k, i, cols)
                run += 4 * (turns - last)
            for m in range(run, n):
                step(m, None, cols if m < n // 4 * 4 else ALL)

        def linear_out(m, i, a, b):
            return BIG[:, m, a:b] if i is None else BIG[:, bass.ds(i * 4 + m, 1), a:b].rearrange("p o t -> p (o t)")

        def linear_scalar(act, p):
            stage, n, _ = LINEARS[p]
            n0 = SLAB_AT[stage][0]

            def step(m, i, cols):
                a, b = cols
                act.wait_ge(slab_done, n0 + m + 1 if i is None else i * 4 + (n0 + m + 1))
                if i is not None or m + 2 < n:
                    split_hi(act, m, n0 + m + 2, D, i, 4)
                if m % 2 == 0:
                    act.activation(linear_out(m, i, a, b), pb[m % 4][:, a:b], ACT.Copy).then_inc(copied[0], 1)

            linear_steps(act, p, step)

        def linear_vector(dve, p):
            stage, n, _ = LINEARS[p]
            n0, s0 = SLAB_AT[stage][0], SPLIT_AT[stage][0]

            def step(m, i, cols):
                a, b = cols
                if i is not None or m + 2 < n:
                    split_lo(dve, m, n0 + m + 2, s0 + m + 3 if i is None else i * 4 + (s0 + m + 3))
                if m % 2:
                    dve.wait_ge(slab_done, n0 + m + 1 if i is None else i * 4 + (n0 + m + 1))
                    dve.tensor_copy(linear_out(m, i, a, b), pb[m % 4][:, a:b]).then_inc(copied[1], 1)

            linear_steps(dve, p, step)

        def all_copied(eng, p, who):
            eng.wait_ge(copied[who], linear_copies_before(p + 1, who))

        def add_tile(dve, cols, x, gate, bank, added):
            for s, p, q in segments(cols):
                ins = dve.scalar_tensor_tensor(out=x[:, p:q], in0=bank[:, p:q], scalar=gate[:, s:s + 1], in1=x[:, p:q],
                                               op0=ALU.mult, op1=ALU.add)
            ins.then_inc(added, 1)

        OUT_HI, OUT_LO = HID[:, 0:KT, :], HID[:, KT:2 * KT, :]

        def residual_tensor(pe, r):
            stage, (a, b), _ = RESIDUALS[r]
            s0 = VECTOR_SPLIT_AT[stage][0]
            pe.wait_ge(first_ready, 2 * FIRST_SPLITS.index(stage) + 2)
            with pe.Fori(0, KT // 4) as i:
                for k in range(4):
                    pe.wait_ge(split_ready, i * 4 + (s0 + k + 1))
                    pe.wait_ge(mixer_added, i * 4 + (r * KT + k + 1))
                    for kt in range(KT):
                        if k == 0:
                            pe.wait_ge(mixer_split, r * KT + kt + 1)
                        mm = split_product(pe, pb[k][:, a:b], k, kt, OUT_HI[:, kt, a:b], OUT_LO[:, kt, a:b], kt == 0,
                                           kt == KT - 1)
                    mm.then_inc(slab_done, 1)

        def residual_scalar(act, r):
            stage, (a, b), _ = RESIDUALS[r]
            n0 = SLAB_AT[stage][0]
            first_splits_scalar(act, stage)
            act.wait_ge(mixer_ready, r + 1)
            for kt in range(KT):
                act.activation(OUT_HI[:, kt, a:b], H[:, kt, a:b], ACT.Copy).then_inc(mixer_hi, 1)
            for m in range(2, KT):
                act.wait_ge(slab_done, n0 + m - 1)
                split_hi(act, m, n0 + m)

        def residual_vector(dve, r):
            stage, cols, gate = RESIDUALS[r]
            a, b = cols
            n0, s0 = SLAB_AT[stage][0], SPLIT_AT[stage][0]
            for kt in range(KT):
                dve.wait_ge(mixer_hi, r * KT + kt + 1)
                dve.tensor_tensor(OUT_LO[:, kt, a:b], H[:, kt, a:b], OUT_HI[:, kt, a:b].bitcast(F32), ALU.subtract)\
                   .then_inc(mixer_split, 1)
            for m in range(KT):
                if m + 2 < KT:
                    split_lo(dve, m, n0 + m + 2, s0 + m + 3)
                dve.wait_ge(slab_done, n0 + m + 1)
                add_tile(dve, cols, X[:, m, :], MODS[:, gate + m, :], pb[m % 4], mixer_added)

        HIDDEN, GATE = WORK[:, 17:19, :], WORK[:, 19, :]
        PER = 8

        def mods_before(f):
            return FIRST_MODS + 2 * FT * f

        def ffn_loop(eng, f, turn):
            n0, turns = SLAB_AT[f"ffn_in{f}"][0], FT // 2 - 1
            with eng.Fori(0, turns) as i:
                turn(i, n0, 0)
            turn(None, n0 + PER * turns, 2 * turns)

        def ffn_tensor(pe, f):
            a, b = FFNS[f][0]
            stage = f"ffn_in{f}"
            norm, s0 = (0, 2, 3, 5)[f], VECTOR_SPLIT_AT[stage][0]
            pe.wait_ge(mods_ready, f + 1)
            pe.wait_ge(first_ready, 2 * FIRST_SPLITS.index(stage) + 2)
            t = 0
            for turns, cond in FFN_RUNS[f]:
                t0, q0 = f * FT + t, mods_before(f) + 2 * t
                with pe.Fori(0, turns) as i:
                    for k in range(4):
                        pe.wait_ge(split_ready, i * 4 + (s0 + 2 * t + k + 1))
                        pe.wait_ge(hidden if k % 2 else gated, i * 2 + (t0 + k // 2 + 1))
                        for kt in range(KT):
                            if k == 0:
                                pe.wait_ge(input_split, norm * KT + kt + 1)
                            mm = split_product(pe, pb[k][:, a:b], k, kt, H_HI[:, kt, a:b], H_LO[:, kt, a:b], kt == 0,
                                               kt == KT - 1)
                        mm.then_inc(slab_done, 1)
                        mod_product(pe, q0 + k, cond, 6 * (2 * t + k), i)
                t += 2 * turns
            s0 = VECTOR_SPLIT_AT[f"ffn_out{f}"][0]
            pe.wait_ge(mods_ready, f + 2)
            with pe.Fori(0, KT // 4) as i:
                for k in range(4):
                    pe.wait_ge(ffn_added, i * 4 + (f * KT + k + 1))
                    t = 0
                    for part, n in enumerate(OUT_PARTS):
                        s = len(OUT_PARTS) * k + part
                        pe.wait_ge(split_ready, i * 4 * len(OUT_PARTS) + (s0 + s + 3))
                        for q in range(n):
                            if k == 0:
                                pe.wait_ge(hidden_split, f * FT + t + 1)
                            mm = split_product(pe, pb[4 + k][:, a:b], s, q, HID[:, t, a:b], HID[:, FT + t, a:b], t == 0,
                                               t == FT - 1)
                            t += 1
                        mm.then_inc(slab_done, 1)

        def out_slabs(f):
            n0 = SLAB_AT[f"ffn_out{f}"][0]
            return [(n0 + s, OUT_PARTS[s % len(OUT_PARTS)] * P) for s in range(len(OUT_PARTS) * KT)]

        def hidden_tile(t, i, a, b):
            return HID[:, t, a:b] if i is None else HID[:, bass.ds(i * 2 + t, 1), a:b].rearrange("p o t -> p (o t)")

        def ffn_scalar(act, f):
            a, b = FFNS[f][0]
            slabs = out_slabs(f)

            def turn(i, n, t):
                act.activation(warm[:, :], epsb[:, 0:1], ACT.Silu)
                for k in range(4):
                    j, with_mod = k // 2, i is not None or k < 3
                    q = mods_before(f) + 2 * t + k + 1
                    act.wait_ge(slab_done, counted(i, n + 2 * k + 1, PER))
                    if i is None and k >= 2:
                        split_hi(act, k, *slabs[k - 2])
                    else:
                        split_hi(act, k, n + 2 * k + 4, D, i, PER)
                    if with_mod:
                        mod_firsts(act, n + 2 * k + 3, n + 2 * k + 1, i, PER)
                    if k % 2:
                        act.wait_ge(hidden, counted(i, 2 + f * FT + t + j + 1, 2))
                        act.activation(hidden_tile(t + j, i, a, b), HIDDEN[:, j, a:b], ACT.Copy).then_inc(hidden_hi, 1)
                    if with_mod:
                        mod_seconds(act, n + 2 * k + 3, q, i)
                    if k % 2 == 0:
                        act.wait_ge(hidden, counted(i, 1 + f * FT + t + j + 1, 2))
                        act.activation(GATE[:, a:b], pb[2 * j][:, a:b], ACT.Silu).then_inc(gated, 1)

            n0 = SLAB_AT[f"ffn_in{f}"][0]
            act.wait_ge(input_split, ((0, 2, 3, 5)[f] + 1) * KT)
            mod_split_scalar(act, n0 + 1, mods_before(f), n0 - 1)
            ffn_loop(act, f, turn)
            for s in range(2, len(slabs)):
                act.wait_ge(slab_done, slabs[s - 2][0] + 1)
                split_hi(act, s, *slabs[s])

        def ffn_vector(dve, f):
            (a, b), gate = FFNS[f]
            slabs, s0, s1 = out_slabs(f), SPLIT_AT[f"ffn_in{f}"][0], SPLIT_AT[f"ffn_out{f}"][0]

            def turn(i, n, t):
                for k in range(4):
                    j = k // 2
                    if k % 2:
                        dve.drain()
                        dve.wait_ge(slab_done, counted(i, n + 2 * k + 1, PER))
                        dve.wait_ge(gated, counted(i, 2 + f * FT + t + j + 1, 2))
                        dve.tensor_tensor(HIDDEN[:, j, a:b], GATE[:, a:b], pb[k][:, a:b], ALU.mult).then_inc(hidden, 1)
                    if i is None and k >= 2:
                        split_lo(dve, k, slabs[k - 2][0], s1 + k - 1, slabs[k - 2][1])
                    else:
                        split_lo(dve, k, n + 2 * k + 4, counted(i, s0 + 2 * t + k + 3, 4))
                    if i is not None or k < 3:
                        mod_split_vector(dve, n + 2 * k + 3, mods_before(f) + 2 * t + k + 1, i)
                    if k % 2:
                        dve.wait_ge(hidden_hi, counted(i, f * FT + t + j + 1, 2))
                        dve.tensor_tensor(hidden_tile(FT + t + j, i, a, b), HIDDEN[:, j, a:b],
                                          hidden_tile(t + j, i, a, b).bitcast(F32), ALU.subtract).then_inc(hidden_split, 1)

            mod_split_vector(dve, SLAB_AT[f"ffn_in{f}"][0] + 1, mods_before(f))
            ffn_loop(dve, f, turn)
            mods_vector(dve, f + 1, SLAB_AT[f"ffn_out{f}"][0])
            for s in range(2, len(slabs) + 2):
                if s < len(slabs):
                    split_lo(dve, s, slabs[s][0], s1 + s + 1, slabs[s][1])
                if (s - 1) % len(OUT_PARTS) == 0:
                    kt = (s - 1) // len(OUT_PARTS) - 1
                    dve.wait_ge(slab_done, slabs[s - 2][0] + 1)
                    for q, p, r in segments((a, b)):
                        ins = dve.scalar_tensor_tensor(out=X[:, kt, p:r], in0=pb[4 + kt % 4][:, p:r],
                                                       scalar=MODS[:, gate + kt, q:q + 1], in1=X[:, kt, p:r],
                                                       op0=ALU.mult, op1=ALU.add)
                    ins.then_inc(ffn_added, 1)

        def attention_operands(which, t, b, qt):
            q0, nk = qt * P, (TC if qt < 2 else T)
            rows = slice(HD * b, HD * b + HD)
            if which == "even":
                pairs = [(BIG[rows, t, q0:q0 + P], BIG[rows, 4, 0:nk])]
                return pairs, nk, H[rows, t, q0:q0 + P], HD * b
            if which == "odd":
                pairs = [(BIG[rows, t, q0:q0 + P], BIG[rows, 8 + t // 4, 0:nk])]
                return pairs, nk, H[rows, t, q0:q0 + P], t // 4 * P + HD * b
            if which == "mla":
                rope = slice(64 * (1 - b), 64 * (1 - b) + 32)
                pairs = [(WORK[rows, 2 * t + b, q0:q0 + P], WORK[rows, 8 + t, 0:nk]),
                         (WORK[rope, 2 * t + b, q0:q0 + P], BIG[rope, 29, 0:nk])]
                return pairs, nk, H[rows, t, q0:q0 + P], t * P + HD * b
            pairs = [(BIG[rows, 8 + t, q0:q0 + P], BIG[rows, 12 + t, 0:nk])]
            return pairs, nk, H[rows, 4 + t, q0:q0 + P], t * P + HD * b

        score_bank = (pb[0], pb[1], pb[6])
        PROBS = WORK[:, 24:27, :]

        def attend_tensor(pe, a):
            which, u0 = ATTENTIONS[a], units_before(a)
            units = attention_units(which)
            n = len(units)
            pe.wait_ge(heads_ready, a + 1)
            pe.wait_ge(values_ready, a + 1)
            for it in range(n + 3):
                if it < n:
                    pairs, nk, _, _ = attention_operands(which, *units[it])
                    if it >= 3:
                        pe.wait_ge(probs_ready, u0 + it - 2)
                    for i, (q, k) in enumerate(pairs):
                        mm = pe.matmul(score_bank[it % 3][:, 0:nk], q, k, start=i == 0, stop=i == len(pairs) - 1)
                    mm.then_inc(scores_ready, 1)
                u = it - 2
                if 0 <= u < n:
                    nk = attention_operands(which, *units[u])[1]
                    pe.wait_ge(probs_scaled, u0 + u + 1)
                    if u >= 2:
                        pe.wait_ge(turned_copied, u0 + u - 1)
                    for i in range(nk // P):
                        mm = pe.transpose(pb[2 + u % 2][:, i * P:(i + 1) * P], PROBS[:, u % 3, i * P:(i + 1) * P],
                                          C("ident"))
                    mm.then_inc(probs_turned, 1)
                u = it - 3
                if 0 <= u < n:
                    _, nk, _, ch = attention_operands(which, *units[u])
                    b = units[u][1]
                    pe.wait_ge(turned_copied, u0 + u + 1)
                    if u >= 2:
                        pe.wait_ge(mixed_copied, u0 + u - 1)
                    for i in range(nk // P):
                        mm = pe.matmul(pb[4 + u % 2][HD * b:HD * b + HD, 0:P], WORK[:, 12 + i, ch:ch + HD],
                                       WORK[:, 22 + u % 2, i * P:(i + 1) * P], start=i == 0, stop=i == nk // P - 1)
                    mm.then_inc(mixed, 1)

        def attend_vector(dve, a):
            which, u0 = ATTENTIONS[a], units_before(a)
            units = attention_units(which)
            n = len(units)
            if which == "odd":
                dve.wait_ge(tables_loaded, 16 * 2)
            if which == "na":
                dve.wait_ge(tables_loaded, 16 * 4)
                dve.wait_ge(nab_loaded, 16)
            for it in range(n + 4):
                if it < n:
                    t, b, qt = units[it]
                    nk = attention_operands(which, t, b, qt)[1]
                    sc, st = score_bank[it % 3], stat[:, it % 3, :]
                    dve.wait_ge(scores_ready, u0 + it + 1)
                    if which in ("odd", "na"):
                        mask = TAB("wmask" if which == "odd" else "namask", (qt - 2) * TC, TC)
                        dve.tensor_tensor(sc[:, TC:T], sc[:, TC:T], mask, ALU.add)
                        dve.drain()
                    if which == "na":
                        bias = WORK[:, 0:8, :].rearrange("p a (b k) -> p (a b) k", k=TC)[:, it, :]
                        dve.tensor_tensor(sc[:, TC:T], sc[:, TC:T], bias, ALU.add)
                        dve.drain()
                    ins = dve.tensor_reduce(st[:, 0:1], sc[:, 0:nk], AX.X, ALU.max, negate=True)
                    if which == "odd":
                        dve.drain()
                        sink = V("sink", 8 * (t // 4) + 4 * b + t % 4)
                        ins = dve.scalar_tensor_tensor(out=st[:, 0:1], in0=sink, scalar=-1.0, in1=st[:, 0:1],
                                                       op0=ALU.mult, op1=ALU.min)
                        if qt == 3:
                            dve.drain()
                            ins = dve.tensor_scalar(st[:, 0:1], st[:, 0:1], 0.0, None, ALU.min)
                    ins.then_inc(max_ready, 1)
                u = it - 1
                if 0 <= u < n:
                    nk = attention_operands(which, *units[u])[1]
                    st, probs = stat[:, u % 3, :], PROBS[:, u % 3, 0:nk]
                    dve.wait_ge(probs_ready, u0 + u + 1)
                    if which == "odd":
                        dve.tensor_tensor(st[:, 1:2], st[:, 1:2], st[:, 2:3], ALU.add)
                        dve.drain()
                        if units[u][2] == 3:
                            dve.scalar_tensor_tensor(out=st[:, 1:2], in0=C("padkeys"), scalar=st[:, 4:5],
                                                     in1=st[:, 1:2], op0=ALU.mult, op1=ALU.add)
                            dve.drain()
                    dve.reciprocal(st[:, 3:4], st[:, 1:2])
                    dve.drain()
                    dve.tensor_scalar(probs, probs, st[:, 3:4], None, ALU.mult).then_inc(probs_scaled, 1)
                u = it - 4
                if 0 <= u < n:
                    b = units[u][1]
                    o = attention_operands(which, *units[u])[2]
                    dve.wait_ge(mixed, u0 + u + 1)
                    dve.tensor_copy(o, pb[4 + u % 2][HD * b:HD * b + HD, 0:P]).then_inc(mixed_copied, 1)
            if which == "odd":
                dve.drain().then_inc(mixer_ready, 1)

        def attend_scalar(act, a):
            which, u0 = ATTENTIONS[a], units_before(a)
            units = attention_units(which)
            n = len(units)
            for it in range(n + 2):
                if it < n:
                    t, b, qt = units[it]
                    nk = attention_operands(which, t, b, qt)[1]
                    st = stat[:, it % 3, :]
                    act.wait_ge(max_ready, u0 + it + 1)
                    if it >= 3:
                        act.wait_ge(probs_turned, u0 + it - 2)
                    if which == "odd":
                        act.activation(st[:, 2:3], V("sink", 8 * (t // 4) + 4 * b + t % 4), ACT.Exp, bias=st[:, 0:1])
                        if qt == 3:
                            act.activation(st[:, 4:5], st[:, 0:1], ACT.Exp)
                    act.activation(PROBS[:, it % 3, 0:nk], score_bank[it % 3][:, 0:nk], ACT.Exp, bias=st[:, 0:1],
                                   accum_out=st[:, 1:2]).then_inc(probs_ready, 1)
                u = it - 2
                if 0 <= u < n:
                    nk = attention_operands(which, *units[u])[1]
                    act.wait_ge(probs_turned, u0 + u + 1)
                    if u >= 2:
                        act.wait_ge(mixed, u0 + u - 1)
                    act.activation(WORK[:, 22 + u % 2, 0:nk], pb[2 + u % 2][:, 0:nk], ACT.Copy)\
                       .then_inc(turned_copied, 1)

        qk_squared, qk_summed, qk_rooted = sem("head_squared"), sem("head_squares_summed"), sem("head_rms_ready")
        qk_normed, qk_turned = sem("head_normed"), sem("head_rotated_half_ready")
        values_turned = sem("values_transposed")
        q_turned, q_rotated, k_turned = sem("query_half_ready"), sem("queries_rotated"), sem("key_half_ready")
        low_squared, low_summed, low_rooted = sem("low_rank_squared"), sem("low_rank_summed"), sem("low_rank_rms_ready")
        low_normed = sem("low_rank_normed")
        q_copied, k_copied, v_copied = sem("mla_query_copied"), sem("mla_key_copied"), sem("mla_value_copied")
        mq_turned, mq_rotated, mk_turned = sem("mla_query_half_ready"), sem("mla_queries_rotated"), sem("mla_key_half_ready")

        def rotate(dve, jobs, scale, scratch, turned):
            for i, (x, bank, cos, sin) in enumerate(jobs):
                tmp = scratch[:, i, :]
                dve.scalar_tensor_tensor(out=tmp[:, 0:TC], in0=x[:, TC:T], scalar=scale, in1=cos, op0=ALU.mult,
                                         op1=ALU.mult)
                dve.wait_ge(turned, i + 1)
                dve.scalar_tensor_tensor(out=tmp[:, TC:T], in0=bank[:, TC:T], scalar=scale, in1=sin, op0=ALU.mult,
                                         op1=ALU.mult)
            dve.drain()
            for i, (x, _, _, _) in enumerate(jobs):
                dve.tensor_tensor(x[:, TC:T], scratch[:, i, 0:TC], scratch[:, i, TC:T], ALU.add)

        def turn_values(pe, src, n, bank0):
            for tt in range(TT):
                for j in range(n):
                    mm = pe.transpose(pb[bank0 + tt][:, j * P:(j + 1) * P], src[:, j, tt * P:(tt + 1) * P], C("ident"))
            return mm

        def even_heads_scalar(act):
            all_copied(act, 0, 1)
            act.drain()
            for i in range(5):
                act.activation(WORK[:, i, :], BIG[:, i, :], ACT.Square).then_inc(qk_squared, 1)
            for i in range(5):
                act.wait_ge(qk_summed, i + 1)
                act.activation(WORK[:, i, :], pb[i][:, :], ACT.Sqrt, bias=epsb[:, 1:2] if i < 4 else epsb[:, 0:1],
                               scale=1.0 if i < 4 else 1.0 / HD).then_inc(qk_rooted, 1)
            act.wait_ge(values_turned, 1)
            act.activation(WORK[:, 12:16, 0:P], tiles(pb[5][:, :]), ACT.Copy).then_inc(values_ready, 1)

        def even_heads_tensor(pe):
            all_copied(pe, 0, 0)
            all_copied(pe, 0, 1)
            for i in range(5):
                pe.wait_ge(qk_squared, i + 1)
                pe.matmul(pb[i][:, :], C("blk"), WORK[:, i, :], start=True, stop=True).then_inc(qk_summed, 1)
            for tt in range(TT):
                mm = pe.transpose(pb[5][:, tt * P:(tt + 1) * P], BIG[:, 5, tt * P:(tt + 1) * P], C("ident"))
            mm.then_inc(values_turned, 1)
            for i in range(5):
                pe.wait_ge(qk_normed, i + 1)
                pe.matmul(pb[i][:, TC:T], C("rot"), BIG[:, i, TC:T], start=True, stop=True).then_inc(qk_turned, 1)

        def even_heads_vector(dve):
            for i in range(5):
                dve.wait_ge(qk_rooted, i + 1)
                dve.reciprocal(pb[i][:, :], WORK[:, i, :])
                dve.drain()
                dve.scalar_tensor_tensor(out=BIG[:, i, :], in0=BIG[:, i, :], scalar=V("qgain" if i < 4 else "kgain"),
                                         in1=pb[i][:, :], op0=ALU.mult, op1=ALU.mult).then_inc(qk_normed, 1)
            dve.drain()
            rotate(dve, [(BIG[:, i, :], pb[i], C("cosa"), C("sina")) for i in range(5)], 1.0, WORK[:, 0:5, :], qk_turned)
            dve.drain().then_inc(heads_ready, 1)

        def odd_heads_tensor(pe):
            all_copied(pe, 1, 0)
            all_copied(pe, 1, 1)
            for i in range(8):
                pe.matmul(pb[i][:, TC:T], C("rot"), BIG[:, i, TC:T], start=True, stop=True).then_inc(q_turned, 1)
            pe.wait_ge(q_rotated, 1)
            for i in range(2):
                pe.matmul(pb[i][:, TC:T], C("rot"), BIG[:, 8 + i, TC:T], start=True, stop=True).then_inc(k_turned, 1)
            turn_values(pe, BIG[:, 10:12, :], 2, 2).then_inc(values_turned, 1)

        def odd_heads_vector(dve):
            all_copied(dve, 1, 0)
            rotate(dve, [(BIG[:, i, :], pb[i], C("cosa"), C("sina")) for i in range(8)], HD ** -0.5, WORK[:, 0:8, :], q_turned)
            dve.drain().then_inc(q_rotated, 1)
            rotate(dve, [(BIG[:, 8 + i, :], pb[i], C("cosa"), C("sina")) for i in range(2)], 1.0, WORK[:, 0:2, :], k_turned)
            dve.drain().then_inc(heads_ready, 1)

        def odd_heads_scalar(act):
            act.wait_ge(values_turned, 2)
            for tt in range(TT):
                ins = act.activation(WORK[:, 12 + tt, 0:2 * P], pb[2 + tt][:, 0:2 * P], ACT.Copy)
            ins.then_inc(values_ready, 1)

        UP0 = SLAB_AT["mla_up"][0]

        def mla_heads_scalar(act):
            all_copied(act, 2, 1)
            act.drain()
            for i in range(5):
                act.activation(WORK[:, i, :], BIG[:, i, :], ACT.Square).then_inc(low_squared, 1)
            for i, n in enumerate((3, 2)):
                act.wait_ge(low_summed, i + 1)
                act.activation(WORK[:, 5 + i, :], pb[i][:, :], ACT.Sqrt, bias=epsb[:, 0:1], scale=1.0 / (n * P))\
                   .then_inc(low_rooted, 1)
            act.wait_ge(low_normed, 5)
            for h in range(8):
                act.wait_ge(slab_done, UP0 + h // 2 + 1)
                act.activation(WORK[:, h, :], pb[h][:, :], ACT.Copy, scale=96 ** -0.5).then_inc(q_copied, 1)
            act.wait_ge(slab_done, UP0 + 5)
            for t in range(4):
                act.activation(WORK[:, 8 + t, :], pb[t][:, :], ACT.Copy).then_inc(k_copied, 1)
            act.wait_ge(values_turned, 3)
            for tt in range(TT):
                ins = act.activation(WORK[:, 12 + tt, :], pb[4 + tt][:, :], ACT.Copy)
            ins.then_inc(values_ready, 1)

        def mla_heads_tensor(pe):
            all_copied(pe, 2, 0)
            all_copied(pe, 2, 1)
            for i in range(5):
                bank, first, last = (0, 0, 2) if i < 3 else (1, 3, 4)
                pe.wait_ge(low_squared, i + 1)
                mm = pe.matmul(pb[bank][:, :], C("ones"), WORK[:, i, :], start=i == first, stop=i == last)
                if i == last:
                    mm.then_inc(low_summed, 1)
            pe.wait_ge(low_normed, 3)
            for n in range(4):
                w = take(pe, UP0 + n)
                if n == 3:
                    pe.wait_ge(low_normed, 5)
                for j in range(2):
                    for i in range(3):
                        mm = pe.matmul(pb[2 * n + j][:, :], w[:, (3 * j + i) * P:(3 * j + i + 1) * P], BIG[:, i, :],
                                       start=i == 0, stop=i == 2)
                mm.then_inc(slab_done, 1)
            for n in range(2):
                w = take(pe, UP0 + 4 + n)
                pe.wait_ge(q_copied, 4 * n + 4)
                for t in range(4):
                    for i in range(2):
                        mm = pe.matmul(pb[4 * n + t][:, :], w[:, (2 * t + i) * P:(2 * t + i + 1) * P], BIG[:, 3 + i, :],
                                       start=i == 0, stop=i == 1)
                mm.then_inc(slab_done, 1)
            for h in range(8):
                pe.wait_ge(*((k_copied, h + 1) if h < 4 else (v_copied, h - 3)))
                pe.matmul(pb[h][:, TC:T], C("rotm"), WORK[:, h, TC:T], start=True, stop=True).then_inc(mq_turned, 1)
            pe.wait_ge(mq_rotated, 1)
            pe.matmul(pb[0][:, TC:T], C("rotm"), BIG[:, 29, TC:T], start=True, stop=True).then_inc(mk_turned, 1)
            turn_values(pe, WORK[:, 16:20, :], 4, 4).then_inc(values_turned, 1)

        def mla_heads_vector(dve):
            for i in range(2):
                dve.wait_ge(low_rooted, i + 1)
                dve.reciprocal(pb[6 + i][:, :], WORK[:, 5 + i, :])
            dve.drain()
            for i in range(5):
                dve.scalar_tensor_tensor(out=BIG[:, i, :], in0=BIG[:, i, :], scalar=V("qn", i) if i < 3 else V("kvn", i - 3),
                                         in1=pb[6 + i // 3][:, :], op0=ALU.mult, op1=ALU.mult).then_inc(low_normed, 1)
            dve.wait_ge(slab_done, UP0 + 6)
            for t in range(4):
                dve.tensor_copy(WORK[:, 16 + t, :], pb[4 + t][:, :]).then_inc(v_copied, 1)
            dve.wait_ge(q_copied, 8)
            dve.wait_ge(tables_loaded, 16 * 3)
            rotate(dve, [(WORK[:, h, :], pb[h], TAB("cosmo" if h % 2 else "cosme"),
                          TAB("sinmo" if h % 2 else "sinme"))
                         for h in range(8)], 1.0, WORK[:, 20:28, :], mq_turned)
            dve.drain().then_inc(mq_rotated, 1)
            rotate(dve, [(BIG[:, 29, :], pb[0], TAB("cosmk"), TAB("sinmk"))], 1.0, WORK[:, 20:21, :], mk_turned)
            dve.drain().then_inc(heads_ready, 1)

        def na_heads_gpsimd(pool):
            pool.wait_ge(modulated, 8 * KT)
            pool.dma_start(WORK[:, 0:8, :].rearrange("p a b -> p (a b)"), nabias).then_inc(nab_loaded, 16)

        def na_heads_tensor(pe):
            all_copied(pe, 3, 0)
            all_copied(pe, 3, 1)
            turn_values(pe, BIG[:, 16:20, :], 4, 0).then_inc(values_turned, 1)

        def na_heads_scalar(act):
            all_copied(act, 3, 1)
            act.drain()
            for i in (0, 1, 8, 9, 10, 11):
                ins = act.activation(BIG[:, i, TC:T], BIG[:, i, TC:T], ACT.Copy, scale=HD ** -0.5)
            ins.then_inc(heads_ready, 1)
            act.wait_ge(values_turned, 4)
            for tt in range(TT):
                ins = act.activation(WORK[:, 12 + tt, :], pb[tt][:, :], ACT.Copy)
            ins.then_inc(values_ready, 1)

        def add_neighbours(pool, x, y, before, after):
            from_before, from_after = WORK[:, 20, :], WORK[:, 21, :]
            pool.tensor_scalar(from_before, x, before, None, ALU.mult)
            pool.tensor_scalar(from_after, x, after, None, ALU.mult)
            pool.drain()
            y, from_before, from_after = (z.rearrange("p (s t) -> p s t", s=2) for z in (y, from_before, from_after))
            pool.tensor_tensor(y[:, :, 1:], y[:, :, 1:], from_before[:, :, :-1], ALU.add)
            pool.drain()
            pool.tensor_tensor(y[:, :, :-1], y[:, :, :-1], from_after[:, :, 1:], ALU.add)
            pool.drain()
        R_, K_, V_, WL, AL, GL = 5, 9, 13, 17, 18, 19
        KK = BIG[:, 0:4, :]
        EIT, FF = BIG[:, 20:24, :], BIG[:, 24:28, :]
        RR = WORK[:, 0:4, :]
        VTOK = WORK[:, 4:8, :]
        TOK = WORK[:, 8:11, :]
        SIG, CUM, AA, EX = (WORK[:, 11 + i, :] for i in range(4))
        FACTORS = [[WORK[:, 15 + i, :] for i in range(3)], [SPARE[:, i, :] for i in range(3)]]
        STATE = [tiles(WORK[:, 18 + i, 0:4 * HD], HD) for i in range(2)]
        MT, MB, TI, TTI, XS = ([WORK[:, 18 + 5 * hb + i, :] for hb in range(2)] for i in range(5))
        NGH = [BIG[:, 28 + hb, :] for hb in range(2)]
        shifted, ranks_ready = sem("tokens_shifted"), sem("low_ranks_ready")
        started_shift = sem("shift_of_first_features")
        SHIFTS_GPSIMD = 10
        kk_started = sem("removal_keys_before_norm")
        kk_squared, kk_summed, kk_rooted, kk_ready = (sem(f"removal_key_{x}") for x in ("squared", "summed", "rms", "ready"))
        v_turned = sem("rwkv_values_transposed")
        lora_ready, rates_ready = sem("decay_and_rate_products"), sem("decay_and_rate_ready")
        decay_summed, decays_ready = sem("log_decays_summed"), sem("decays_ready")
        factors_ready = sem("alpha_beta_kappa_rho_ready")
        factors_turned, factors_by_token = sem("factors_transposed"), sem("factors_by_token_ready")
        within_ready, triangles_ready = sem("alpha_beta_products"), sem("triangles_masked")
        t_started, level_masked = sem("inverse_started"), sem("level_mask_applied")
        x_ready, x_copied = sem("off_block_product_ready"), sem("off_block_product_copied")
        z_ready, t_updated = sem("inverse_update_ready"), sem("inverse_updated")
        mixes_ready, mixes_masked = sem("kappa_rho_products"), sem("kappa_rho_masked")
        kv_ready, rhs_ready = sem("kappa_alpha_values_ready"), sem("right_sides_ready")
        solved, solved_copied = sem("right_sides_solved"), sem("solutions_copied")
        group_ready, group_added, inputs_copied = sem("group_products"), sem("group_added"), sem("state_inputs_copied")
        step_ready, outputs_ready, state_ready = sem("state_products"), sem("state_outputs"), sem("state_ready")

        def wkv_features_gpsimd(pool):
            pool.wait_ge(values_turned, 1)
            for i in range(SHIFTS_GPSIMD):
                x, y = BIG[:, 6 + i, :], BIG[:, 5 + i, :]
                pool.tensor_scalar(y, x, mu_rest[:, i:i + 1], None, ALU.mult)
                add_neighbours(pool, x, y, V("mu", i), V("mu", 15 + i))
            pool.drain().then_inc(started_shift, 1)

        def wkv_features_vector(dve):
            dve.wait_ge(started_shift, 1)
            for i in range(SHIFTS_GPSIMD, 15):
                x, y = BIG[:, 6 + i, :], BIG[:, 5 + i, :]
                dve.tensor_scalar(y, x, mu_rest[:, i:i + 1], None, ALU.mult)
                dve.drain()
                for before in (True, False):
                    for a, b in (CTX, LAT):
                        to, of = (slice(a + 1, b), slice(a, b - 1)) if before else (slice(a, b - 1), slice(a + 1, b))
                        dve.scalar_tensor_tensor(out=y[:, to], in0=x[:, of], scalar=V("mu", i if before else 15 + i),
                                                 in1=y[:, to], op0=ALU.mult, op1=ALU.add)
                    dve.drain()
            dve.drain().then_inc(shifted, 1)
            for j in range(4):
                dve.tensor_scalar(KK[:, j, :], BIG[:, K_ + j, :], V("kk", j), None, ALU.mult)
            dve.drain().then_inc(kk_started, 1)
            dve.wait_ge(v_turned, 1)
            for tt in range(TT):
                dve.tensor_copy(VTOK[:, tt, :], pb[4 + tt][:, :])
            for j in range(4):
                dve.wait_ge(kk_rooted, j + 1)
                dve.reciprocal(WORK[:, 8 + j, :], WORK[:, 8 + j, :])
            dve.drain()
            for j in range(4):
                dve.tensor_tensor(KK[:, j, :], KK[:, j, :], WORK[:, 8 + j, :], ALU.mult)
            dve.drain().then_inc(kk_ready, 1)

        def wkv_features_scalar(act):
            act.wait_ge(shifted, 1)
            act.activation(BIG[:, WL, :], BIG[:, WL, :], ACT.Tanh)
            act.activation(BIG[:, GL, :], BIG[:, GL, :], ACT.Sigmoid).then_inc(ranks_ready, 1)
            act.wait_ge(kk_started, 1)
            for j in range(4):
                act.activation(WORK[:, 8 + j, :], KK[:, j, :], ACT.Square).then_inc(kk_squared, 1)
            for j in range(4):
                act.wait_ge(kk_summed, j + 1)
                act.activation(WORK[:, 8 + j, :], pb[j][:, :], ACT.Sqrt, bias=epsb[:, 0:1]).then_inc(kk_rooted, 1)

        def wkv_features_tensor(pe):
            pe.wait_ge(kk_started, 1)
            turn_values(pe, BIG[:, V_:V_ + 4, :], 4, 4).then_inc(v_turned, 1)
            for j in range(4):
                pe.wait_ge(kk_squared, j + 1)
                pe.matmul(pb[j][:, :], C("blk"), WORK[:, 8 + j, :], start=True, stop=True).then_inc(kk_summed, 1)

        NLEV = 2 * len(BLOCK_LEVELS)

        def chunk_order(d):
            return list(range(NCH)) if d == 0 else [3, 2, 1, 0, 7, 6, 5, 4]

        def heads_of(j):
            return [(hb, slice(HD * hb, HD * hb + HD), slice(j * P + hb * HD, j * P + hb * HD + HD)) for hb in (0, 1)]

        def tok(i):
            return slice(i * P, (i + 1) * P)

        def wkv_tensor(pe):
            pe.wait_ge(ranks_ready, 1)
            pe.wait_ge(kk_ready, 1)
            wkv_low_ranks(pe, 0)
            for d in range(2):
                for j in range(4):
                    wkv_group_tensor(pe, d, j, 4 * d + j)
                for s, c in enumerate(chunk_order(d)):
                    if s:
                        st = STATE[(s - 1) % 2]
                        pe.wait_ge(state_ready, NCH * d + s)
                        pairs = [(j, rows, slice(j * HD, (j + 1) * HD)) for j in range(4) for _, rows, _ in heads_of(j)]
                        cc = slice(c * HD, (c + 1) * HD)
                        if s < NCH - 1:
                            for j, rows, o in pairs:
                                mm = pe.matmul(pb[2 + s % 2][rows, o], EIT[rows, j, cc], st[rows, j, :], start=True, stop=True)
                            mm.then_inc(step_ready, 1)
                        for j, rows, o in pairs:
                            mm = pe.matmul(pb[s % 2][rows, o], st[rows, j, :], RR[rows, j, cc], start=True, stop=True)
                        mm.then_inc(outputs_ready, 1)

        def wkv_low_ranks(pe, g):
            low, j = slice(HD * (g // 4), HD * (g // 4) + HD), g % 4
            pe.matmul(pb[6][:, :], S("w2", low.start, low.stop, j * P, P), BIG[low, WL, :], start=True, stop=True)
            pe.matmul(pb[7][:, :], S("a2", low.start, low.stop, j * P, P), BIG[low, AL, :], start=True, stop=True)\
              .then_inc(lora_ready, 1)

        def wkv_group_tensor(pe, d, j, g):
            AL_, BE_, KA_ = FACTORS[g % 2]
            pe.wait_ge(factors_ready, g + 1)
            if g:
                pe.wait_ge(inputs_copied, g)
                pe.wait_ge(group_added, g)
            for i, x in enumerate((AL_, BE_, KA_)):
                for tt in range(TT):
                    mm = pe.transpose(pb[i][:, tok(tt)], x[:, tok(tt)], C("ident"))
            mm.then_inc(factors_turned, 1)
            for hb, rows, _ in heads_of(j):
                for tt in range(TT):
                    pe.matmul(pb[4 + hb][:, tok(tt)], BE_[rows, tok(tt)], AL_[rows, tok(tt)], start=True, stop=True)
                for tt in range(TT):
                    mm = pe.matmul(pb[6 + hb][:, tok(tt)], AL_[rows, tok(tt)], BE_[rows, tok(tt)], start=True, stop=True)
                mm.then_inc(within_ready, 1)
            pe.wait_ge(factors_by_token, g + 1)
            for li in range(len(BLOCK_LEVELS)):
                for hb in range(2):
                    q = NLEV * g + 2 * li + hb
                    pe.wait_ge(level_masked, q + 1)
                    if li:
                        pe.wait_ge(t_updated, q - 1)
                    else:
                        pe.wait_ge(t_started, 2 * g + hb + 1)
                    for tt in range(TT):
                        mm = pe.matmul(pb[hb][:, tok(tt)], MB[hb][:, tok(tt)], TI[hb][:, tok(tt)], start=True, stop=True)
                    mm.then_inc(x_ready, 1)
                if li == 0 and g < 7:
                    wkv_low_ranks(pe, g + 1)
                for hb in range(2):
                    q = NLEV * g + 2 * li + hb
                    pe.wait_ge(x_copied, q + 1)
                    for tt in range(TT):
                        pe.matmul(pb[2 + hb][:, tok(tt)], TTI[hb][:, tok(tt)], XS[hb][:, tok(tt)], start=True, stop=True)
                    for tt in range(TT):
                        mm = pe.matmul(pb[4 + hb][:, tok(tt)], XS[hb][:, tok(tt)], TTI[hb][:, tok(tt)], start=True,
                                       stop=True)
                    mm.then_inc(z_ready, 1)
            for hb, rows, _ in heads_of(j):
                pe.wait_ge(t_updated, NLEV * (g + 1) - 1 + hb)
                for tt in range(TT):
                    pe.matmul(pb[hb][:, tok(tt)], KA_[rows, tok(tt)], AL_[rows, tok(tt)], start=True, stop=True)
                for tt in range(TT):
                    pe.matmul(pb[2 + hb][:, tok(tt)], KA_[rows, tok(tt)], RR[rows, j, tok(tt)], start=True, stop=True)
                for tt in range(TT):
                    mm = pe.matmul(pb[4 + hb][:, tok(tt)], BE_[rows, tok(tt)], RR[rows, j, tok(tt)], start=True, stop=True)
                mm.then_inc(mixes_ready, 1)
            if g < 7:
                pe.wait_ge(rates_ready, g + 2)
            for hb, _, ch in heads_of(j):
                pe.wait_ge(mixes_masked, 2 * g + hb + 1)
                for tt in range(TT):
                    mm = pe.matmul(pb[6 + hb][:, tt * HD:(tt + 1) * HD], MB[hb][:, tok(tt)], VTOK[:, tt, ch], start=True,
                                   stop=True)
                mm.then_inc(kv_ready, 1)
            for hb in range(2):
                pe.wait_ge(rhs_ready, 2 * g + hb + 1)
                for tt in range(TT):
                    mm = pe.matmul(pb[hb][:, tok(tt)], TTI[hb][:, tok(tt)], TI[hb][:, tok(tt)], start=True, stop=True)
                mm.then_inc(solved, 1)
            for hb, rows, ch in heads_of(j):
                pe.wait_ge(solved_copied, 2 * g + hb + 1)
                gh = tiles(NGH[hb])
                for tt in range(TT):
                    pe.matmul(pb[2][rows, tok(tt)], gh[:, tt, 0:HD], MT[hb][:, tok(tt)], start=True, stop=True)
                for tt in range(TT):
                    pe.matmul(pb[3][rows, tok(tt)], VTOK[:, tt, ch], XS[hb][:, tok(tt)], start=True, stop=False)
                    pe.matmul(pb[3][rows, tok(tt)], gh[:, tt, HD:P], MT[hb][:, tok(tt)], start=False, stop=True)
                for half in range(2):
                    tr = slice(HD * half, HD * half + HD)
                    for tt in range(TT):
                        o = slice(tt * HD, (tt + 1) * HD)
                        hc = slice(tt * P + HD * hb, tt * P + HD * hb + HD)
                        pe.matmul(pb[4 + 2 * half][rows, o], gh[tr, tt, 0:HD], TOK[tr, 1, hc], start=True, stop=True)
                        pe.matmul(pb[5 + 2 * half][rows, o], TOK[tr, 2, hc], VTOK[tr, tt, ch], start=True, stop=False)
                        mm = pe.matmul(pb[5 + 2 * half][rows, o], TOK[tr, 1, hc], gh[tr, tt, HD:P], start=False, stop=True)
            mm.then_inc(group_ready, 1)

        def wkv_scalar(act):
            act.wait_ge(kk_ready, 1)

            def rates(g):
                act.wait_ge(lora_ready, g + 1)
                act.activation(SIG, pb[6][:, :], ACT.Sigmoid, bias=V("w0", g))
                act.activation(AA, pb[7][:, :], ACT.Sigmoid, bias=V("a0", g)).then_inc(rates_ready, 1)

            def decays(g):
                AL_, _, KA_ = FACTORS[g % 2]
                act.wait_ge(decay_summed, g + 1)
                act.activation(AL_, SIG, ACT.Exp, scale=-DECAY_C)
                act.activation(EX, CUM, ACT.Exp, scale=-DECAY_C)
                act.activation(KA_, CUM, ACT.Exp, scale=DECAY_C).then_inc(decays_ready, 1)

            rates(0)
            decays(0)
            for g in range(8):
                j = g % 4
                act.wait_ge(factors_turned, g + 1)
                for i in range(3):
                    ins = act.activation(TOK[:, i, :], pb[i][:, :], ACT.Copy)
                ins.then_inc(factors_by_token, 1)
                for li in range(len(BLOCK_LEVELS)):
                    for hb in range(2):
                        act.wait_ge(x_ready, NLEV * g + 2 * li + hb + 1)
                        act.activation(XS[hb], pb[hb][:, :], ACT.Copy).then_inc(x_copied, 1)
                    if g < 7 and li == 0:
                        rates(g + 1)
                    if g < 7 and li == 2:
                        decays(g + 1)
                for hb in range(2):
                    act.wait_ge(t_updated, NLEV * (g + 1) - 1 + hb)
                    act.activation(tiles(TI[hb])[:, :, 0:HD], tiles(TOK[:, 0, :])[:, :, HD * hb:HD * hb + HD], ACT.Copy)
                for hb in range(2):
                    act.wait_ge(kv_ready, 2 * g + hb + 1)
                    act.activation(tiles(TI[hb])[:, :, HD:P], tiles(pb[6 + hb][:, 0:TT * HD], HD), ACT.Copy)\
                       .then_inc(rhs_ready, 1)
                for hb in range(2):
                    act.wait_ge(solved, 2 * g + hb + 1)
                    act.activation(NGH[hb], pb[hb][:, :], ACT.Copy, scale=-1.0).then_inc(solved_copied, 1)
                act.wait_ge(group_ready, g + 1)
                for half in range(2):
                    f = FF[:, j, :].rearrange("p (t h v) -> p t h v", h=2, v=HD)[:, :, half, :]
                    ins = act.activation(f, tiles(pb[5 + 2 * half][:, 0:TT * HD], HD), ACT.Copy)
                ins.then_inc(inputs_copied, 1)

        def wkv_gpsimd(pool):
            wkv_factors(pool, 0)
            for g in range(8):
                for li, b in enumerate(BLOCK_LEVELS):
                    mask = C("mu" if g < 4 else "ml", LEVELS.index(b) * P, P)
                    for hb in range(2):
                        if li:
                            pool.wait_ge(x_ready, NLEV * g + 2 * li + hb - 1)
                        else:
                            pool.wait_ge(triangles_ready, 2 * g + hb + 1)
                        pool.tensor_tensor(tiles(MB[hb]), tiles(MT[hb]), over(mask, TT), ALU.mult)\
                            .then_inc(level_masked, 1)
                if g < 7:
                    wkv_factors(pool, g + 1)

        def wkv_factors(pool, g):
            d, j = g // 4, g % 4
            AL_, BE_, KA_ = FACTORS[g % 2]
            if g == 0:
                pool.wait_ge(kk_ready, 1)
            pool.wait_ge(rates_ready, g + 1)
            pool.tensor_tensor(BE_, KK[:, j, :], AA, ALU.mult)
            pool.drain()
            pool.tensor_scalar(AA, AA, V("ka", j), omka[:, j:j + 1], ALU.mult, ALU.add)
            pool.drain()
            pool.tensor_tensor(AA, AA, BIG[:, K_ + j, :], ALU.mult)
            pool.drain()
            pool.wait_ge(decays_ready, g + 1)
            pool.tensor_tensor(AL_, AL_, KK[:, j, :], ALU.mult)
            pool.tensor_tensor(BE_, BE_, KA_, ALU.mult)
            pool.drain()
            pool.tensor_tensor(KA_, KA_, AA, ALU.mult)
            pool.tensor_copy(wstat[:, d, j, :], EX[:, (CHUNK - 1 if d == 0 else 0)::CHUNK])
            if g == 4:
                pool.wait_ge(state_ready, NCH)
            pool.tensor_tensor(RR[:, j, :], BIG[:, R_ + j, :], EX, ALU.mult).then_inc(factors_ready, 1)

        def wkv_vector(dve):
            dve.wait_ge(tables_loaded, 16)
            wkv_decay_sums(dve, 0)
            for d in range(2):
                for j in range(4):
                    wkv_group_vector(dve, d, j, 4 * d + j)
                for s, c in enumerate(chunk_order(d)):
                    st = STATE[s % 2]
                    cc = slice(c * HD, (c + 1) * HD)
                    decay = along(wstat[:, d, :, c:c + 1].rearrange("p j o -> p (j o)"), HD)
                    if s == 0:
                        dve.wait_ge(inputs_copied, 4 * d + 4)
                        dve.tensor_tensor(st, FF[:, :, cc], decay, ALU.mult)
                    elif s < NCH - 1:
                        dve.wait_ge(step_ready, (NCH - 2) * d + s)
                        dve.tensor_tensor(st, FF[:, :, cc], tiles(pb[2 + s % 2][:, 0:4 * HD], HD), ALU.add)
                        dve.drain()
                        dve.tensor_tensor(st, st, decay, ALU.mult)
                    if s < NCH - 1:
                        dve.drain().then_inc(state_ready, 1)
                    if s:
                        dve.wait_ge(outputs_ready, (NCH - 1) * d + s)
                        y = H[:, 4:8, cc]
                        dve.tensor_tensor(y, y, tiles(pb[s % 2][:, 0:4 * HD], HD), ALU.add)
                dve.drain().then_inc(state_ready, 1)

        def wkv_decay_sums(dve, g):
            step = 1 if g < 4 else -1
            dve.wait_ge(rates_ready, g + 1)
            dve.tensor_tensor_scan(CUM[:, ::step], TAB("reset"), SIG[:, ::step], 0.0, ALU.mult, ALU.add)
            dve.drain()
            dve.tensor_tensor(SIG, CUM, SIG, ALU.subtract).then_inc(decay_summed, 1)

        def wkv_group_vector(dve, d, j, g):
            strict, incl = C("su" if d == 0 else "sl"), C("iu" if d == 0 else "il")
            one, one_t = (C("ml", 0, P), C("mu", 0, P)) if d == 0 else (C("mu", 0, P), C("ml", 0, P))
            for hb in range(2):
                dve.wait_ge(within_ready, 2 * g + hb + 1)
                dve.tensor_tensor(tiles(MT[hb]), tiles(pb[4 + hb][:, :]), over(strict, TT), ALU.mult)\
                   .then_inc(triangles_ready, 1)
                dve.tensor_tensor(tiles(TI[hb]), tiles(pb[6 + hb][:, :]), over(one, TT), ALU.mult)
                dve.drain()
                dve.tensor_tensor(tiles(TTI[hb]), tiles(MT[hb]), over(one_t, TT), ALU.mult)
                dve.tensor_tensor(tiles(TI[hb]), over(C("ident"), TT), tiles(TI[hb]), ALU.subtract)
                dve.drain()
                dve.tensor_tensor(tiles(TTI[hb]), over(C("ident"), TT), tiles(TTI[hb]), ALU.subtract).then_inc(t_started, 1)
            for li in range(len(BLOCK_LEVELS)):
                for hb in range(2):
                    dve.wait_ge(z_ready, NLEV * g + 2 * li + hb + 1)
                    dve.tensor_tensor(TI[hb], TI[hb], pb[2 + hb][:, :], ALU.subtract)
                    dve.tensor_tensor(TTI[hb], TTI[hb], pb[4 + hb][:, :], ALU.subtract).then_inc(t_updated, 1)
                if g < 7 and li == 1:
                    wkv_decay_sums(dve, g + 1)
            for hb in range(2):
                dve.wait_ge(mixes_ready, 2 * g + hb + 1)
                dve.tensor_tensor(tiles(MB[hb]), tiles(pb[hb][:, :]), over(strict, TT), ALU.mult)
                dve.tensor_tensor(tiles(XS[hb]), tiles(pb[2 + hb][:, :]), over(incl, TT), ALU.mult)
                dve.tensor_tensor(tiles(MT[hb]), tiles(pb[4 + hb][:, :]), over(incl, TT), ALU.mult)\
                   .then_inc(mixes_masked, 1)
            dve.wait_ge(group_ready, g + 1)
            dve.tensor_tensor(RR[:, j, :], RR[:, j, :], pb[2][:, :], ALU.add)
            if d == 0:
                dve.tensor_copy(H[:, 4 + j, :], pb[3][:, :])
            else:
                dve.tensor_tensor(H[:, 4 + j, :], H[:, 4 + j, :], pb[3][:, :], ALU.add)
            for half in range(2):
                e = EIT[:, j, :].rearrange("p (t h k) -> p t h k", h=2, k=HD)[:, :, half, :]
                ins = dve.tensor_tensor(e, tiles(pb[4 + 2 * half][:, 0:TT * HD], HD), over(TAB("ident64"), TT), ALU.add)
            ins.then_inc(group_added, 1)

        y_summed, y_centred, y_squared = sem("output_summed"), sem("output_centred"), sem("output_squared")
        var_summed, y_rooted = sem("output_squares_summed"), sem("output_deviation_ready")
        bonus_summed, out_gate_ready = sem("bonus_summed"), sem("output_gate_ready")

        def wkv_readout_tensor(pe):
            pe.wait_ge(state_ready, 2 * NCH)
            for j in range(4):
                pe.matmul(pb[j][:, :], C("blk"), H[:, 4 + j, :], start=True, stop=True).then_inc(y_summed, 1)
            for j in range(4):
                mm = pe.matmul(pb[4 + j][:, :], S("g2", 0, P, j * P, P), BIG[:, GL, :], start=True, stop=True)
            mm.then_inc(out_gate_ready, 1)
            for j in range(4):
                pe.wait_ge(y_squared, j + 1)
                pe.matmul(pb[j][:, :], C("blk"), WORK[:, j, :], start=True, stop=True).then_inc(var_summed, 1)
            for j in range(4):
                pe.wait_ge(y_rooted, j + 1)
                pe.matmul(pb[j][:, :], C("blk"), WORK[:, 4 + j, :], start=True, stop=True).then_inc(bonus_summed, 1)

        def wkv_readout_scalar(act):
            for j in range(4):
                act.wait_ge(y_centred, j + 1)
                act.activation(WORK[:, j, :], H[:, 4 + j, :], ACT.Square).then_inc(y_squared, 1)
            for j in range(4):
                act.wait_ge(var_summed, j + 1)
                act.activation(WORK[:, j, :], pb[j][:, :], ACT.Sqrt, bias=epsb[:, 2:3], scale=1.0 / HD)\
                   .then_inc(y_rooted, 1)

        def wkv_readout_vector(dve):
            for j in range(4):
                dve.scalar_tensor_tensor(out=WORK[:, 4 + j, :], in0=BIG[:, R_ + j, :], scalar=V("rk", j),
                                         in1=BIG[:, K_ + j, :], op0=ALU.mult, op1=ALU.mult)
                dve.wait_ge(y_summed, j + 1)
                dve.scalar_tensor_tensor(out=H[:, 4 + j, :], in0=pb[j][:, :], scalar=-1.0 / HD, in1=H[:, 4 + j, :],
                                         op0=ALU.mult, op1=ALU.add).then_inc(y_centred, 1)
            for j in range(4):
                dve.wait_ge(y_rooted, j + 1)
                dve.reciprocal(WORK[:, j, :], WORK[:, j, :])
            dve.drain()
            for j in range(4):
                dve.scalar_tensor_tensor(out=H[:, 4 + j, :], in0=H[:, 4 + j, :], scalar=V("gnw", j), in1=WORK[:, j, :],
                                         op0=ALU.mult, op1=ALU.mult)
            dve.drain()
            for j in range(4):
                dve.wait_ge(bonus_summed, j + 1)
                dve.tensor_tensor(WORK[:, j, :], BIG[:, V_ + j, :], pb[j][:, :], ALU.mult)
            dve.drain()
            for j in range(4):
                dve.scalar_tensor_tensor(out=H[:, 4 + j, :], in0=H[:, 4 + j, :], scalar=V("gnb", j), in1=WORK[:, j, :],
                                         op0=ALU.add, op1=ALU.add)
            dve.drain()
            dve.wait_ge(out_gate_ready, 1)
            for j in range(4):
                dve.tensor_tensor(H[:, 4 + j, :], H[:, 4 + j, :], pb[4 + j][:, :], ALU.mult)
            dve.drain().then_inc(mixer_ready, 1)

        MVTOK = WORK[:, 0:4, :]
        ROWS = 64
        IGR, LFR, BCR, MMR, AR, RBR = (WORK[0:ROWS, 4 + i, :] for i in range(6))
        ACOL = WORK[:, 10, 0:TT * ROWS].rearrange("p (t r) -> p t r", r=ROWS)
        TMP1, LOGS, RD = WORK[0:ROWS, 11, :], WORK[0:ROWS, 12, :], WORK[:, 13, :]
        WGT = [WORK[:, 14:18, :], WORK[:, 22:26, :]]
        DEN, EM = [WORK[:, 18, :], WORK[:, 19, :]], [WORK[:, 26, :], WORK[:, 27, :]]
        SELROW = WORK[0:ROWS, 20:22, :].rearrange("p a (b c) -> p (a b) c", c=P)
        conv_ready, conv_silu = sem("convolution_ready"), sem("convolution_silu")
        mv_turned, mv_ready = sem("mlstm_values_transposed"), sem("mlstm_values_by_token_ready")
        gates_summed, gates_biased, gates_logged = sem("mlstm_gates_gathered"), sem("mlstm_gates_biased"), sem("mlstm_gates_logged")
        stabilised = sem("mlstm_stabiliser_ready")
        acol_turned, acol_ready = sem("mlstm_key_terms_transposed"), sem("mlstm_key_terms_ready")
        rows_spread, qk_ready = sem("mlstm_query_terms_spread"), sem("mlstm_scores_ready")
        rd_ready, exps_ready = sem("mlstm_diagonal_masked"), sem("mlstm_weights_exponential")
        weights_ready, sums_ready = sem("mlstm_weights_ready"), sem("mlstm_sums_ready")
        den_ready, unit_done = sem("mlstm_denominator_ready"), sem("mlstm_unit_done")

        def place_of(d, tile):
            return tile if d == 0 else (1, 0, 3, 2)[tile]

        def later_runs(d, si):
            later = [t for t in range(TT) if place_of(d, t) > place_of(d, si)]
            runs = []
            for t in later:
                if runs and runs[-1][1] == t:
                    runs[-1][1] = t + 1
                else:
                    runs.append([t, t + 1])
            return runs

        UNITS = [(d, h) for h in range(4) for d in range(2)]

        def mlstm_gpsimd(pool):
            pool.wait_ge(heads_ready, 3)
            for i in range(8):
                pool.tensor_scalar(SPARE[:, i, :], BIG[:, 5 + i, :], V("cw", 8 + i), V("cb", i), ALU.mult, ALU.add)
                add_neighbours(pool, BIG[:, 5 + i, :], SPARE[:, i, :], V("cw", i), V("cw", 16 + i))
            pool.drain().then_inc(conv_ready, 1)

        def mlstm_vector(dve):
            dve.wait_ge(gates_biased, 1)
            dve.tensor_scalar(LFR, pb[5][0:ROWS, :], vec[0:ROWS, VO["bf"][0]:VO["bf"][0] + 1], 0.0, ALU.add, ALU.min)
            dve.wait_ge(gates_logged, 1)
            dve.drain()
            dve.tensor_tensor(LFR, LFR, LOGS, ALU.subtract)
            dve.memset(RD[0:ROWS, :], 1.0)
            dve.drain()
            ones = RD[0:32, :]
            lf, ig, bc, mm = (x[0:32, :] for x in (LFR, IGR, BCR, MMR))
            dve.tensor_tensor_scan(bc, ones, lf, 0.0, ALU.mult, ALU.add)
            dve.tensor_tensor_scan(mm, lf, ig, 0.0, ALU.add, ALU.max)
            ones = RD[32:64, 0:TC]
            c, l = ([x[32:64, a:b] for x in (LFR, IGR, BCR, MMR)] for a, b in (CTX, LAT))
            dve.tensor_tensor_scan(c[2][:, ::-1], ones, c[0][:, ::-1], 0.0, ALU.mult, ALU.add)
            dve.tensor_tensor_scan(c[3][:, ::-1], c[0][:, ::-1], c[1][:, ::-1], 0.0, ALU.add, ALU.max)
            dve.drain()
            dve.tensor_tensor_scan(l[2][:, ::-1], ones, l[0][:, ::-1], c[2][:, 0:1], ALU.mult, ALU.add)
            dve.tensor_tensor_scan(l[3][:, ::-1], l[0][:, ::-1], l[1][:, ::-1], c[3][:, 0:1], ALU.add, ALU.max)
            dve.drain()
            dve.tensor_tensor(AR, IGR, BCR, ALU.subtract)
            dve.tensor_tensor(RBR, BCR, MMR, ALU.subtract)
            for d in range(2):
                dve.tensor_copy(SELROW[:, 4 * d:4 * d + 4, :], along(C("ident", 32 * d, 4)[0:ROWS, :], P))
            dve.drain().then_inc(stabilised, 1)
            for u in range(len(UNITS) + 1):
                if u < len(UNITS):
                    d, h = UNITS[u]
                    dve.wait_ge(rows_spread, u + 1)
                    dve.tensor_tensor(tiles(RD), tiles(pb[0][:, :]), over(C("nu" if d == 0 else "nl"), TT), ALU.add)\
                       .then_inc(rd_ready, 1)
                    dve.wait_ge(exps_ready, u + 1)
                    dve.wait_ge(qk_ready, u + 1)
                    for si in range(TT):
                        for a, b in [[si, si + 1]] + later_runs(d, si):
                            w = WGT[u % 2][:, si, a * P:b * P]
                            ins = dve.scalar_tensor_tensor(out=w, in0=pb[2 + si][:, a * P:b * P], scalar=P ** -0.5, in1=w,
                                                           op0=ALU.mult, op1=ALU.mult)
                    ins.then_inc(weights_ready, 1)
                if u:
                    d, h = UNITS[u - 1]
                    den = DEN[(u - 1) % 2]
                    dve.wait_ge(den_ready, u)
                    dve.tensor_tensor(den, den, EM[(u - 1) % 2], ALU.max)
                    dve.drain()
                    dve.reciprocal(den, den)
                    dve.drain()
                    if d == 0:
                        dve.tensor_tensor(H[:, 4 + h, :], den, pb[6][:, :], ALU.mult).then_inc(unit_done, 1)
                    else:
                        dve.tensor_tensor(den, den, pb[6][:, :], ALU.mult)
                        dve.drain()
                        dve.tensor_tensor(H[:, 4 + h, :], H[:, 4 + h, :], den, ALU.add).then_inc(unit_done, 1)

        def mlstm_scalar(act):
            act.wait_ge(conv_ready, 1)
            for i in range(8):
                act.activation(BIG[:, 5 + i, :], SPARE[:, i, :], ACT.Silu).then_inc(conv_silu, 1)
            act.wait_ge(gates_summed, 1)
            act.activation(IGR, pb[4][0:ROWS, :], ACT.Identity, bias=vec[0:ROWS, VO["bi"][0]:VO["bi"][0] + 1])
            act.activation(TMP1, pb[5][0:ROWS, :], ACT.Abs, bias=vec[0:ROWS, VO["bf"][0]:VO["bf"][0] + 1])\
               .then_inc(gates_biased, 1)
            act.drain()
            act.activation(TMP1, TMP1, ACT.Exp, scale=-1.0)
            act.drain()
            act.activation(LOGS, TMP1, ACT.Ln, bias=1.0).then_inc(gates_logged, 1)
            act.wait_ge(mv_turned, 1)
            for tt in range(TT):
                ins = act.activation(MVTOK[:, tt, :], pb[tt][:, :], ACT.Copy)
            ins.then_inc(mv_ready, 1)
            act.wait_ge(acol_turned, 1)
            act.activation(ACOL, tiles(pb[0][:, 0:TT * ROWS], ROWS), ACT.Copy).then_inc(acol_ready, 1)
            act.drain()
            for u in range(len(UNITS) + 1):
                if u < len(UNITS):
                    d, h = UNITS[u]
                    row = 32 * d + h
                    act.wait_ge(rows_spread, u + 1)
                    if u >= 2:
                        act.wait_ge(unit_done, u - 1)
                    act.activation(EM[u % 2], pb[1][:, :], ACT.Exp, scale=-1.0)
                    act.wait_ge(rd_ready, u + 1)
                    for si in range(TT):
                        s = slice(si * P, (si + 1) * P)
                        ins = act.activation(WGT[u % 2][:, si, s], RD[:, s], ACT.Exp, bias=ACOL[:, si, row:row + 1])
                        for a, b in later_runs(d, si):
                            ins = act.activation(WGT[u % 2][:, si, a * P:b * P], pb[0][:, a * P:b * P], ACT.Exp,
                                                 bias=ACOL[:, si, row:row + 1])
                    ins.then_inc(exps_ready, 1)
                if u:
                    act.wait_ge(sums_ready, u)
                    act.activation(DEN[(u - 1) % 2], pb[7][:, :], ACT.Abs).then_inc(den_ready, 1)

        def mlstm_tensor(pe):
            pe.wait_ge(mixed_copied, units_before(3))
            pe.matmul(pb[4][0:ROWS, :], C("sel_i"), BIG[:, 29, :], start=True, stop=True)
            pe.matmul(pb[5][0:ROWS, :], C("sel_f"), BIG[:, 29, :], start=True, stop=True).then_inc(gates_summed, 1)
            turn_values(pe, BIG[:, 13:17, :], 4, 0).then_inc(mv_turned, 1)
            pe.wait_ge(mv_ready, 1)
            pe.wait_ge(stabilised, 1)
            for tt in range(TT):
                mm = pe.transpose(pb[0][:, tt * ROWS:(tt + 1) * ROWS], AR[:, tt * P:(tt + 1) * P],
                                  C("ident")[0:ROWS, 0:ROWS])
            mm.then_inc(acol_turned, 1)
            pe.wait_ge(acol_ready, 1)
            pe.wait_ge(conv_silu, 8)
            for u in range(len(UNITS) + 1):
                if u < len(UNITS):
                    d, h = UNITS[u]
                    if u:
                        pe.wait_ge(weights_ready, u)
                    sel = SELROW[:, 4 * d + h, :]
                    pe.matmul(pb[0][:, :], sel, RBR, start=True, stop=True)
                    pe.matmul(pb[1][:, :], sel, MMR, start=True, stop=True).then_inc(rows_spread, 1)
                    for si in range(TT):
                        for a, b in [[si, si + 1]] + later_runs(d, si):
                            mm = pe.matmul(pb[2 + si][:, a * P:b * P], BIG[:, 9 + h, si * P:(si + 1) * P],
                                           BIG[:, 5 + h, a * P:b * P], start=True, stop=True)
                    mm.then_inc(qk_ready, 1)
                if u:
                    d, h = UNITS[u - 1]
                    pe.wait_ge(weights_ready, u)
                    if u >= 2:
                        pe.wait_ge(unit_done, u - 1)
                    for t in range(TT):
                        earlier = [s for s in range(TT) if place_of(d, s) <= place_of(d, t)]
                        for bank in (6, 7):
                            for s in earlier:
                                mm = pe.matmul(pb[bank][:, t * P:(t + 1) * P],
                                               MVTOK[:, s, h * P:(h + 1) * P] if bank == 6 else C("ones"),
                                               WGT[(u - 1) % 2][:, s, t * P:(t + 1) * P], start=s == earlier[0],
                                               stop=s == earlier[-1])
                    mm.then_inc(sums_ready, 1)

        READOUTS = [(4, 17, 21, ALL, "mn"), (0, None, 20, LAT, "gln")]
        gates_ready, out_gated = sem("readout_gates_ready"), sem("readout_heads_gated")
        out_squared, out_summed, out_rooted = (sem(f"readout_{x}") for x in ("squared", "summed", "rms_ready"))

        def readout_scalar(act, k):
            h0, o0, z0, (a, b), _ = READOUTS[k]
            if o0 is not None:
                for h in range(4):
                    act.activation(BIG[:, o0 + h, a:b], BIG[:, o0 + h, a:b], ACT.Sigmoid)
            for i in range(KT):
                ins = act.activation(BIG[:, z0 + i, a:b], BIG[:, z0 + i, a:b], ACT.Silu)
            ins.then_inc(gates_ready, 1)
            act.wait_ge(out_gated, k + 1)
            for h in range(4):
                act.activation(WORK[:, h, a:b], H[:, h0 + h, a:b], ACT.Square).then_inc(out_squared, 1)
            for h in range(4):
                act.wait_ge(out_summed, 4 * k + h + 1)
                act.activation(WORK[:, h, a:b], pb[h][:, a:b], ACT.Sqrt, bias=epsb[:, 0:1], scale=1.0 / P)\
                   .then_inc(out_rooted, 1)

        def readout_tensor(pe, k):
            a, b = READOUTS[k][3]
            for h in range(4):
                pe.wait_ge(out_squared, 4 * k + h + 1)
                pe.matmul(pb[h][:, a:b], C("ones"), WORK[:, h, a:b], start=True, stop=True).then_inc(out_summed, 1)

        def readout_vector(dve, k):
            h0, o0, z0, (a, b), gain = READOUTS[k]
            dve.wait_ge(gates_ready, k + 1)
            dve.drain()
            if o0 is not None:
                for h in range(4):
                    dve.tensor_tensor(H[:, h0 + h, a:b], H[:, h0 + h, a:b], BIG[:, o0 + h, a:b], ALU.mult)
            dve.drain().then_inc(out_gated, 1)
            for h in range(4):
                dve.wait_ge(out_rooted, 4 * k + h + 1)
                dve.reciprocal(WORK[:, h, a:b], WORK[:, h, a:b])
            dve.drain()
            for h in range(4):
                dve.scalar_tensor_tensor(out=H[:, h0 + h, a:b], in0=H[:, h0 + h, a:b], scalar=V(gain, h),
                                         in1=WORK[:, h, a:b], op0=ALU.mult, op1=ALU.mult)
            dve.drain()
            for i in range(KT):
                dve.tensor_tensor(H[:, i, a:b], H[:, i, a:b], BIG[:, z0 + i, a:b], ALU.mult)
            dve.drain().then_inc(mixer_ready, 1)

        GVTOK = WORK[:, 0:4, :]
        LGT, BSUM, TMP2, ONES_ROW = WORK[:, 4, :], WORK[:, 5, :], WORK[:, 6, :], WORK[:, 7, :]
        QC2 = [WORK[:, 8, :], WORK[:, 20, :]]
        QL2 = [WORK[:, a:a + 4, :].rearrange("p a (b t) -> p (a b) t", t=TC) for a in (9, 21)]
        PART = WORK[:, 13:17, :]
        NEAR2, FAR2 = [WORK[:, a, 0:TC] for a in (17, 26)], [WORK[:, a, TC:TC + P] for a in (17, 26)]
        CTXA2 = [WORK[:, a, :] for a in (18, 25)]
        GLA_LEVELS = LEVELS + (P,)
        gv_turned, gv_ready = sem("gla_values_transposed"), sem("gla_values_by_token_ready")
        forget_ready, forget_logged = sem("gla_gate_product"), sem("gla_gate_logged")
        spans_ready, spans_exp, spans_used = sem("gla_log_decays_ready"), sem("gla_decays_ready"), sem("gla_factors_ready")
        pairs_ready, pairs_read, far_summed = sem("gla_scores_ready"), sem("gla_scores_masked"), sem("gla_far_scores_ready")
        near_ready, far_ready = sem("gla_near_scores_masked"), sem("gla_far_scores_copied")
        gla_mixed, gla_added = sem("gla_values_mixed"), sem("gla_output_added")

        def halves(ap, b):
            return ap.rearrange("p (n h b) -> p n h b", h=2, b=b)

        def gla_tensor(pe):
            pe.wait_ge(mixed_copied, units_before(4))
            turn_values(pe, BIG[:, 4:8, :], 4, 0).then_inc(gv_turned, 1)
            pe.wait_ge(gv_ready, 1)

            def forget(g):
                low = slice(32 * (g // 2), 32 * (g // 2) + 16)
                pe.matmul(pb[7][:, :], S("wg", low.start, low.stop, g % 2 * P, P), BIG[low, 28, :], start=True, stop=True)\
                  .then_inc(forget_ready, 1)

            def pairs(u):
                g, hb = u // 2, u % 2
                d, j, rows = g // 2, g % 2, slice(HD * hb, HD * hb + HD)
                QC, QL = QC2[g % 2], QL2[g % 2]
                if hb == 0:
                    pe.wait_ge(spans_used, g + 1)
                    if g < 3:
                        forget(g + 1)
                for li in range(len(LEVELS) + 1):
                    if u and li % 2 == 0:
                        pe.wait_ge(pairs_read, 4 * (u - 1) + li // 2 + 1)
                    for i in range(2):
                        o = (li % 2) * TC + i * P
                        k = q = QL[rows, min(li, len(LEVELS) - 1), i * P:(i + 1) * P]
                        if li == len(LEVELS):
                            k, q = (BIG[rows, t + j, TC + i * P:TC + (i + 1) * P] for t in (2, 0))
                        mm = pe.matmul(pb[li // 2][:, o:o + P], k, q, start=True, stop=True)
                    if li % 2:
                        mm.then_inc(pairs_ready, 1)
                if u:
                    pe.wait_ge(far_ready, u)
                e, l = (slice(x * P, (x + 1) * P) for x in ((0, 1) if d == 0 else (1, 0)))
                pe.matmul(pb[4][:, 0:P], QL[rows, 7, e], QL[rows, 7, l], start=True, stop=True)
                for s in range(2):
                    mm = pe.matmul(pb[5][:, s * TC:(s + 1) * TC], QC[rows, s * P:(s + 1) * P], QC[rows, TC:T],
                                   start=True, stop=True)
                mm.then_inc(far_summed, 1)

            forget(0)
            pairs(0)
            for u in range(8):
                early, late = (2, 3) if u < 4 else (3, 2)
                h = u % 4
                hc, NEAR, FAR, CTXA = slice(h * P, (h + 1) * P), NEAR2[u % 2], FAR2[u % 2], CTXA2[u % 2]
                if u < 7:
                    pairs(u + 1)
                pe.wait_ge(near_ready, u + 1)
                pe.wait_ge(far_ready, u + 1)
                if u:
                    pe.wait_ge(gla_added, u)
                for t in (2, 3):
                    terms = [(2 + (t - 2), NEAR[:, (t - 2) * P:(t - 1) * P])]
                    terms += [(early, FAR)] if t == late else []
                    terms += [(s, CTXA[:, s * TC + (t - 2) * P:s * TC + (t - 1) * P]) for s in range(2)]
                    for i, (s, a) in enumerate(terms):
                        mm = pe.matmul(pb[6][:, (t - 2) * P:(t - 1) * P], GVTOK[:, s, hc], a, start=i == 0,
                                       stop=i == len(terms) - 1)
                mm.then_inc(gla_mixed, 1)

        def gla_scalar(act):
            act.wait_ge(gv_turned, 1)
            for tt in range(TT):
                ins = act.activation(GVTOK[:, tt, :], pb[tt][:, :], ACT.Copy)
            ins.then_inc(gv_ready, 1)

            def log_gate(g):
                act.wait_ge(forget_ready, g + 1)
                if g:
                    act.wait_ge(spans_ready, g)
                act.activation(TMP2, pb[7][:, :], ACT.Abs, bias=V("bg", g))
                act.drain()
                act.activation(TMP2, TMP2, ACT.Exp, scale=-1.0)
                act.drain()
                act.activation(TMP2, TMP2, ACT.Ln, bias=1.0).then_inc(forget_logged, 1)

            def decays(g):
                act.wait_ge(spans_ready, g + 1)
                act.activation(QC2[g % 2], QC2[g % 2], ACT.Exp, scale=1.0 / 16)
                act.activation(QL2[g % 2], QL2[g % 2], ACT.Exp, scale=1.0 / 16).then_inc(spans_exp, 1)

            def far(u):
                act.wait_ge(far_summed, u + 1)
                act.activation(CTXA2[u % 2], pb[5][:, :], ACT.Copy)
                act.activation(FAR2[u % 2], pb[4][:, 0:P], ACT.Copy).then_inc(far_ready, 1)

            log_gate(0)
            decays(0)
            for g in range(4):
                far(2 * g)
                if g < 3:
                    log_gate(g + 1)
                    decays(g + 1)
                far(2 * g + 1)

        def gla_vector(dve):
            dve.memset(ONES_ROW, 1.0)

            def log_spans(g):
                d, j = g // 2, g % 2
                hk, hq = (0, 1) if d == 0 else (1, 0)
                QC, QL = QC2[g % 2], QL2[g % 2]
                dve.wait_ge(forget_logged, g + 1)
                dve.tensor_scalar(LGT, pb[7][:, :], V("bg", g), 0.0, ALU.add, ALU.min)
                dve.drain()
                dve.tensor_tensor(LGT, LGT, TMP2, ALU.subtract)
                dve.drain()
                if d == 0:
                    dve.tensor_tensor_scan(BSUM, ONES_ROW, LGT, 0.0, ALU.mult, ALU.add)
                else:
                    dve.tensor_tensor_scan(BSUM[:, 0:TC][:, ::-1], ONES_ROW[:, 0:TC], LGT[:, 0:TC][:, ::-1], 0.0,
                                           ALU.mult, ALU.add)
                    dve.drain()
                    dve.tensor_tensor_scan(BSUM[:, TC:T][:, ::-1], ONES_ROW[:, 0:TC], LGT[:, TC:T][:, ::-1],
                                           BSUM[:, 0:1], ALU.mult, ALU.add)
                dve.drain()
                ref = BSUM[:, TC - 1:TC] if d == 0 else BSUM[:, 0:1]
                dve.tensor_scalar(QC[:, 0:TC], BSUM[:, 0:TC], -1.0, ref, ALU.mult, ALU.add)
                dve.tensor_scalar(QC[:, TC:T], BSUM[:, TC:T], ref, None, ALU.subtract)
                for li, b in enumerate(GLA_LEVELS):
                    src, dst = halves(BSUM[:, TC:T], b), halves(QL[:, li, :], b)
                    r = b - 1 if d == 0 else 0
                    refs = src[:, :, hk, r:r + 1].to_broadcast([P, TC // (2 * b), b])
                    dve.tensor_tensor(dst[:, :, hq, :], src[:, :, hq, :], refs, ALU.subtract)
                    dve.tensor_tensor(dst[:, :, hk, :], refs, src[:, :, hk, :], ALU.subtract)
                dve.drain().then_inc(spans_ready, 1)

            def factors(g):
                d, j = g // 2, g % 2
                hk, hq = (0, 1) if d == 0 else (1, 0)
                QC, QL = QC2[g % 2], QL2[g % 2]
                dve.wait_ge(spans_exp, g + 1)
                dve.tensor_tensor(QC[:, 0:TC], QC[:, 0:TC], BIG[:, 2 + j, 0:TC], ALU.mult)
                dve.tensor_tensor(QC[:, TC:T], QC[:, TC:T], BIG[:, j, TC:T], ALU.mult)
                for li, b in enumerate(GLA_LEVELS):
                    dst = halves(QL[:, li, :], b)
                    for half, src in ((hq, BIG[:, j, TC:T]), (hk, BIG[:, 2 + j, TC:T])):
                        dve.tensor_tensor(dst[:, :, half, :], dst[:, :, half, :], halves(src, b)[:, :, half, :], ALU.mult)
                dve.drain().then_inc(spans_used, 1)

            def near(u):
                mask = lambda li: C("mu" if u < 4 else "ml", li * P, P)
                dve.drain()
                for li in range(len(LEVELS) + 1):
                    if li % 2 == 0:
                        dve.wait_ge(pairs_ready, 4 * u + li // 2 + 1)
                    m = mask(li) if li < len(LEVELS) else C("ident")
                    o = (li % 2) * TC
                    ins = dve.tensor_tensor(tiles(PART[:, li // 2, o:o + TC]), tiles(pb[li // 2][:, o:o + TC]), over(m, 2),
                                            ALU.mult)
                    if li % 2:
                        ins.then_inc(pairs_read, 1)
                dve.drain()
                dve.tensor_tensor(PART[:, 0, :], PART[:, 0, :], PART[:, 1, :], ALU.add)
                dve.tensor_tensor(PART[:, 2, :], PART[:, 2, :], PART[:, 3, :], ALU.add)
                dve.drain()
                dve.tensor_tensor(PART[:, 0, :], PART[:, 0, :], PART[:, 2, :], ALU.add)
                dve.drain()
                dve.tensor_tensor(NEAR2[u % 2], PART[:, 0, 0:TC], PART[:, 0, TC:T], ALU.add).then_inc(near_ready, 1)

            def add_output(u):
                y = H[:, u % 4, TC:T]
                dve.wait_ge(gla_mixed, u + 1)
                if u < 4:
                    dve.tensor_copy(y, pb[6][:, 0:TC]).then_inc(gla_added, 1)
                else:
                    dve.tensor_tensor(y, y, pb[6][:, 0:TC], ALU.add).then_inc(gla_added, 1)

            log_spans(0)
            factors(0)
            for u in range(8):
                near(u)
                if u < 6:
                    (factors if u % 2 else log_spans)(u // 2 + 1)
                if u:
                    add_output(u - 1)
            add_output(7)

        block = ctx.enter_context(nc.Block())

        @block.tensor
        def _(pe):
            mods_tensor(pe)
            pe.wait_ge(loaded, 16 * 3)
            norm_tensor(pe, 0)
            ffn_tensor(pe, 0)
            norm_tensor(pe, 1)
            linear_tensor(pe, 0)
            even_heads_tensor(pe)
            attend_tensor(pe, 0)
            wkv_features_tensor(pe)
            wkv_tensor(pe)
            wkv_readout_tensor(pe)
            residual_tensor(pe, 0)
            norm_tensor(pe, 2)
            ffn_tensor(pe, 1)
            norm_tensor(pe, 3)
            ffn_tensor(pe, 2)
            norm_tensor(pe, 4)
            linear_tensor(pe, 1)
            odd_heads_tensor(pe)
            attend_tensor(pe, 1)
            residual_tensor(pe, 1)
            norm_tensor(pe, 5)
            ffn_tensor(pe, 3)
            gain_norm_tensor(pe, 0)
            norm_tensor(pe, 6)
            linear_tensor(pe, 2)
            mla_heads_tensor(pe)
            attend_tensor(pe, 2)
            mlstm_tensor(pe)
            readout_tensor(pe, 0)
            residual_tensor(pe, 2)
            norm_tensor(pe, 7)
            linear_tensor(pe, 3)
            na_heads_tensor(pe)
            attend_tensor(pe, 3)
            gla_tensor(pe)
            readout_tensor(pe, 1)
            residual_tensor(pe, 3)
            gain_norm_tensor(pe, 1)

        @block.vector
        def _(dve):
            setup_vector(dve)
            conditions_vector(dve)
            first_mods_vector(dve)
            mods_vector(dve, 0, MOD_BATCHES[0][1])
            dve.wait_ge(loaded, 16 * 3)
            norm_vector(dve, 0)
            ffn_vector(dve, 0)
            norm_vector(dve, 1)
            linear_vector(dve, 0)
            even_heads_vector(dve)
            attend_vector(dve, 0)
            wkv_features_vector(dve)
            wkv_vector(dve)
            wkv_readout_vector(dve)
            residual_vector(dve, 0)
            norm_vector(dve, 2)
            ffn_vector(dve, 1)
            norm_vector(dve, 3)
            ffn_vector(dve, 2)
            norm_vector(dve, 4)
            linear_vector(dve, 1)
            odd_heads_vector(dve)
            attend_vector(dve, 1)
            residual_vector(dve, 1)
            norm_vector(dve, 5)
            ffn_vector(dve, 3)
            gain_norm_vector(dve, 0)
            norm_vector(dve, 6)
            linear_vector(dve, 2)
            mla_heads_vector(dve)
            attend_vector(dve, 2)
            mlstm_vector(dve)
            readout_vector(dve, 0)
            residual_vector(dve, 2)
            norm_vector(dve, 7)
            linear_vector(dve, 3)
            attend_vector(dve, 3)
            gla_vector(dve)
            readout_vector(dve, 1)
            residual_vector(dve, 3)
            gain_norm_vector(dve, 1)

        @block.scalar
        def _(act):
            setup_scalar(act)
            mods_scalar(act)
            inputs_scalar(act)
            norm_scalar(act, 0, "ffn_in0")
            ffn_scalar(act, 0)
            norm_scalar(act, 1, "even_in", ffn_added, 4 + 1)
            linear_scalar(act, 0)
            even_heads_scalar(act)
            attend_scalar(act, 0)
            wkv_features_scalar(act)
            wkv_scalar(act)
            wkv_readout_scalar(act)
            residual_scalar(act, 0)
            norm_scalar(act, 2, "ffn_in1", mixer_added, 4 + 1)
            ffn_scalar(act, 1)
            norm_scalar(act, 3, "ffn_in2", ffn_added, 4 + KT + 1)
            ffn_scalar(act, 2)
            norm_scalar(act, 4, "odd_in", ffn_added, 4 + 2 * KT + 1)
            linear_scalar(act, 1)
            odd_heads_scalar(act)
            attend_scalar(act, 1)
            residual_scalar(act, 1)
            norm_scalar(act, 5, "ffn_in3", mixer_added, 4 + KT + 1)
            ffn_scalar(act, 3)
            gain_norm_scalar(act, 0, ffn_added, 4 + 3 * KT + 1)
            act.wait_ge(ctx2_loaded, 16)
            norm_scalar(act, 6, "l0_in", scaled, GAIN_NORMS[0][2] * KT + 1)
            linear_scalar(act, 2)
            mla_heads_scalar(act)
            attend_scalar(act, 2)
            mlstm_scalar(act)
            readout_scalar(act, 0)
            residual_scalar(act, 2)
            norm_scalar(act, 7, "l1_in", mixer_added, 4 + 2 * KT + 1)
            linear_scalar(act, 3)
            na_heads_scalar(act)
            attend_scalar(act, 3)
            gla_scalar(act)
            readout_scalar(act, 1)
            residual_scalar(act, 3)
            gain_norm_scalar(act, 1, mixer_added, 4 + 3 * KT + 1)

        def load_table(pool, first, last, stage):
            a, b = TO[first][0], sum(TO[last])
            pool.wait_ge(slab_done, sum(SLAB_AT[stage]))
            pool.dma_start(SPARE[:, :, :].rearrange("p a t -> p (a t)")[:, 3 * T:3 * T + b - a], tables[:, a:b])\
                .then_inc(tables_loaded, 16)

        @block.gpsimd
        def _(pool):
            pool.wait_ge(mod_third, 2 * RING)
            pool.dma_start(X[:, :, :], xin).then_inc(loaded, 16)
            pool.dma_start(cst[:, :], consts).then_inc(loaded, 16)
            pool.dma_start(smallw[:, :], small).then_inc(loaded, 16)
            first_splits_gpsimd(pool, "ffn_in0")
            add_squares_gpsimd(pool, NORMS[1][0], NORMS[1][4])
            first_splits_gpsimd(pool, "even_in")
            load_table(pool, "reset", "ident64", "even_in")
            wkv_features_gpsimd(pool)
            wkv_gpsimd(pool)
            first_splits_gpsimd(pool, "even_out")
            add_squares_gpsimd(pool, NORMS[2][0], NORMS[2][4])
            first_splits_gpsimd(pool, "ffn_in1")
            add_squares_gpsimd(pool, NORMS[3][0], NORMS[3][4])
            first_splits_gpsimd(pool, "ffn_in2")
            add_squares_gpsimd(pool, NORMS[4][0], NORMS[4][4])
            first_splits_gpsimd(pool, "odd_in")
            load_table(pool, "wmask", "wmask", "odd_in")
            first_splits_gpsimd(pool, "odd_out")
            pool.wait_ge(scaled, 5 * KT)
            pool.dma_start(X[:, :, 0:TC], ctx2).then_inc(ctx2_loaded, 16)
            add_squares_gpsimd(pool, NORMS[5][0], NORMS[5][4])
            first_splits_gpsimd(pool, "ffn_in3")
            add_squares_gpsimd(pool, LAT, GAIN_NORMS[0][2])
            first_splits_gpsimd(pool, "l0_in")
            load_table(pool, "cosme", "sinmk", "l0_in")
            mlstm_gpsimd(pool)
            first_splits_gpsimd(pool, "l0_out")
            add_squares_gpsimd(pool, NORMS[7][0], NORMS[7][4])
            first_splits_gpsimd(pool, "l1_in")
            load_table(pool, "namask", "namask", "l1_in")
            na_heads_gpsimd(pool)
            first_splits_gpsimd(pool, "l1_out")
            add_squares_gpsimd(pool, LAT, GAIN_NORMS[1][2])

        @block.sync
        def _(sp):
            sp.dma_start(vec[:, :], vecs).then_inc(vectors_loaded, 16)

            def last_read(n):
                stage = [name for name, (at, _) in SLAB_AT.items() if at <= n][-1]
                q = n - SLAB_AT[stage][0]
                if stage == "mods":
                    return mod_third, 2 * (q + 1), 2 * RING
                if stage.startswith("ffn_in") and q % 2:
                    return mod_third, 2 * (mods_before(int(stage[-1])) + q // 2 + 1), RING
                if stage in SPLIT_AT and stage not in FIRST_SPLITS:
                    return split_ready, VECTOR_SPLIT_AT[stage][0] + q + 3, RING
                if stage in SPLIT_AT:
                    each = 2 if stage.startswith("ffn") else 1
                    if q // each < 2:
                        return first_ready, 2 * FIRST_SPLITS.index(stage) + q // each + 1, 0
                    return split_ready, VECTOR_SPLIT_AT[stage][0] + q // each + 1, RING // each
                return slab_done, n + 1, RING

            def load(n, src, i=None):
                if n >= RING:
                    left, count, step = last_read(n - RING)
                    sp.wait_ge(left, count if i is None else i * step + count)
                sp.dma_start(ring[:, n % RING, 0:src.shape[-1]], src).then_inc(slot_full[n % RING], 16)

            row = 0
            for stage, count in SLABS:
                n = SLAB_AT[stage][0]
                if stage.startswith("ffn_out"):
                    for s in range(count):
                        m, part = divmod(s, len(OUT_PARTS))
                        t = sum(OUT_PARTS[:part])
                        load(n + s, stream_f[int(stage[-1]) * KT + m, :, t * P:(t + OUT_PARTS[part]) * P])
                    continue
                first = min(count, RING if n == 0 else 2 * RING)
                for k in range(first):
                    load(n + k, stream_k[row + k])
                turns = (count - first) // RING
                if turns:
                    with sp.Fori(0, turns) as i:
                        for k in range(first, first + RING):
                            load(n + k, stream_k[bass.ds(i * RING + (row + k), 1), :, :].rearrange("o p c -> (o p) c"), i)
                for k in range(first + turns * RING, count):
                    load(n + k, stream_k[row + k])
                row += count
            sp.wait_ge(scaled, 10 * KT)
            sp.dma_start(out, X[:, :, TC:T]).then_inc(stored, 16)
            sp.wait_ge(stored, 16)


def shape_constants():
    p, f = np.arange(P)[:, None], np.arange(P)[None, :]
    c = {"ident": p == f, "ones": np.ones((P, P)), "blk": p // HD == f // HD, "ident64": p % 64 == np.arange(64)[None, :]}
    rot = np.zeros((P, P))
    for i in range(0, P, 2):
        rot[i + 1, i], rot[i, i + 1] = -1, 1
    rotm = np.zeros((P, P))
    for base in (0, 16, 64, 80):
        for i in range(base, base + 8):
            rotm[i + 8, i], rotm[i, i + 8] = -1, 1
    c |= {"rot": rot, "rotm": rotm}
    sel_i, sel_f = np.zeros((P, 64)), np.zeros((P, 64))
    for d in range(2):
        for h in range(4):
            sel_i[32 + 8 * d + h, 32 * d + h] = 1
            sel_f[32 + 8 * d + 4 + h, 32 * d + h] = 1
    c |= {"sel_i": sel_i, "sel_f": sel_f}
    up = [(p // (2 * b) == f // (2 * b)) & (p % (2 * b) < b) & (f % (2 * b) >= b) for b in LEVELS]
    chunk = p // CHUNK == f // CHUNK
    c |= {"mu": np.concatenate(up, 1), "ml": np.concatenate([u.T for u in up], 1), "su": chunk & (p < f),
          "sl": chunk & (p > f), "iu": chunk & (p <= f), "il": chunk & (p >= f),
          "nu": np.where(p <= f, 0, NEG), "nl": np.where(p >= f, 0, NEG)}
    t = np.arange(TC)
    row, col = (t // GRID_W).astype(np.float32), (t % GRID_W).astype(np.float32)
    inv = np.float32(10000.0) ** (-np.arange(16, dtype=np.float32) / np.float32(16))
    ang = np.concatenate([row[:, None] * inv, col[:, None] * inv], 1).T
    pair = np.arange(P) % HD // 2
    c |= {"cosa": np.cos(ang)[pair], "sina": np.sin(ang)[pair]}
    inv = np.float32(1.0) / np.float32(10000.0) ** (np.arange(8, dtype=np.float32) / np.float32(8))
    ang = np.concatenate([row[:, None] * inv, col[:, None] * inv], 1).T
    r32 = np.arange(32)
    ang = ang[r32 // 16 * 8 + r32 % 8]
    for name, bases in (("me", (64,)), ("mo", (0,)), ("mk", (0, 64))):
        cos, sin = np.ones((P, TC), np.float32), np.zeros((P, TC), np.float32)
        for b in bases:
            cos[b:b + 32], sin[b:b + 32] = np.cos(ang), np.sin(ang)
        c["cos" + name], c["sin" + name] = cos, sin
    q, k = np.arange(TC)[:, None], np.arange(TC)[None, :]
    halves = lambda m: m.reshape(2, P, TC).transpose(1, 0, 2).reshape(P, 2 * TC)
    c["wmask"] = halves(np.where((np.abs(k - q) <= 128) & (k >= 128), 0, NEG))
    c["padkeys"] = p + 1
    start = np.clip(q % GRID_W - 8, 0, GRID_W - 16)
    inside = (k % GRID_W >= start) & (k % GRID_W < start + 16)
    c["namask"] = halves(np.where(inside, 0, NEG))
    c["reset"] = np.broadcast_to(np.arange(T)[None, :] % CHUNK != 0, (P, T))
    return [np.concatenate([np.asarray(c[n], np.float32) for n, _ in names], 1) for names in (CONSTS, TABLES)]


def lay_out(a):
    heads = lambda order: np.concatenate([np.arange(h * HD, h * HD + HD) for h in order])
    even = heads([h for t in range(4) for h in (t, 4 + t)])
    odd = heads([h for q in range(2) for j in range(4) for h in (8 * q + j, 8 * q + 4 + j)])
    slabs_k, slabs_f = [], []

    def tiled(w):
        n = w.shape[1] // P
        return w.reshape(KT, P, n, P).transpose(2, 1, 0, 3).reshape(n, P, D)

    def square(w):
        slabs_k.append(tiled(w))

    mods = np.concatenate([tiled(w) for w in (a["w_mod"][0], a["w_mod"][1], a["l0_w_mod_2"], a["l1_w_mod_2"])], 0)

    def ffn(f, w_in, w_out):
        w_in = tiled(w_in.reshape(D, 2, FT, P).transpose(0, 2, 1, 3).reshape(D, 2 * DFF))
        m = mods[np.arange(2 * FT) % len(mods[slice(*MOD_BATCHES[f + 1])]) + MOD_BATCHES[f + 1][0]]
        slabs_k.append(np.stack([w_in, m], 1).reshape(-1, P, D))
        slabs_f.append(w_out.reshape(FT, P, KT, P).transpose(2, 1, 0, 3).reshape(KT, P, DFF))

    def padded(w, cols):
        out = np.zeros((w.shape[0], len(cols)), np.float32)
        keep = np.flatnonzero(cols >= 0)
        out[:, keep] = w[:, cols[keep]]
        return out

    slabs_k.append(mods[:MOD_BATCHES[0][1]])
    ffn(0, a["ffn_in"][0, 0], a["ffn_out"][0, 0])
    w = a["even_w_in"][0]
    square(np.concatenate([w[:, even], w[:, 512:]], 1))
    w = a["even_w_out"][0]
    square(np.concatenate([w[even], w[512:]], 0))
    ffn(1, a["ffn_in"][0, 1], a["ffn_out"][0, 1])
    ffn(2, a["ffn_in"][1, 0], a["ffn_out"][1, 0])
    w = a["odd_w_in"][0]
    square(np.concatenate([w[:, odd], w[:, 1024:]], 1))
    square(a["odd_w_out"][0][odd])
    ffn(3, a["ffn_in"][1, 1], a["ffn_out"][1, 1])

    none = lambda n: np.full(n, -1)
    c = np.arange(a["l0_w_in_2"].shape[1])
    krope, gates = c[640:672], c[2720:2736]
    square(padded(a["l0_w_in_2"], np.concatenate([c[0:640], c[672:2720], c[2736:3760], krope, gates, none(16), krope,
                                                  none(32)])))
    uq = np.zeros((4, P, D), np.float32)
    for h in range(8):
        q = np.arange(96 * h, 96 * h + 96)
        cols = np.concatenate([q, none(32)] if h % 2 == 0 else [q[64:], none(32), q[:64]])
        w = padded(a["l0_mla_w_uq_2"], cols).reshape(3, P, P).transpose(1, 0, 2).reshape(P, 3 * P)
        uq[h // 2, :, h % 2 * 3 * P:(h % 2 + 1) * 3 * P] = w
    slabs_k.append(uq)
    ukv = a["l0_mla_w_ukv_2"].reshape(2, P, 4, 2, 2, HD)
    slabs_k.append(ukv.transpose(4, 1, 2, 0, 3, 5).reshape(2, P, D))
    square(a["l0_w_out_2"])
    c = np.arange(a["l1_w_in_2"].shape[1])
    square(padded(a["l1_w_in_2"], np.concatenate([c[0:1024], c[1056:3616], c[1024:1040], none(16), c[1040:1056],
                                                  none(80)])))
    square(a["l1_w_out_2"])

    col = lambda v: np.asarray(v).reshape(-1, P).T
    def gate_rows(v):
        out = np.zeros((P, 1), np.float32)
        out[0:4, 0], out[32:36, 0] = v[0], v[1]
        return out

    pair = lambda lat, ctx: np.stack([col(ctx), col(lat)], 2).reshape(P, 2 * KT)
    v = {"c": pair(a["c"][0], a["c_ctx"]), "bmod0": col(a["b_mod"][0]), "bmod1": col(a["b_mod"][1]),
         "qgain": np.concatenate([a["q_gain"][0]] * 2)[:, None], "kgain": np.concatenate([a["k_gain"][0]] * 2)[:, None],
         "mu": col(a["rwkv_mu"][0]), "w0": col(a["rwkv_w0"][0]), "a0": col(a["rwkv_a0"][0]), "kk": col(a["rwkv_k_k"][0]),
         "ka": col(a["rwkv_k_a"][0]), "rk": col(a["rwkv_r_k"][0]), "gnw": col(a["rwkv_gn_w"][0]),
         "gnb": col(a["rwkv_gn_b"][0]), "sink": np.broadcast_to(a["sink"][0][None, :], (P, 16)),
         "fgain": col(a["final_gain"]), "c2": pair(a["c_2"][0], a["c_ctx_2"]), "n0": col(a["l0_norm_2"]),
         "bm0": col(a["l0_b_mod_2"]), "qn": col(a["l0_mla_q_norm_2"]), "kvn": col(a["l0_mla_kv_norm_2"]),
         "cw": col(a["l0_mlstm_conv_w_2"]), "cb": col(a["l0_mlstm_conv_b_2"]), "bi": gate_rows(a["l0_mlstm_b_i_2"]),
         "bf": gate_rows(a["l0_mlstm_b_f_2"]), "mn": col(a["l0_mlstm_norm_2"]), "n1": col(a["l1_norm_2"]),
         "bm1": col(a["l1_b_mod_2"]), "bg": col(a["l1_gla_b_gate_2"]), "gln": col(a["l1_gla_norm_2"]),
         "fn": col(a["final_norm_2"])}
    wg = np.zeros((P, 256), np.float32)
    wg[0:16], wg[32:48] = a["l1_gla_w_gate_2"][0], a["l1_gla_w_gate_2"][1]
    small = np.concatenate([a["rwkv_w2"][0].reshape(P, 512), a["rwkv_a2"][0].reshape(P, 512), a["rwkv_g2"][0], wg], 1)
    consts, tables = shape_constants()
    tok = lambda x: x[0].T.reshape(KT, P, TC).transpose(1, 0, 2)
    q, k = np.arange(TC)[:, None], np.arange(TC)[None, :]
    bias = a["l1_na_rpb_2"][:, k // GRID_W - q // GRID_W + 7, np.clip(k % GRID_W - q % GRID_W + 15, 0, 30)]
    bias = np.stack([bias[2 * t + b, (qt - 2) * P:(qt - 1) * P] for t, b, qt in attention_units("na")], 1)
    return {"xin": np.concatenate([tok(a["ctx"]), tok(a["x"])], 2), "ctx2": tok(a["ctx_2"]),
            "stream_k": np.concatenate(slabs_k, 0), "stream_f": np.concatenate(slabs_f, 0),
            "vecs": np.concatenate([v[n] for n, _ in VECS], 1), "consts": consts, "tables": tables, "small": small,
            "nabias": bias.reshape(P, -1)}


INPUTS = ["xin", "ctx2", "stream_k", "stream_f", "vecs", "consts", "tables", "small", "nabias"]


def kernel(**inputs):
    import concourse.bacc as bacc
    from concourse.bass_utils import run_bass_kernel_spmd

    laid = lay_out({n: np.asarray(x) for n, x in inputs.items()})
    nc = bacc.Bacc("TRN2", target_bir_lowering=False, num_devices=1)
    arrays, args = {}, []
    for name in INPUTS:
        arrays[name] = np.ascontiguousarray(laid[name])
        args.append(nc.dram_tensor(name, arrays[name].shape, F32, kind="ExternalInput").ap())
    result = nc.dram_tensor("result", (P, KT, TC), F32, kind="ExternalOutput").ap()
    build(nc, *args, result)
    r = run_bass_kernel_spmd(nc, [arrays], core_ids=[0]).results[0]["result"]
    return np.ascontiguousarray(r.transpose(2, 1, 0).reshape(1, TC, D))
```
